# Optimizing a Trainium2 kernel written in Bass

```python
import jax, jax.numpy as jnp
from jax import lax
import numpy as np
import math

D_MODEL = 1024
BATCH = 1
SEQ = 512
DEPTH = 1

CONV_DIM = 512
CONV_WIDTH = 3
N_HEADS = 16
N_KV_HEADS = 4
HEAD_DIM = 64
GROUP = N_HEADS // N_KV_HEADS
CMP_LEN = 32
CMP_STRIDE = 16
CMP_HIDDEN = 256
SEL_LEN = 64
SEL_TOP = 16
WINDOW = 512
Q_BLOCK = 64
N_NSA_BRANCHES = 3
D_FF = -(-8 * D_MODEL // (3 * 256)) * 256
EPS = 1e-6

Q_COLS = N_HEADS * HEAD_DIM
KV_COLS = N_KV_HEADS * HEAD_DIM
IN_SIZES = (CONV_DIM, CONV_DIM, CONV_DIM, Q_COLS,
            KV_COLS, KV_COLS, KV_COLS, KV_COLS, KV_COLS, KV_COLS,
            N_NSA_BRANCHES * N_HEADS, D_MODEL, D_MODEL)
IN_COLS = sum(IN_SIZES)


def _split_points():
    pts, acc = [], 0
    for s in IN_SIZES[:-1]:
        acc += s
        pts.append(acc)
    return pts

def rmsnorm(x, g):
    xf = x.astype(jnp.float32)
    y = xf * lax.rsqrt(jnp.mean(xf * xf, axis=-1, keepdims=True) + EPS)
    return (y * g.astype(jnp.float32)).astype(x.dtype)

def masked_softmax(s, mask):
    s = jnp.where(mask, s.astype(jnp.float32), -jnp.inf)
    m = jnp.max(s, axis=-1, keepdims=True)
    m = jnp.where(jnp.isfinite(m), m, 0.0)
    e = jnp.exp(s - m)
    return e / jnp.maximum(jnp.sum(e, axis=-1, keepdims=True), 1e-30)

def short_conv_mixer(b_gate, c_gate, h_in, conv_w, w_out):
    S = h_in.shape[1]
    u = c_gate * h_in
    up = jnp.pad(u, ((0, 0), (CONV_WIDTH - 1, 0), (0, 0)))
    conv = sum(up[:, k:k + S, :] * conv_w[k] for k in range(CONV_WIDTH))
    return (b_gate * conv) @ w_out

def compress(kv, pos, w1, w2, n_cmp):
    B = kv.shape[0]
    idx = jnp.arange(n_cmp)[:, None] * CMP_STRIDE + jnp.arange(CMP_LEN)[None, :]
    blk = kv[:, idx] + pos[None, None, :, None, :]
    blk = blk.transpose(0, 3, 1, 2, 4).reshape(B, N_KV_HEADS, n_cmp, CMP_LEN * HEAD_DIM)
    return jax.nn.gelu(blk @ w1) @ w2

def overlap_matrix(n_cmp, n_sel):
    cs = np.arange(n_cmp)[:, None] * CMP_STRIDE
    ss = np.arange(n_sel)[None, :] * SEL_LEN
    ov = np.maximum(0, np.minimum(cs + CMP_LEN, ss + SEL_LEN) - np.maximum(cs, ss))
    return jnp.asarray(ov / CMP_LEN, dtype=jnp.float32)

def nsa_attention(q, k_cmp, v_cmp, k_sel, v_sel, k_win, v_win, overlap, n_top):
    B, _, _, S, _ = q.shape
    n_cmp = k_cmp.shape[2]
    n_sel = k_sel.shape[2]
    scale = HEAD_DIM ** -0.5
    cmp_end = jnp.arange(n_cmp) * CMP_STRIDE + CMP_LEN - 1
    blk_ids = jnp.arange(n_sel)
    bi = jnp.arange(B)[:, None, None]
    hi = jnp.arange(N_KV_HEADS)[None, :, None]

    def block(b):
        q0 = b * Q_BLOCK
        qb = lax.dynamic_slice_in_dim(q, q0, Q_BLOCK, axis=3)
        t = q0 + jnp.arange(Q_BLOCK)
        s = jnp.einsum('bhgqd,bhnd->bhgqn', qb, k_cmp) * scale
        p_cmp = masked_softmax(s, cmp_end[None, :] <= t[:, None])
        o_cmp = jnp.einsum('bhgqn,bhnd->bhgqd', p_cmp.astype(v_cmp.dtype), v_cmp)
        imp = jnp.einsum('bhgqn,nm->bhqm', p_cmp, overlap)
        cur = t // SEL_LEN
        forced = (blk_ids[None, :] == 0) | (blk_ids[None, :] == cur[:, None]) | (blk_ids[None, :] == cur[:, None] - 1)
        imp = jnp.where(forced, jnp.inf, imp)
        imp = jnp.where(blk_ids[None, :] * SEL_LEN <= t[:, None], imp, -jnp.inf)
        top_val, top_idx = lax.top_k(imp, n_top)
        blk_ok = top_val > -jnp.inf
        flat = top_idx.reshape(B, N_KV_HEADS, Q_BLOCK * n_top)
        ks = k_sel[bi, hi, flat].reshape(B, N_KV_HEADS, Q_BLOCK, n_top * SEL_LEN, HEAD_DIM)
        vs = v_sel[bi, hi, flat].reshape(B, N_KV_HEADS, Q_BLOCK, n_top * SEL_LEN, HEAD_DIM)
        kpos = top_idx[..., None] * SEL_LEN + jnp.arange(SEL_LEN)
        smask = (kpos <= t[None, None, :, None, None]) & blk_ok[..., None]
        smask = smask.reshape(B, N_KV_HEADS, Q_BLOCK, n_top * SEL_LEN)
        s = jnp.einsum('bhgqd,bhqkd->bhgqk', qb, ks) * scale
        p = masked_softmax(s, smask[:, :, None])
        o_sel = jnp.einsum('bhgqk,bhqkd->bhgqd', p.astype(vs.dtype), vs)
        kw = lax.dynamic_slice_in_dim(k_win, q0, Q_BLOCK + WINDOW, axis=2)
        vw = lax.dynamic_slice_in_dim(v_win, q0, Q_BLOCK + WINDOW, axis=2)
        wpos = q0 - WINDOW + jnp.arange(Q_BLOCK + WINDOW)
        diff = t[:, None] - wpos[None, :]
        wmask = (diff >= 0) & (diff < WINDOW) & (wpos[None, :] >= 0)
        s = jnp.einsum('bhgqd,bhkd->bhgqk', qb, kw) * scale
        p = masked_softmax(s, wmask)
        o_win = jnp.einsum('bhgqk,bhkd->bhgqd', p.astype(vw.dtype), vw)
        return jnp.stack([o_cmp, o_sel, o_win], axis=0)

    out = lax.map(block, jnp.arange(S // Q_BLOCK))
    out = out.transpose(1, 2, 0, 5, 3, 4, 6)
    return out.reshape(N_NSA_BRANCHES, B, S, N_HEADS, HEAD_DIM)

def first_inputs(seed: int = 0) -> dict:
    key = jax.random.key(seed)
    ks = jax.random.split(key, 20)
    L = DEPTH
    nrm = lambda k, shape, fan_in: jax.random.normal(k, shape, jnp.float32) * (fan_in ** -0.5)
    gain = lambda k, shape: 1.0 + 0.05 * jax.random.normal(k, shape, jnp.float32)
    return {
        "x": jax.random.normal(ks[0], (BATCH, SEQ, D_MODEL), jnp.float32),
        "w_in": nrm(ks[1], (L, D_MODEL, IN_COLS), D_MODEL),
        "conv_w": nrm(ks[2], (L, CONV_WIDTH, CONV_DIM), CONV_WIDTH),
        "w_conv_out": nrm(ks[3], (L, CONV_DIM, D_MODEL), CONV_DIM),
        "cmp_pos_k": 0.1 * jax.random.normal(ks[4], (L, CMP_LEN, HEAD_DIM), jnp.float32),
        "cmp_w1_k": nrm(ks[5], (L, CMP_LEN * HEAD_DIM, CMP_HIDDEN), CMP_LEN * HEAD_DIM),
        "cmp_w2_k": nrm(ks[6], (L, CMP_HIDDEN, HEAD_DIM), CMP_HIDDEN),
        "cmp_pos_v": 0.1 * jax.random.normal(ks[7], (L, CMP_LEN, HEAD_DIM), jnp.float32),
        "cmp_w1_v": nrm(ks[8], (L, CMP_LEN * HEAD_DIM, CMP_HIDDEN), CMP_LEN * HEAD_DIM),
        "cmp_w2_v": nrm(ks[9], (L, CMP_HIDDEN, HEAD_DIM), CMP_HIDDEN),
        "w_attn_out": nrm(ks[10], (L, Q_COLS, D_MODEL), Q_COLS),
        "w_o": nrm(ks[11], (L, D_MODEL, D_MODEL), D_MODEL),
        "g_mix": gain(ks[12], (L, D_MODEL)),
        "g_ffn": gain(ks[13], (L, D_MODEL)),
        "w_gate": nrm(ks[14], (L, D_MODEL, D_FF), D_MODEL),
        "w_up": nrm(ks[15], (L, D_MODEL, D_FF), D_MODEL),
        "w_down": nrm(ks[16], (L, D_FF, D_MODEL), D_FF),
        "g_final": gain(ks[17], (D_MODEL,)),
    }

def first_block(x, w_in, conv_w, w_conv_out, cmp_pos_k, cmp_w1_k, cmp_w2_k, cmp_pos_v, cmp_w1_v, cmp_w2_v,
              w_attn_out, w_o, g_mix, g_ffn, w_gate, w_up, w_down, g_final):
    B, S, _ = x.shape
    n_cmp = (S - CMP_LEN) // CMP_STRIDE + 1
    n_sel = S // SEL_LEN
    n_top = min(SEL_TOP, n_sel)
    overlap = overlap_matrix(n_cmp, n_sel)
    split_pts = _split_points()
    h = x
    for l in range(DEPTH):
        n = rmsnorm(h, g_mix[l])
        proj = n @ w_in[l]
        (b_gate, c_gate, h_conv, q, k_c, v_c, k_s, v_s, k_w, v_w,
         g_br, g_conv, g_attn) = jnp.split(proj, split_pts, axis=-1)
        y_conv = short_conv_mixer(b_gate, c_gate, h_conv, conv_w[l], w_conv_out[l])
        q = q.reshape(B, S, N_KV_HEADS, GROUP, HEAD_DIM).transpose(0, 2, 3, 1, 4)
        kvh = lambda t: t.reshape(B, S, N_KV_HEADS, HEAD_DIM)
        k_cmp = compress(kvh(k_c), cmp_pos_k[l], cmp_w1_k[l], cmp_w2_k[l], n_cmp)
        v_cmp = compress(kvh(v_c), cmp_pos_v[l], cmp_w1_v[l], cmp_w2_v[l], n_cmp)
        selb = lambda t: kvh(t).reshape(B, n_sel, SEL_LEN, N_KV_HEADS, HEAD_DIM).transpose(0, 3, 1, 2, 4)
        winp = lambda t: jnp.pad(kvh(t).transpose(0, 2, 1, 3), ((0, 0), (0, 0), (WINDOW, 0), (0, 0)))
        o_all = nsa_attention(q, k_cmp, v_cmp, selb(k_s), selb(v_s), winp(k_w), winp(v_w), overlap, n_top)
        br_gates = jax.nn.sigmoid(g_br).reshape(B, S, N_NSA_BRANCHES, N_HEADS)
        o = jnp.einsum('bsch,cbshd->bshd', br_gates, o_all).reshape(B, S, Q_COLS)
        y_attn = o @ w_attn_out[l]
        mix = jax.nn.sigmoid(g_conv) * y_conv + jax.nn.sigmoid(g_attn) * y_attn
        h = h + mix @ w_o[l]
        n = rmsnorm(h, g_ffn[l])
        h = h + (jax.nn.silu(n @ w_gate[l]) * (n @ w_up[l])) @ w_down[l]
    return rmsnorm(h, g_final)


N_MEM = 256
MLA_HEADS = 4
QK_NOPE = 128
QK_ROPE = 64
QK_HEAD = QK_NOPE + QK_ROPE
V_HEAD = 128
Q_LORA = 384
KV_LORA = 256
ROPE_THETA = 10000.0
Q_BLOCK_2 = 128
HG_HEADS = 4
HG_DK = 128
HG_DV = 128
HG_CHUNK = 64
MEM_HEADS = 4
MEM_HEAD_DIM = 128
MLA_WIDTH = MLA_HEADS * V_HEAD
HG_KWIDTH = HG_HEADS * HG_DK
HG_WIDTH = HG_HEADS * HG_DV
MEM_WIDTH = MEM_HEADS * MEM_HEAD_DIM
MIX_WIDTH = MLA_WIDTH + HG_WIDTH + MEM_WIDTH
D_FF_2 = -(-8 * D_MODEL // (3 * 256)) * 256
IN_SIZES_2 = (Q_LORA, KV_LORA, QK_ROPE, HG_KWIDTH, HG_KWIDTH, HG_WIDTH, HG_WIDTH, MEM_WIDTH)
IN_WIDTH = Q_LORA + KV_LORA + QK_ROPE + 2 * HG_KWIDTH + 2 * HG_WIDTH + MEM_WIDTH


def rmsnorm_2(x, g):
    xf = x.astype(jnp.float32)
    y = xf * lax.rsqrt(jnp.mean(xf * xf, axis=-1, keepdims=True) + EPS) * g.astype(jnp.float32)
    return y.astype(x.dtype)

def apply_rope(x, pos):
    half = QK_ROPE // 2
    inv_freq = jnp.power(ROPE_THETA, -jnp.arange(half, dtype=jnp.float32) / half)
    ang = pos.astype(jnp.float32)[:, :, None, None] * inv_freq
    cos, sin = jnp.cos(ang), jnp.sin(ang)
    xf = x.astype(jnp.float32)
    x1, x2 = xf[..., :half], xf[..., half:]
    return jnp.concatenate([x1 * cos - x2 * sin, x2 * cos + x1 * sin], axis=-1).astype(x.dtype)

def causal_block_attention(q, k, v):
    B, S, H, Dqk = q.shape
    Dv = v.shape[-1]
    nq = S // Q_BLOCK_2
    scale = Dqk ** -0.5
    qb = q.astype(jnp.float32).reshape(B, nq, Q_BLOCK_2, H, Dqk).transpose(1, 0, 2, 3, 4)
    starts = jnp.arange(nq, dtype=jnp.int32) * Q_BLOCK_2
    kf = k.astype(jnp.float32)
    vf = v.astype(jnp.float32)
    kpos = jnp.arange(S, dtype=jnp.int32)

    def one_block(args):
        qblk, start = args
        s = jnp.einsum('bqhd,bkhd->bhqk', qblk, kf) * scale
        qpos = start + jnp.arange(Q_BLOCK_2, dtype=jnp.int32)
        mask = kpos[None, :] <= qpos[:, None]
        s = jnp.where(mask[None, None], s, -jnp.inf)
        p = jax.nn.softmax(s, axis=-1)
        return jnp.einsum('bhqk,bkhd->bqhd', p, vf)

    out = lax.map(one_block, (qb, starts))
    return out.transpose(1, 0, 2, 3, 4).reshape(B, S, H, Dv).astype(v.dtype)

def mla_group(c_q, c_kv, k_rope, pos, q_a_norm, w_uq, kv_a_norm, w_ukv, q_norm, k_norm):
    B, S, _ = c_q.shape
    q = (rmsnorm_2(c_q, q_a_norm) @ w_uq).reshape(B, S, MLA_HEADS, QK_HEAD)
    kv = (rmsnorm_2(c_kv, kv_a_norm) @ w_ukv).reshape(B, S, MLA_HEADS, QK_NOPE + V_HEAD)
    k_nope, v = kv[..., :QK_NOPE], kv[..., QK_NOPE:]
    k_pe = jnp.broadcast_to(k_rope[:, :, None, :], (B, S, MLA_HEADS, QK_ROPE))
    k = jnp.concatenate([k_nope, k_pe], axis=-1)
    q = rmsnorm_2(q, q_norm)
    k = rmsnorm_2(k, k_norm)
    q = jnp.concatenate([q[..., :QK_NOPE], apply_rope(q[..., QK_NOPE:], pos)], axis=-1)
    k = jnp.concatenate([k[..., :QK_NOPE], apply_rope(k[..., QK_NOPE:], pos)], axis=-1)
    o = causal_block_attention(q, k, v)
    return o.reshape(B, S, MLA_WIDTH)

def hgrn2_group(q_raw, f_raw, i_raw, g_raw, lb, out_gain):
    B, S, _ = q_raw.shape
    n = S // HG_CHUNK
    f32 = jnp.float32
    q = jax.nn.silu(q_raw.astype(f32)) * (HG_DK ** -0.5)
    lbf = lb.astype(f32)
    f = lbf + (1.0 - lbf) * jax.nn.sigmoid(f_raw.astype(f32))
    k = 1.0 - f
    logf = jnp.log(f)
    v = i_raw.astype(f32)

    def chunks(t, d):
        return t.reshape(B, n, HG_CHUNK, HG_HEADS, d).transpose(1, 0, 3, 2, 4)

    qc, kc, vc = chunks(q, HG_DK), chunks(k, HG_DK), chunks(v, HG_DV)
    bc = jnp.cumsum(chunks(logf, HG_DK), axis=3)
    causal = jnp.tril(jnp.ones((HG_CHUNK, HG_CHUNK), dtype=bool))

    def chunk_step(state, xs):
        qx, kx, vx, bx = xs
        diff = bx[:, :, :, None, :] - bx[:, :, None, :, :]
        decay = jnp.where(causal[None, None, :, :, None], jnp.exp(jnp.minimum(diff, 0.0)), 0.0)
        a = jnp.einsum('bhtd,bhsd,bhtsd->bhts', qx, kx, decay)
        o = (jnp.einsum('bhts,bhse->bhte', a, vx)
             + jnp.einsum('bhtd,bhde->bhte', qx * jnp.exp(bx), state))
        b_last = bx[:, :, -1:, :]
        new_state = (jnp.exp(b_last[:, :, 0, :])[..., None] * state
                     + jnp.einsum('bhsd,bhse->bhde', kx * jnp.exp(b_last - bx), vx))
        return new_state, o

    s0 = jnp.zeros((B, HG_HEADS, HG_DK, HG_DV), f32)
    _, o = lax.scan(chunk_step, s0, (qc, kc, vc, bc))
    o = o.transpose(1, 0, 3, 2, 4).reshape(B, S, HG_HEADS, HG_DV)
    o = rmsnorm_2(o, out_gain.reshape(HG_HEADS, HG_DV)).reshape(B, S, HG_WIDTH)
    return (o * jax.nn.silu(g_raw.astype(f32))).astype(q_raw.dtype)

def mem_group(q_raw, mem_h, w_mem_kv, q_norm, k_norm):
    B, S, _ = q_raw.shape
    M = mem_h.shape[1]
    q = rmsnorm_2(q_raw.reshape(B, S, MEM_HEADS, MEM_HEAD_DIM), q_norm)
    kv = (mem_h @ w_mem_kv).reshape(B, M, 2, MEM_HEADS, MEM_HEAD_DIM)
    k = rmsnorm_2(kv[:, :, 0], k_norm)
    v = kv[:, :, 1]
    s = jnp.einsum('bqhd,bkhd->bhqk', q.astype(jnp.float32), k.astype(jnp.float32)) * (MEM_HEAD_DIM ** -0.5)
    p = jax.nn.softmax(s, axis=-1)
    o = jnp.einsum('bhqk,bkhd->bqhd', p, v.astype(jnp.float32))
    return o.reshape(B, S, MEM_WIDTH).astype(q_raw.dtype)

def second_inputs(seed: int = 0) -> dict:
    key = jax.random.key(seed)
    ks = jax.random.split(key, 32)
    f32 = jnp.float32

    def dense(k, shape, fan_in):
        return jax.random.normal(k, shape, f32) * (fan_in ** -0.5)

    def gain(k, shape):
        return 1.0 + 0.05 * jax.random.normal(k, shape, f32)

    L = DEPTH
    x = jax.random.normal(ks[0], (BATCH, SEQ, D_MODEL), f32)
    mem = jax.random.normal(ks[1], (BATCH, N_MEM, D_MODEL), f32)
    offset = jax.random.randint(ks[2], (BATCH, 1), 0, 4096, dtype=jnp.int32)
    positions = offset + jnp.arange(SEQ, dtype=jnp.int32)[None, :]
    return {
        'x': x,
        'mem': mem,
        'positions': positions,
        'norm_mix': gain(ks[3], (L, D_MODEL)),
        'norm_mem': gain(ks[4], (L, D_MODEL)),
        'w_in': dense(ks[5], (L, D_MODEL, IN_WIDTH), D_MODEL),
        'q_a_norm': gain(ks[6], (L, Q_LORA)),
        'w_uq': dense(ks[7], (L, Q_LORA, MLA_HEADS * QK_HEAD), Q_LORA),
        'kv_a_norm': gain(ks[8], (L, KV_LORA)),
        'w_ukv': dense(ks[9], (L, KV_LORA, MLA_HEADS * (QK_NOPE + V_HEAD)), KV_LORA),
        'mla_q_norm': gain(ks[10], (L, QK_HEAD)),
        'mla_k_norm': gain(ks[11], (L, QK_HEAD)),
        'hg_lb_logits': 0.1 * jax.random.normal(ks[12], (L + 1, HG_KWIDTH), f32),
        'hg_out_norm': gain(ks[13], (L, HG_WIDTH)),
        'w_mem_kv': dense(ks[14], (L, D_MODEL, 2 * MEM_WIDTH), D_MODEL),
        'mem_q_norm': gain(ks[15], (L, MEM_HEAD_DIM)),
        'mem_k_norm': gain(ks[16], (L, MEM_HEAD_DIM)),
        'mla_out_norm': gain(ks[17], (L, MLA_WIDTH)),
        'mem_out_norm': gain(ks[18], (L, MEM_WIDTH)),
        'w_out': dense(ks[19], (L, MIX_WIDTH, D_MODEL), MIX_WIDTH),
        'norm_ffn': gain(ks[20], (L, D_MODEL)),
        'w_gate': dense(ks[21], (L, D_MODEL, D_FF_2), D_MODEL),
        'w_up': dense(ks[22], (L, D_MODEL, D_FF_2), D_MODEL),
        'w_down': dense(ks[23], (L, D_FF_2, D_MODEL), D_FF_2),
    }

def second_block(x, mem, positions, norm_mix, norm_mem, w_in, q_a_norm, w_uq, kv_a_norm, w_ukv,
              mla_q_norm, mla_k_norm, hg_lb_logits, hg_out_norm, w_mem_kv, mem_q_norm, mem_k_norm,
              mla_out_norm, mem_out_norm, w_out, norm_ffn, w_gate, w_up, w_down):
    lb_all = jnp.cumsum(jax.nn.softmax(hg_lb_logits.astype(jnp.float32), axis=0), axis=0)
    offsets = [0]
    for sz in IN_SIZES_2:
        offsets.append(offsets[-1] + sz)
    for l in range(DEPTH):
        h = rmsnorm_2(x, norm_mix[l])
        mem_h = rmsnorm_2(mem, norm_mem[l])
        proj = h @ w_in[l]
        c_q, c_kv, k_rope, hq, hf, hi, hg, mq = [proj[..., offsets[j]:offsets[j + 1]] for j in range(len(IN_SIZES_2))]
        y_mla = mla_group(c_q, c_kv, k_rope, positions, q_a_norm[l], w_uq[l], kv_a_norm[l], w_ukv[l],
                          mla_q_norm[l], mla_k_norm[l])
        y_hg = hgrn2_group(hq, hf, hi, hg, lb_all[l], hg_out_norm[l])
        y_mem = mem_group(mq, mem_h, w_mem_kv[l], mem_q_norm[l], mem_k_norm[l])
        mix = jnp.concatenate([rmsnorm_2(y_mla, mla_out_norm[l]), y_hg, rmsnorm_2(y_mem, mem_out_norm[l])], axis=-1)
        x = x + (mix @ w_out[l]).astype(x.dtype)
        h2 = rmsnorm_2(x, norm_ffn[l])
        x = x + ((jax.nn.silu(h2 @ w_gate[l]) * (h2 @ w_up[l])) @ w_down[l]).astype(x.dtype)
    return x


def setup_inputs(seed=0):
    out = dict(first_inputs(seed))
    for name, value in second_inputs(seed + 1).items():
        if name != "x":
            out[name + "_2"] = value
    return out


def reference(
    x, w_in, conv_w, w_conv_out, cmp_pos_k, cmp_w1_k, cmp_w2_k, cmp_pos_v, cmp_w1_v, cmp_w2_v,
    w_attn_out, w_o, g_mix, g_ffn, w_gate, w_up, w_down, g_final, mem_2, positions_2,
    norm_mix_2, norm_mem_2, w_in_2, q_a_norm_2, w_uq_2, kv_a_norm_2, w_ukv_2, mla_q_norm_2,
    mla_k_norm_2, hg_lb_logits_2, hg_out_norm_2, w_mem_kv_2, mem_q_norm_2, mem_k_norm_2,
    mla_out_norm_2, mem_out_norm_2, w_out_2, norm_ffn_2, w_gate_2, w_up_2, w_down_2,
):
    x = first_block(
        x, w_in, conv_w, w_conv_out, cmp_pos_k, cmp_w1_k, cmp_w2_k, cmp_pos_v, cmp_w1_v,
        cmp_w2_v, w_attn_out, w_o, g_mix, g_ffn, w_gate, w_up, w_down, g_final,
    )
    return second_block(
        x, mem_2, positions_2, norm_mix_2, norm_mem_2, w_in_2, q_a_norm_2, w_uq_2, kv_a_norm_2,
        w_ukv_2, mla_q_norm_2, mla_k_norm_2, hg_lb_logits_2, hg_out_norm_2, w_mem_kv_2,
        mem_q_norm_2, mem_k_norm_2, mla_out_norm_2, mem_out_norm_2, w_out_2, norm_ffn_2,
        w_gate_2, w_up_2, w_down_2,
    )


_drawn_inputs = setup_inputs


def setup_inputs(seed=0):
    import zlib

    import numpy as np

    out = dict(_drawn_inputs(seed))
    spreads = {}
    factors = {'cmp_pos_k': 8.0,
     'q_a_norm_2': 2.721,
     'mla_q_norm_2': 2.776,
     'mla_k_norm_2': 2.769,
     'hg_lb_logits_2': 8.0,
     'hg_out_norm_2': 3.986,
     'mem_q_norm_2': 3.381,
     'mla_out_norm_2': 3.414,
     'mem_out_norm_2': 3.598,
     'norm_ffn_2': 4.468}
    for name, (base, spread) in spreads.items():
        noise = np.random.default_rng([zlib.crc32(name.encode()), seed]).standard_normal(out[name].shape)
        drawn = base * np.exp(spread * noise) if base else spread * noise
        out[name] = __import__('jax').numpy.asarray(drawn.astype(out[name].dtype))
    for name, factor in factors.items():
        out[name] = (out[name] * factor).astype(out[name].dtype)
    return out
```

```python
from contextlib import ExitStack

import numpy as np

import concourse.bass as bass
from concourse import mybir

F32 = mybir.dt.float32
F32R = mybir.dt.float32r
I32 = mybir.dt.int32
ALU = mybir.AluOpType
ACT = mybir.ActivationFunctionType
AX = mybir.AxisListType

P = 128
D = 1024
S = 512
TT = S // P
KC = D // P
CONV = 512
CW = 3
NH, NKV, HD = 16, 4, 64
GROUP = NH // NKV
CMP_LEN, CMP_STRIDE, CMP_HID = 32, 16, 256
NCMP = (S - CMP_LEN) // CMP_STRIDE + 1
NPAIR = CMP_LEN // 2
DFF = 2816
FC = DFF // P
EPS = 1e-6
NEG = -1e30
FLOOR = -1e29

NMEM = 256
QLORA, KVLORA, ROPE, NOPE, VH = 384, 256, 64, 128, 128
QKH = NOPE + ROPE
H2 = 4
W2 = 512
MIX2 = 3 * W2
LEVELS = 7

C_B, C_C, C_H, C_Q = 0, CONV, 2 * CONV, 3 * CONV
C_KC = C_Q + NH * HD
C_VC, C_KS, C_VS, C_KW, C_VW = (C_KC + 256 * n for n in range(1, 6))
C_BR = C_VW + 256
C_GC = C_BR + 3 * NH
C_GA = C_GC + D
I_CQ, I_CKV, I_KR = 0, QLORA, QLORA + KVLORA
I_HQ = I_KR + ROPE
I_HF, I_HI, I_HG, I_MQ = (I_HQ + W2 * n for n in range(1, 5))

CONST_COLS = {}
_at = 0
for _name, _n in (("ident", P), ("causal", S), ("cmp", TT * NCMP), ("ones", P), ("rot", P),
                  ("freq", 1), ("eps", 1), ("level", (LEVELS + 1) * P)):
    CONST_COLS[_name] = (_at, _at + _n)
    _at += _n
NCONST = _at

GAIN_ROWS = {}
_at = 0
for _name, _n in (("g_mix", 8), ("g_ffn", 8), ("g_final", 8), ("conv_w", CW * 4), ("pos_k", NPAIR),
                  ("pos_v", NPAIR), ("norm_mix", 8), ("norm_mem", 8), ("q_a", 3), ("kv_a", 2),
                  ("mla_q", 2), ("mla_k", 2), ("lb", 8), ("hg_out", 4), ("mem_q", 1), ("mem_k", 1),
                  ("mla_out", 4), ("mem_out", 4), ("norm_ffn", 8)):
    GAIN_ROWS[_name] = _at
    _at += _n
NGAIN = _at


def shape_constants():
    c = np.zeros((P, NCONST), np.float32)

    def put(name, value):
        a, b = CONST_COLS[name]
        c[:, a:b] = value.reshape(P, b - a)

    i = np.arange(P)
    put("ident", np.eye(P, dtype=np.float32))
    causal = np.zeros((P, S), np.float32)
    causal[:, S - P:] = np.where(i[None, :] > i[:, None], NEG, 0.0)
    put("causal", causal)
    t = np.arange(TT)[None, :, None] * P + i[:, None, None]
    end = np.arange(NCMP)[None, None, :] * CMP_STRIDE + CMP_LEN - 1
    put("cmp", np.where(end <= t, 0.0, NEG).astype(np.float32))
    put("ones", np.ones((P, P), np.float32))
    rot = np.zeros((P, P), np.float32)
    half = ROPE // 2
    for base in (0, ROPE):
        for k in range(half):
            rot[base + half + k, base + k] = -1.0
            rot[base + k, base + half + k] = 1.0
    put("rot", rot)
    freq = np.power(np.float32(10000.0), -np.arange(half, dtype=np.float32) / np.float32(half))
    put("freq", np.tile(freq.astype(np.float32), P // half)[:, None])
    put("eps", np.full((P, 1), EPS, np.float32))
    s, t = i[:, None], i[None, :]
    level = np.zeros((P, LEVELS + 1, P), np.float32)
    level[:, 0] = s == t
    for n in range(LEVELS):
        m = 1 << n
        level[:, n + 1] = (s // (2 * m) == t // (2 * m)) & (s // m % 2 == 0) & (t // m % 2 == 1)
    put("level", level)
    return c


class Signal:

    def __init__(self, sem):
        self.sem, self.n = sem, 0

    def reserve(self, n):
        base = self.n
        self.n += n
        return base


LOADS = {"q": 8, "kv_cmp": 1, "k": 2, "v": 2, "attn_out": 2, "up": 2, "up_2": 2, "lat_b": 3,
         "uq_nope": 4, "uq_rope": 4, "ukv_k": 4, "ukv_v": 4}


class Job:

    def __init__(self, name, blocks, panels, chunks, groups, freed_by, cols, rows=P, natural=False,
                 tokens=S, banks=None):
        self.name, self.blocks, self.panels, self.chunks, self.groups = name, blocks, panels, chunks, groups
        self.freed_by, self.cols, self.rows, self.natural, self.tokens = freed_by, cols, rows, natural, tokens
        self.tiles = len(freed_by)
        self.banks = banks or list(range(self.tiles))
        self.used = chunks * cols
        self.loads = LOADS.get(name, 1)
        self.looped = blocks >= 3 and panels % 2 == 0
        self.last_group = {}
        self.end_of_panel = {}
        for n, (panel, tile, _) in enumerate(groups):
            self.last_group[tile] = n + 1
            self.end_of_panel[panel] = n + 1


def wide(chunks, tiles, panels):
    return [(h, t, [(k, h * chunks + k) for k in range(chunks)]) for h in range(panels) for t in range(tiles)]


def deep(chunks, tiles):
    return [(2 * t + h, t, [(k, h * chunks + k) for k in range(chunks)]) for t in range(tiles) for h in range(2)]


def make_jobs():
    a, v = "act", "dve"
    return [
        Job("conv_in", 3, 2, 4, wide(4, 4, 2), [a] * 4, 512),
        Job("gate_attn", 2, 2, 4, wide(4, 4, 2), [a] * 4, 512),
        Job("conv_out", 2, 1, 4, wide(4, 4, 1), [v] * 4, 512),
        Job("gate_conv", 2, 2, 4, wide(4, 4, 2), [a] * 4, 512),
        Job("q", 2, 2, 4, wide(4, 4, 2), [a] * 4, 512),
        Job("kv_cmp", 1, 2, 4, wide(4, 4, 2), [v] * 4, 512),
        Job("k", 1, 2, 4, wide(4, 4, 2), [a] * 4, 512),
        Job("v", 1, 2, 4, wide(4, 4, 2), [a] * 4, 512, natural=True),
        Job("gates", 1, 1, 8, wide(8, 4, 1), [a] * 4, 3 * NH, natural=True),
        Job("cmp_k", 1, 2, 8, wide(8, 2, 2), [a] * 2, CMP_HID, tokens=NKV * NCMP),
        Job("cmp_v", 1, 2, 8, wide(8, 2, 2), [a] * 2, CMP_HID, tokens=NKV * NCMP, banks=[2, 3]),
        Job("attn_out", 2, 2, 4, wide(4, 4, 2), [v] * 4, 512),
        Job("w_o", 2, 2, 4, wide(4, 4, 2), [v] * 4, 512),
        Job("up", 11, 2, 4, wide(4, 4, 2), [a, a, "val", "val"], 512),
        Job("down", 4, 4, 11, deep(11, 2), [v] * 2, P),
        Job("mem_k", 1, 2, 4, wide(4, 4, 2), [a] * 4, 512, tokens=NMEM),
        Job("mem_v", 1, 2, 4, wide(4, 2, 2), [a] * 2, 512, natural=True),
        Job("f", 1, 2, 4, wide(4, 4, 2), [a] * 4, 512),
        Job("hq", 1, 2, 4, wide(4, 4, 2), [a] * 4, 512),
        Job("lat_a", 1, 2, 4, wide(4, 4, 2), [a] * 4, 512),
        Job("lat_b", 1, 2, 4, wide(4, 2, 2), [a] * 2, 256),
        Job("mq", 1, 2, 4, wide(4, 4, 2), [a] * 4, 512),
        Job("i", 1, 2, 4, wide(4, 4, 2), [a] * 4, 512, natural=True),
        Job("g", 1, 2, 4, wide(4, 4, 2), [a] * 4, 512),
        Job("uq_nope", 1, 1, 3, wide(3, 4, 1), [a] * 4, 512),
        Job("uq_rope", 1, 1, 3, wide(3, 2, 1), [a] * 2, 256),
        Job("ukv_k", 1, 1, 2, wide(2, 4, 1), [a] * 4, 512),
        Job("ukv_v", 1, 1, 2, wide(2, 4, 1), [a] * 4, 512, natural=True),
        Job("w_out", 2, 3, 4, wide(4, 4, 3), [v] * 4, 512),
        Job("up_2", 11, 2, 4, wide(4, 4, 2), [a, a, "val", "val"], 512),
        Job("down_2", 4, 4, 11, deep(11, 2), [v] * 2, P),
    ]


def plan(jobs, signals, splits, before, split):
    ends, loads, panel, group = [], [0, 0], 0, 0
    tenant = {}
    for job in jobs:
        if job.name in before:
            for name, n in before[job.name]:
                split[name] = signals["val"].reserve(n)
        if job.name in splits:
            job.split0 = signals["val"].reserve(splits[job.name])
        job.panel0, job.group0, job.load0 = panel, group, list(loads)
        job.free0 = {f: job.split0 if f == "val" else signals[f].n for f in set(job.freed_by)}
        job.tenant0 = {b: tenant.get(b) for b in job.banks}
        for f in job.freed_by:
            if f != "val":
                signals[f].reserve(job.blocks)
        for i in range(job.blocks):
            for h in range(job.panels):
                ends.append(group + len(job.groups) * i + job.end_of_panel[h])
                loads[(panel + job.panels * i + h) % 2] += job.loads
        panel += job.blocks * job.panels
        group += job.blocks * len(job.groups)
        for t, b in enumerate(job.banks):
            tenant[b] = (job.freed_by[t], freed(job, t, job.blocks - 1))
    return ends


def freed(job, tile, block):
    f = job.freed_by[tile]
    each = job.freed_by.count(f)
    return job.free0[f] + each * block + job.freed_by[:tile].count(f) + 1


def tile_done(job, tile, block):
    return job.group0 + len(job.groups) * block + job.last_group[tile]


def build(nc, A, out):
    KB = 1024
    BASE = 16 * KB + 128

    def at(name, shape, dt, kb):
        return nc.alloc_sbuf_tensor_at(name, shape, dt, offset=BASE + int(kb * KB))

    raw = [at(f"raw{n}", [P, 2048], F32, 8 * n) for n in range(2)]
    w_hi = [at(f"w_hi{n}", [P, 2048], F32R, 16 + 8 * n) for n in range(2)]
    w_lo = [at(f"w_lo{n}", [P, 2048], F32R, 32 + 8 * n) for n in range(2)]
    consts = at("consts", [P, NCONST], F32, 48)
    gains = at("gains", [P, P], F32, 56.5)
    stat = at("stat", [P, 4, 4, 8], F32, 57)
    h = at("h", [P, KC, S], F32, 58)
    XN, AR, TAIL = 74, 106, 202
    xn_hi = at("xn_hi", [P, KC, S], F32R, XN)
    xn_lo = at("xn_lo", [P, KC, S], F32R, XN + 16)
    val = [at(f"val{n}", [P, S], F32, TAIL + 2 * n) for n in range(2)]
    w2k = at("w2k", [P, 2, P], F32, TAIL + 4)
    w2v = at("w2v", [P, 2, HD], F32, TAIL + 5)

    sq = [at(f"sq{n}", [P, S], F32, AR + 88 + 2 * n) for n in range(2)]
    rstd = [at(f"rstd{n}", [P, S], F32, AR + 92 + 2 * n) for n in range(2)]

    x_rows = at("x_rows", [P, TT, D], F32, AR)
    gain_rows = at("gain_rows", [P, P], F32, AR + 16)
    bch = at("bch", [P, 12, S], F32, AR)
    u = at("u", [P, 4, S + 2], F32, AR + 24)
    cv_hi = at("cv_hi", [P, 4, S], F32R, AR + 72.75)
    cv_lo = at("cv_lo", [P, 4, S], F32R, AR + 80.75)
    g_attn = at("g_attn", [P, KC, S], F32, AR + 40.75)
    mixc = at("mixc", [P, KC, S], F32, AR + 56.75)
    sig = at("sig", [P, 2, S], F32, AR + 88.75)
    q = at("q", [P, KC, S], F32, AR)
    kT = at("kT", [P, 4, S], F32, AR + 16)
    gates = at("gates", [P, 3 * NH, TT], F32, AR + 24)
    v_rows = at("v_rows", [P, TT, 2 * NKV * HD], F32, AR + 25)
    blk = [at("blk_k", [P, NPAIR, NKV, NCMP], F32, AR + 33), at("blk_v", [P, NPAIR, NKV, NCMP], F32, AR + 88.25)]
    blk_hi = [at("blk_k_hi", [P, NPAIR, NKV * NCMP], F32R, AR + 72.75),
              at("blk_v_hi", [P, NPAIR, NKV * NCMP], F32R, XN)]
    blk_lo = [at("blk_k_lo", [P, NPAIR, NKV * NCMP], F32R, AR + 80.5),
              at("blk_v_lo", [P, NPAIR, NKV * NCMP], F32R, XN + 7.75)]
    PW = 1280 + TT * NCMP
    prob = [at(f"prob{n}", [P, PW], F32, XN + 5.5 * n) for n in range(4)]
    k_cmp = at("k_cmp", [P, NKV * NCMP], F32, XN + 22.25)
    v_cmp = at("v_cmp", [P, NKV, HD], F32, XN + 23)
    hid_cmp = [at(f"hid_cmp{n}", [P, 2, NKV * NCMP], F32, XN + 24 + n) for n in range(2)]
    pT = [[at(f"pT{n}_{b}", [P, S], F32, AR + 72.75 + 8 * n + 2 * b) for b in range(4 - n)] for n in range(2)]
    o_pair = at("o_pair", [P, TT, 2, HD], F32, AR + 86.75)
    o_w = at("o_w", [P, 8, HD], F32, AR + 88.75)
    q_s = at("q_s", [P, S], F32, AR + 90.75)
    oT = q
    o_hi = at("o_hi", [P, KC, S], F32R, AR + 16)
    o_lo = at("o_lo", [P, KC, S], F32R, XN)
    mix_hi = at("mix_hi", [P, KC, S], F32R, XN + 16)
    mix_lo = at("mix_lo", [P, KC, S], F32R, AR)
    mixp = at("mixp", [P, S], F32, AR + 88.75)

    hid_hi = at("hid_hi", [P, FC, S], F32R, AR)
    hid_lo = at("hid_lo", [P, FC, S], F32R, AR + 44)
    silu = at("silu", [P, 2, S], F32, AR + 88)

    mem_rows = at("mem_rows", [P, 2, D], F32, XN)
    memT = at("memT", [P, KC, NMEM], F32, XN + 8)
    mem_hi = at("mem_hi", [P, KC, NMEM], F32R, XN + 16)
    mem_lo = at("mem_lo", [P, KC, NMEM], F32R, XN + 24)
    mem_k = at("mem_k", [P, H2, NMEM], F32, AR + 76)
    mem_v = at("mem_v", [P, 2, W2], F32, AR + 80)
    pre = at("pre", [P, H2, S], F32, AR)
    suf = at("suf", [P, H2, S], F32, AR + 8)
    hq = at("hq", [P, H2, S], F32, AR + 16)
    hk = at("hk", [P, H2, S], F32, AR + 24)
    qt = at("qt", [P, H2, S], F32, AR + 32)
    kt_ = at("kt", [P, H2, S], F32, AR + 40)
    aT = at("aT", [P, H2, S], F32, AR + 48)
    mq = at("mq", [P, H2, S], F32, AR + 56)
    cq = at("cq", [P, 3, S], F32, AR + 64)
    ckv = at("ckv", [P, 2, S], F32, AR + 70)
    kr = at("kr", [P, S], F32, AR + 74)
    hv = at("hv", [P, TT, W2], F32, AR)
    sg = at("sg", [P, H2, S], F32, AR + 8)
    cq_hi = at("cq_hi", [P, 3, S], F32R, AR + 16)
    cq_lo = at("cq_lo", [P, 3, S], F32R, AR + 22)
    ckv_hi = at("ckv_hi", [P, 2, S], F32R, AR + 28)
    ckv_lo = at("ckv_lo", [P, 2, S], F32R, AR + 84)
    state = at("state", [P, H2, P], F32, XN)
    k_rows = at("k_rows", [P, 3, W2], F32, XN + 2)
    o_rows = at("o_rows", [P, TT, W2], F32, XN + 16)
    hgm_hi = at("hgm_hi", [P, 4, S], F32R, XN)
    hgm_lo = at("hgm_lo", [P, 4, S], F32R, XN + 8)
    qn = at("qn", [P, H2, S], F32, AR + 32)
    qr = at("qr", [P, 2, S], F32, AR + 40)
    krh = at("krh", [P, 2, S], F32, AR + 44)
    kn = at("kn", [P, H2, S], F32, AR + 48)
    v2 = at("v2", [P, TT, W2], F32, AR)
    cos = at("cos", [P, S], F32, AR + 64)
    sin = at("sin", [P, S], F32, AR + 66)
    krb = at("krb", [P, S], F32, AR + 68)
    ra = at("ra", [P, S], F32, AR + 70)
    rb = at("rb", [P, S], F32, AR + 72)
    pos_i = at("pos_i", [P, S], I32, AR + 70)
    prob2 = [at(f"prob2_{n}", [P, 1280], F32, AR + 16 + 5 * n) for n in range(3)]
    pT2 = [[at(f"pT2_{n}_{b}", [P, S], F32, XN + 16 + 6 * n + 2 * b) for b in range(3)] for n in range(2)]
    y_mla = at("y_mla", [P, TT, W2], F32, AR + 8)
    y_mem = at("y_mem", [P, TT, W2], F32, AR)
    mlam_hi = at("mlam_hi", [P, 4, S], F32R, AR + 32)
    mlam_lo = at("mlam_lo", [P, 4, S], F32R, AR + 40)
    memm_hi = at("memm_hi", [P, 4, S], F32R, AR + 16)
    memm_lo = at("memm_lo", [P, 4, S], F32R, AR + 48)
    small = at("small", [P, 128], F32, TAIL + 4)
    decay = small[:, 0:16].rearrange("p (h c) -> p h c", c=TT)
    ssq, rroot, rinv = small[:, 16:32], small[:, 32:48], small[:, 48:64]
    lbv = small[:, 64:96]
    squares = [at("squares0", [P, TT, W2], F32, XN), at("squares1", [P, TT, W2], F32, AR + 64)]
    out_rows = at("out_rows", [P, TT, D], F32, AR)

    ctx = ExitStack()
    with ctx:
        ps = [ctx.enter_context(nc.psum_tensor(f"bank{n}", [P, 512], F32)) for n in range(8)]

        def sem(name):
            return ctx.enter_context(nc.semaphore(name))

        raw_loaded = [sem(f"raw_loaded{n}") for n in range(2)]
        w_hi_done, w_lo_done, gemm_done = sem("w_hi_done"), sem("w_lo_done"), sem("gemm_done")
        signals = {f: Signal(sem(f"{f}_freed")) for f in ("act", "dve")}
        signals["val"] = Signal(sem("val_ready"))
        val_ready = signals["val"].sem
        hi_ready, lo_ready = sem("hi_ready"), sem("lo_ready")
        step = Signal(sem("dve_step"))
        x_loaded, consts_loaded, gains_loaded, w2_loaded = (sem(f"{n}_loaded") for n in ("x", "consts", "gains", "w2"))
        xT_done, h_ready, gains_ready = sem("xT_done"), sem("h_ready"), sem("gains_ready")
        gainsT_done = sem("gainsT_done")
        sq_ready, sq_used, root_ready, rstd_ready = (sem(n) for n in ("sq_ready", "sq_used", "root_ready", "rstd_ready"))
        conv_in_ready = sem("conv_in_ready")
        mixc_ready = sem("mixc_ready")
        blk_hi_ready, blk_lo_ready = sem("blk_hi_ready"), sem("blk_lo_ready")
        cmp_done, cmp_ready = sem("cmp_done"), sem("cmp_ready")
        q_staged, scores_done, scores_taken, negm_ready, exp_done = (
            sem(n) for n in ("q_staged", "scores_done", "scores_taken", "negm_ready", "exp_done"))
        pT_done, pT_act, pT_dve, pv_done, o_taken, o_part, pair_done = (
            sem(n) for n in ("pT_done", "pT_act", "pT_dve", "pv_done", "o_taken", "o_part", "pair_done"))
        memT_done, memT_ready, mem_loaded = sem("memT_done"), sem("memT_ready"), sem("mem_loaded")
        decay_logs, level_exp, level_mul, level_moved, level_done, level_kept = (
            sem(n) for n in ("decay_logs", "level_exp", "level_mul", "level_moved", "level_done", "level_kept"))
        between_ready = sem("between_ready")
        f_ready, hk_ready, hq_ready, lb_exp = sem("f_ready"), sem("hk_ready"), sem("hq_ready"), sem("lb_exp")
        k_turned, k_rows_ready, chunk_done, state_ready, chunk_out = (
            sem(n) for n in ("k_turned", "k_rows_ready", "chunk_done", "state_ready", "chunk_out"))
        part_sq, part_used, part_root, part_ready = (sem(n) for n in ("part_sq", "part_used", "part_root", "part_ready"))
        pos_loaded, angle_ready, angle_sin, rot_done, rope_ready = (
            sem(n) for n in ("pos_loaded", "angle_ready", "angle_sin", "rot_done", "rope_ready"))
        scores2, taken2, negm2, exp2, turned2, pT2_act, pT2_dve, pv2, y_ready = (
            sem(n) for n in ("scores2", "taken2", "negm2", "exp2", "turned2", "pT2_act", "pT2_dve", "pv2", "y_ready"))
        rows_sq, rows_root, rows_ready, rows_turned = (
            sem(n) for n in ("rows_sq", "rows_root", "rows_ready", "rows_turned"))
        out_turned, out_act, out_dve = sem("out_turned"), sem("out_act"), sem("out_dve")
        out_sent = sem("out_sent")
        pool_waited, dve_waited = sem("pool_waited"), sem("dve_waited")

        jobs = {}
        for job in make_jobs():
            jobs[job.name] = job

        SPLIT = {"norm_mix": signals["val"].reserve(8), "conv": signals["val"].reserve(4),
                 "o": signals["val"].reserve(8)}
        splits = {"attn_out": 8, "up": FC, "up_2": FC}
        order = list(jobs.values())
        PRE = {"up": [("norm_ffn", 8)], "mem_k": [("norm_mem", 8), ("norm_mix_2", 8)],
               "i": [("cq", 3), ("ckv", 2)], "w_out": [("hgm", 4), ("mlam", 4), ("memm", 4)],
               "up_2": [("norm_ffn_2", 8)]}
        ends = plan(order, signals, splits, PRE, SPLIT)

        def const(name, *idx):
            a, b = CONST_COLS[name]
            return consts[:, a:b]

        ident = const("ident")
        ones = const("ones")

        def gain(name, c=0):
            r = GAIN_ROWS[name] + c
            return gains[:, r:r + 1]

        def mask_of(w):
            a, b = CONST_COLS["causal"]
            return consts[:, b - w:b]

        W_IN = A["w_in"][0].rearrange("(c p) n -> p c n", p=P)

        def in_cols(a, n, h, chunks=4):
            return W_IN[:, chunks * h:chunks * h + chunks, bass.ds(a, n)]

        def panel_view(slot, job, tensors=raw):
            return tensors[slot][:, 0:job.used].rearrange("p (k n) -> p k n", k=job.chunks)

        def chunk(name, K):
            if name == "w_out":
                part = [(mlam_hi, mlam_lo), (hgm_hi, hgm_lo), (memm_hi, memm_lo)][K // 4]
                return part[0][:, K % 4, :], part[1][:, K % 4, :]
            return operand[name][0][:, K, :], operand[name][1][:, K, :]

        def wide_load(w):
            def load(dst, i, hh):
                return [(dst, w[:, 4 * hh:4 * hh + 4, bass.ds(512 * i, 512)])]
            return load

        def in_load(first):
            def load(dst, i, hh):
                return [(dst, in_cols(512 * i + first, 512, hh))]
            return load

        def in_load2(a, b):
            def load(dst, i, hh):
                return [(dst[:, :, 0:256], in_cols(a, 256, hh)), (dst[:, :, 256:512], in_cols(b, 256, hh))]
            return load

        def q_load(dst, i, hh):
            pairs = dst.rearrange("p k (t a d) -> p k t a d", t=4, a=2)
            return [(pairs[:, k, :, a, :],
                     in_cols(C_Q + 512 * i + 256 * a, 256, hh)[:, k].rearrange("p (t d) -> p t d", t=4))
                    for a in range(2) for k in range(4)]

        def gates_load(dst, i, hh):
            return [(dst, in_cols(C_BR, 3 * NH, 0, 8))]

        def cmp_load(name):
            w = A[name][0].rearrange("(c p) n -> p c n", p=P)

            def load(dst, i, hh):
                return [(dst, w[:, 8 * hh:8 * hh + 8, :])]
            return load

        def attn_out_load(dst, i, hh):
            w = A["w_attn_out"][0].rearrange("(a g j d) n -> a g d j n", a=2, g=2, j=4)
            return [(dst[64 * g:64 * g + 64], w[hh, g, :, :, 512 * i:512 * i + 512]) for g in range(2)]

        def up_load(gate, up):
            wg = A[gate][0].rearrange("(c p) n -> p c n", p=P)
            wu = A[up][0].rearrange("(c p) n -> p c n", p=P)

            def load(dst, i, hh):
                return [(dst[:, :, 0:256], wg[:, 4 * hh:4 * hh + 4, bass.ds(256 * i, 256)]),
                        (dst[:, :, 256:512], wu[:, 4 * hh:4 * hh + 4, bass.ds(256 * i, 256)])]
            return load

        def down_load(name):
            w = A[name][0].rearrange("(c p) n -> p c n", p=P)

            def load(dst, i, hh):
                k = hh % 2
                return [(dst, w[:, 11 * k:11 * k + 11, bass.ds(256 * i + P * (hh // 2), P)])]
            return load

        def rows_load(name):
            return wide_load(A[name][0].rearrange("(c p) n -> p c n", p=P))

        W_IN2 = A["w_in_2"][0].rearrange("(c p) n -> p c n", p=P)

        def in2(first, n=512):
            def load(dst, i, hh):
                return [(dst, W_IN2[:, 4 * hh:4 * hh + 4, first:first + n])]
            return load

        def lat_b_load(dst, i, hh):
            k = slice(4 * hh, 4 * hh + 4)
            return [(dst[:, :, 0:P], W_IN2[:, k, 512:512 + P])] + [
                (dst[:, :, P + ROPE * x:P + ROPE * x + ROPE], W_IN2[:, k, I_KR:I_KR + ROPE]) for x in range(2)]

        def heads_load(name, each, first, width):
            w = A[name][0].rearrange("(c p) n -> p c n", p=P)

            def load(dst, i, hh):
                return [(dst[:, :, width * n:width * n + width], w[:, :, each * n + first:each * n + first + width])
                        for n in range(H2)]
            return load

        def mem_load(first):
            w = A["w_mem_kv_2"][0].rearrange("(c p) n -> p c n", p=P)

            def load(dst, i, hh):
                return [(dst, w[:, 4 * hh:4 * hh + 4, first:first + 512])]
            return load

        load_of = {
            "mem_k": mem_load(0), "mem_v": mem_load(512), "f": in2(I_HF), "hq": in2(I_HQ), "lat_a": in2(0),
            "lat_b": lat_b_load, "mq": in2(I_MQ), "i": in2(I_HI), "g": in2(I_HG),
            "uq_nope": heads_load("w_uq_2", QKH, 0, NOPE), "uq_rope": heads_load("w_uq_2", QKH, NOPE, ROPE),
            "ukv_k": heads_load("w_ukv_2", NOPE + VH, 0, NOPE), "ukv_v": heads_load("w_ukv_2", NOPE + VH, NOPE, VH),
            "w_out": rows_load("w_out_2"), "up_2": up_load("w_gate_2", "w_up_2"), "down_2": down_load("w_down_2"),
            "conv_in": in_load(0), "gate_attn": in_load(C_GA), "conv_out": rows_load("w_conv_out"),
            "gate_conv": in_load(C_GC), "q": q_load, "kv_cmp": in_load(C_KC), "k": in_load2(C_KS, C_KW),
            "v": in_load2(C_VS, C_VW), "gates": gates_load, "cmp_k": cmp_load("cmp_w1_k"),
            "cmp_v": cmp_load("cmp_w1_v"), "attn_out": attn_out_load, "w_o": rows_load("w_o"),
            "up": up_load("w_gate", "w_up"), "down": down_load("w_down"),
        }
        operand = {
            "mem_k": (mem_hi, mem_lo), "mem_v": (mem_hi, mem_lo), "f": (xn_hi, xn_lo), "hq": (xn_hi, xn_lo),
            "lat_a": (xn_hi, xn_lo), "lat_b": (xn_hi, xn_lo), "mq": (xn_hi, xn_lo), "i": (xn_hi, xn_lo),
            "g": (xn_hi, xn_lo), "uq_nope": (cq_hi, cq_lo), "uq_rope": (cq_hi, cq_lo), "ukv_k": (ckv_hi, ckv_lo),
            "ukv_v": (ckv_hi, ckv_lo), "w_out": None, "up_2": (xn_hi, xn_lo), "down_2": (hid_hi, hid_lo),
            "conv_in": (xn_hi, xn_lo), "gate_attn": (xn_hi, xn_lo), "conv_out": (cv_hi, cv_lo),
            "gate_conv": (xn_hi, xn_lo), "q": (xn_hi, xn_lo), "kv_cmp": (xn_hi, xn_lo), "k": (xn_hi, xn_lo),
            "v": (xn_hi, xn_lo), "gates": (xn_hi, xn_lo), "cmp_k": (blk_hi[0], blk_lo[0]),
            "cmp_v": (blk_hi[1], blk_lo[1]), "attn_out": (o_hi, o_lo), "w_o": (mix_hi, mix_lo),
            "up": (xn_hi, xn_lo), "down": (hid_hi, hid_lo),
        }

        def split_wait(base):
            return lambda k: (lo_ready, base + k + 1)

        operand_ready = {
            "mem_k": split_wait(SPLIT["norm_mem"]), "f": split_wait(SPLIT["norm_mix_2"]),
            "uq_nope": split_wait(SPLIT["cq"]), "ukv_k": split_wait(SPLIT["ckv"]), "w_out": lambda k: (lo_ready, SPLIT["memm"] + 4),
            "up_2": split_wait(SPLIT["norm_ffn_2"]), "down_2": split_wait(jobs["up_2"].split0),
            "conv_in": split_wait(SPLIT["norm_mix"]), "conv_out": split_wait(SPLIT["conv"]),
            "cmp_k": lambda k: (blk_lo_ready, 1), "cmp_v": lambda k: (blk_lo_ready, 2),
            "attn_out": split_wait(SPLIT["o"]), "w_o": split_wait(jobs["attn_out"].split0),
            "up": split_wait(SPLIT["norm_ffn"]), "down": split_wait(jobs["up"].split0),
        }

        def over_blocks(eng, job, body, ahead=0):
            body(0)
            if job.looped:
                with eng.Fori(1, job.blocks) as i:
                    body(i)
            else:
                for i in range(1, job.blocks):
                    body(i)

        def loads_until(job, i, hh):
            slot = (job.panel0 + hh) % 2 if job.looped else (job.panel0 + job.panels * i + hh) % 2
            if job.looped:
                before = i * (job.panels // 2) + len([x for x in range(hh) if (hh - x) % 2 == 0]) + 1
            else:
                n = job.panels * i + hh
                before = len([x for x in range(n + 1) if (n - x) % 2 == 0])
            return slot, job.load0[slot] + job.loads * before

        def end_before(job, i, hh):
            if isinstance(i, int):
                p = job.panel0 + job.panels * i + hh
                return ends[p - 2] if p >= 2 else None
            g = len(job.groups)
            if hh >= 2:
                return job.group0 + g * i + job.end_of_panel[hh - 2]
            return job.group0 + g * (i - 1) + job.end_of_panel[hh - 2 + job.panels]

        def sp_job(sp, name):
            job = jobs[name]

            def block(i):
                for hh in range(job.panels):
                    p = job.panel0 + job.panels * i + hh
                    slot = loads_until(job, 0 if job.looped else i, hh)[0]
                    if not isinstance(p, int) or p >= 2:
                        sp.wait_ge(w_lo_done, p - 1)
                    for dst, src in load_of[name](panel_view(slot, job), i, hh):
                        sp.dma_start(dst, src).then_inc(raw_loaded[slot], 16)
            over_blocks(sp, job, block)

        def pool_job(pool, name):
            job = jobs[name]

            def block(i):
                for hh in range(job.panels):
                    p = job.panel0 + job.panels * i + hh
                    slot, n = loads_until(job, i, hh)
                    pool.wait_ge(raw_loaded[slot], n * 16)
                    e = end_before(job, i, hh)
                    if e is not None:
                        pool.wait_ge(gemm_done, e)
                    if not isinstance(i, int):
                        pool.sem_inc(pool_waited, 1)
                    src = raw[slot][:, 0:job.used]
                    hi, lo = w_hi[slot][:, 0:job.used], w_lo[slot][:, 0:job.used]
                    pool.tensor_scalar(hi, src, 1.0, 1.0, ALU.mult, ALU.mult).then_inc(w_hi_done, 1)
                    pool.wait_ge(w_hi_done, p + 1)
                    pool.tensor_tensor(lo, src, hi.bitcast(F32), ALU.subtract).then_inc(w_lo_done, 1)
            over_blocks(pool, job, block)

        def pe_job(pe, name, after=None):
            job = jobs[name]
            seen = set()

            def block(i):
                opened, started = set(), set()
                todo = job.groups
                spread = isinstance(i, int) and i == 0 and name in operand_ready and len(job.groups[0][2]) > 1 \
                    and job.panels < 4
                if spread:
                    now = [x for x in todo if x[0] == 0]
                    todo = [(0, t, [ks[n]]) for n in range(len(now[0][2])) for _, t, ks in now] + [
                        x for x in todo if x[0]]
                for panel, tile, ks in todo:
                    whole = not (spread and panel == 0)
                    p = job.panel0 + job.panels * i + panel
                    slot = loads_until(job, 0 if job.looped else i, panel)[0]
                    if panel not in opened:
                        opened.add(panel)
                        pe.wait_ge(w_lo_done, p + 1)
                    bank = ps[job.banks[tile]]
                    first = tile not in started
                    if first:
                        started.add(tile)
                        if not isinstance(i, int) or i > 0:
                            pe.wait_ge(signals[job.freed_by[tile]].sem, freed(job, tile, i - 1))
                        elif job.tenant0[job.banks[tile]]:
                            f, n = job.tenant0[job.banks[tile]]
                            pe.wait_ge(signals[f].sem, n)
                    last_of_tile = (panel, tile) == [(a, b) for a, b, _ in job.groups if b == tile][-1]
                    hi, lo = panel_view(slot, job, w_hi), panel_view(slot, job, w_lo)
                    for n, (k, K) in enumerate(ks):
                        if K not in seen:
                            seen.add(K)
                            if name in operand_ready:
                                pe.wait_ge(*operand_ready[name](K))
                        xh, xl = chunk(name, K)
                        last_k = n == len(ks) - 1 if whole else K == job.groups[0][2][-1][1]
                        begin, end = first and n == 0, last_of_tile and last_k
                        if job.natural:
                            o = bank[:, 0:job.cols]
                            a, b = xh[:, P * tile:P * tile + P], xl[:, P * tile:P * tile + P]
                            pe.matmul(o, a, hi[:, k, :], start=begin, stop=False)
                            pe.matmul(o, a, lo[:, k, :], start=False, stop=False)
                            mm = pe.matmul(o, b, hi[:, k, :], start=False, stop=end)
                        else:
                            o = bank[:, 0:job.tokens]
                            a = hi[:, k, P * tile:P * tile + P] if job.cols > P else hi[:, k, :]
                            b = lo[:, k, P * tile:P * tile + P] if job.cols > P else lo[:, k, :]
                            pe.matmul(o, a, xh, start=begin, stop=False)
                            pe.matmul(o, a, xl, start=False, stop=False)
                            mm = pe.matmul(o, b, xh, start=False, stop=end)
                    if last_k:
                        mm.then_inc(gemm_done, 1)
                    if last_k and after:
                        after(i, panel, tile)
            over_blocks(pe, job, block)

        def act_hi(act, n, dst, src=None, slot=None):
            act.wait_ge(val_ready, n + 1)
            act.activation(dst, val[slot][:, 0:dst.shape[-1]] if src is None else src, ACT.Copy).then_inc(hi_ready, 1)

        def val_free(dve, n):
            if not isinstance(n, int) or n >= 2:
                dve.wait_ge(lo_ready, n - 1)

        def dve_lo(dve, n, dst, hi, src=None, slot=None):
            dve.wait_ge(hi_ready, n + 1)
            dve.tensor_tensor(dst, val[slot][:, 0:dst.shape[-1]] if src is None else src, hi.bitcast(F32),
                              ALU.subtract).then_inc(lo_ready, 1)

        norms = {}

        def add_norm(name, src, dst, gain_name, chunks, split0, ready, tokens=S, width=None):
            norms[name] = dict(n=len(norms), bank=4 + len(norms) % 2, src=src, dst=dst, gain=gain_name, chunks=chunks, split0=split0,
                               ready=ready, tokens=tokens, width=width or chunks * P, done=h_ready,
                               sq0=sum(x["chunks"] for x in norms.values()))

        add_norm("mix", h, (xn_hi, xn_lo), "g_mix", KC, SPLIT["norm_mix"], lambda c: (h_ready, c + 1))
        add_norm("ffn", h, (xn_hi, xn_lo), "g_ffn", KC, SPLIT["norm_ffn"],
                 lambda c: (signals["dve"].sem, freed(jobs["w_o"], c % 4, c // 4)))
        add_norm("mem", memT, (mem_hi, mem_lo), "norm_mem", KC, SPLIT["norm_mem"], lambda c: (memT_ready, c // 2 + 1),
                 tokens=NMEM)
        add_norm("final", h, (h, None), "g_final", KC, None, None)
        add_norm("mix_2", h, (xn_hi, xn_lo), "norm_mix", KC, SPLIT["norm_mix_2"], None)
        add_norm("cq", cq, (cq_hi, cq_lo), "q_a", 3, SPLIT["cq"],
                 lambda c: (signals["act"].sem, freed(jobs["lat_a"], c, 0)))
        add_norm("ckv", ckv, (ckv_hi, ckv_lo), "kv_a", 2, SPLIT["ckv"],
                 lambda c: (signals["act"].sem, freed(jobs["lat_b"], 0, 0)))

        def add_parts(name, parts, width, tokens, ready):
            add_norm(name, None, None, None, len(parts), None, ready, tokens, width)
            norms[name].update(parts=parts, done=part_ready)

        for n in range(H2):
            k_ = mem_k[:, n, :]
            add_parts(f"mem_k{n}", [(k_, k_, gain("mem_k"), k_)], P, NMEM,
                      lambda c: (signals["act"].sem, freed(jobs["mem_k"], 3, 0)))
        for n in range(H2):
            q_ = mq[:, n, :]
            add_parts(f"mem_q{n}", [(q_, q_, gain("mem_q"), q_)], P, S,
                      lambda c: (signals["act"].sem, freed(jobs["mq"], 3, 0)))
        for n in range(H2):
            r_ = slice(ROPE * (n % 2), ROPE * (n % 2) + ROPE)
            q_, qr_, k_, kr_ = qn[:, n, :], qr[r_, n // 2, :], kn[:, n, :], krh[r_, n // 2, :]
            add_parts(f"q{n}", [(q_, q_, gain("mla_q"), q_), (qr_, qr_, gain("mla_q", 1)[r_, :], qr_)], QKH, S,
                      lambda c: (signals["act"].sem, freed(jobs["uq_rope"], 1, 0)))
            add_parts(f"k{n}", [(k_, k_, gain("mla_k"), k_), (kr[0:ROPE, :], krb[r_, :], None, kr_)], QKH, S,
                      lambda c: (signals["act"].sem, freed(jobs["ukv_k"], 3, 0)))
        add_norm("ffn_2", h, (xn_hi, xn_lo), "norm_ffn", KC, SPLIT["norm_ffn_2"],
                 lambda c: (signals["dve"].sem, freed(jobs["w_out"], c % 4, c // 4)))

        def parts_of(m):
            N = m["tokens"]
            if "parts" in m:
                return m["parts"]
            return [(m["src"][:, c, 0:N], m["src"][:, c, 0:N], gain(m["gain"], c), m["dst"][0][:, c, 0:N])
                    for c in range(m["chunks"])]

        def act_norm(act, name):
            m = norms[name]
            N = m["tokens"]
            for c, (src, *_) in enumerate(parts_of(m)):
                if m["ready"](c) is not None:
                    act.wait_ge(*m["ready"](c))
                k = m["sq0"] + c
                if k >= 2:
                    act.wait_ge(sq_used, k - 1)
                rows = src.shape[0]
                act.activation(sq[k % 2][0:rows, 0:N], src, ACT.Square).then_inc(sq_ready, 1)
            act.wait_ge(sq_used, m["sq0"] + m["chunks"])
            bank = ps[m["bank"]][:, 0:N]
            act.activation(bank, bank, ACT.Sqrt, scale=1.0 / m["width"], bias=const("eps")).then_inc(root_ready, 1)
            if m["split0"] is not None:
                for c in range(m["chunks"]):
                    act_hi(act, m["split0"] + c, m["dst"][0][:, c, :], slot=(m["split0"] + c) % 2)

        def pe_sum(pe, name, c):
            m = norms[name]
            N = m["tokens"]
            if c == 0 and m["n"] >= 2:
                pe.wait_ge(rstd_ready, m["n"] - 1)
            k = m["sq0"] + c
            rows = parts_of(m)[c][0].shape[0]
            pe.wait_ge(sq_ready, k + 1)
            pe.matmul(ps[m["bank"]][:, 0:N], ones[0:rows, :], sq[k % 2][0:rows, 0:N], start=c == 0,
                      stop=c == m["chunks"] - 1).then_inc(sq_used, 1)

        def pe_norm(pe, name, first=0):
            for c in range(first, norms[name]["chunks"]):
                pe_sum(pe, name, c)

        def pe_job_with_sums(pe, name, norm):
            def after(i, panel, tile):
                c = 4 * i + tile - 2
                if panel == jobs[name].panels - 1 and tile >= 2:
                    pe_sum(pe, norm, c)
                elif panel == 0 and i and tile < 2:
                    pe_sum(pe, norm, c)
            pe_job(pe, name, after)
            pe_norm(pe, norm, KC - 2)

        SQ_FINAL = norms["final"]["sq0"]

        def pe_sums(pe, c, start=False, stop=False):
            for x in range(2):
                pe.wait_ge(sq_ready, SQ_FINAL + 2 * c + x + 1)
                pe.matmul(ps[norms["final" if x == 0 else "mix_2"]["bank"]][:, :], ones[:, :], sq[x][:, :],
                          start=start, stop=stop).then_inc(sq_used, 1)

        def act_norms(act):
            job = jobs["down"]

            def squares(i):
                for t in range(2):
                    c = 2 * i + t
                    act.wait_ge(signals["dve"].sem, freed(job, t, i))
                    for x in range(2):
                        act.wait_ge(sq_used, SQ_FINAL + 2 * c + x - 1)
                        g = GAIN_ROWS["g_final"]
                        act.activation(sq[x][:, :], h[:, c, :], ACT.Square,
                                       scale=gains[:, bass.ds(g + c, 1)] if x else 1.0).then_inc(sq_ready, 1)
            over_blocks(act, job, squares)
            act.wait_ge(sq_used, SQ_FINAL + 16)
            b1 = ps[norms["final"]["bank"]]
            act.activation(b1[:, :], b1[:, :], ACT.Sqrt, scale=1.0 / D, bias=const("eps")).then_inc(root_ready, 1)
            act.wait_ge(between_ready, 1)
            act.activation(sq[0][:, :], sq[0][:, :], ACT.Sqrt, scale=1.0 / D, bias=const("eps")).then_inc(root_ready, 1)
            for c in range(KC):
                act_hi(act, SPLIT["norm_mix_2"] + c, xn_hi[:, c, :], slot=(SPLIT["norm_mix_2"] + c) % 2)
                if c == 1:
                    act_take(act, "mem_k", [mem_k[:, t, :] for t in range(H2)])
                    act_take(act, "mem_v", [mem_v[:, t, :] for t in range(2)])

        def dve_norms(dve):
            n1, n2 = norms["final"]["n"], norms["mix_2"]["n"]
            r1, r2 = rstd[n1 % 2], rstd[n2 % 2]
            dve.wait_ge(root_ready, n1 + 1)
            dve.wait_ge(*norm_done(norms["mem"]))
            dve.reciprocal(r1[:], ps[norms["final"]["bank"]][:, :]).then_inc(rstd_ready, 1)
            dve.wait_ge(rstd_ready, n1 + 1)
            dve_step(dve, dve.tensor_tensor(sq[0][:], r1[:], r1[:], ALU.mult))
            dve.tensor_tensor(sq[0][:], sq[0][:], ps[norms["mix_2"]["bank"]][:, :], ALU.mult).then_inc(between_ready, 1)
            s0 = SPLIT["norm_mix_2"]

            def scale(c):
                dve.scalar_tensor_tensor(h[:, c, :], h[:, c, :], gain("g_final", c), r1[:], ALU.mult,
                                         ALU.mult).then_inc(h_ready, 1)
            scale(0)
            scale(1)
            dve.wait_ge(root_ready, n2 + 1)
            dve.reciprocal(r2[:], sq[0][:]).then_inc(rstd_ready, 1)
            dve.wait_ge(rstd_ready, n2 + 1)

            def value(c):
                val_free(dve, s0 + c)
                dve.wait_ge(h_ready, KC + c + 1)
                dve.scalar_tensor_tensor(val[(s0 + c) % 2][:, :], h[:, c, :], gain("norm_mix", c), r2[:],
                                         ALU.mult, ALU.mult).then_inc(val_ready, 1)
            for c in range(KC):
                value(c)
                if c + 2 < KC:
                    scale(c + 2)
                if c == 1:
                    dve.wait_ge(gemm_done, tile_done(jobs["mem_v"], 1, 0))
                if c:
                    dve_lo(dve, s0 + c - 1, xn_lo[:, c - 1, :], xn_hi[:, c - 1, :], slot=(s0 + c - 1) % 2)
            dve_lo(dve, s0 + c, xn_lo[:, c, :], xn_hi[:, c, :], slot=(s0 + c) % 2)

        def dve_step(dve, ins):
            ins.then_inc(step.sem, 1)
            dve.wait_ge(step.sem, step.reserve(1) + 1)

        def norm_done(m):
            if m["split0"] is not None:
                return lo_ready, m["split0"] + m["chunks"]
            if "parts" in m:
                return part_ready, sum(len(x["parts"]) for x in norms.values() if "parts" in x and x["n"] <= m["n"])
            return h_ready, 2 * KC

        def dve_norm(dve, name):
            m = norms[name]
            N = m["tokens"]
            r = rstd[m["n"] % 2]
            dve.wait_ge(root_ready, m["n"] + 1)
            if m["n"] >= 2:
                dve.wait_ge(*norm_done([x for x in norms.values() if x["n"] == m["n"] - 2][0]))
            dve.reciprocal(r[:, 0:N], ps[m["bank"]][:, 0:N]).then_inc(rstd_ready, 1)
            dve.wait_ge(rstd_ready, m["n"] + 1)
            s0 = m["split0"]
            if s0 is None:
                done = m["done"]
                for _, src, g, dst in parts_of(m):
                    a = dst.start_partition()
                    rr = r[a:a + dst.shape[0], 0:N]
                    if g is None:
                        ins = dve.tensor_tensor(dst, src, rr, ALU.mult)
                    else:
                        ins = dve.scalar_tensor_tensor(dst, src, g, rr, ALU.mult, ALU.mult)
                    ins.then_inc(done, 1)
                return
            for c in range(m["chunks"]):
                val_free(dve, s0 + c)
                dve.scalar_tensor_tensor(val[(s0 + c) % 2][:, 0:N], m["src"][:, c, 0:N], gain(m["gain"], c),
                                         r[:, 0:N], ALU.mult, ALU.mult).then_inc(val_ready, 1)
                if c:
                    dve_lo(dve, s0 + c - 1, m["dst"][1][:, c - 1, :], m["dst"][0][:, c - 1, :], slot=(s0 + c - 1) % 2)
            c = m["chunks"] - 1
            dve_lo(dve, s0 + c, m["dst"][1][:, c, :], m["dst"][0][:, c, :], slot=(s0 + c) % 2)

        PACK = [[(3, 0)], [(2, 0), (0, 384)], [(1, 0)]]
        POFF = {3: 0, 2: 512, 0: 896, 1: 1024}
        UNITS = 2 * NH
        SCALE = HD ** -0.5

        def unit_parts(c):
            return 64 * (c // 2), c % 2

        def qk_bank(pe, a, it, c, b):
            r, win = unit_parts(c)
            un = 4 * it + c
            rows = slice(r, r + 64)
            kt = kT[:, 2 * win + a, :]
            if b == 0 and not win:
                pe.wait_ge(q_staged, 2 * it + c // 2 + 1)
            n = 3 * un + b
            bank = ps[(3 * c + b) % 3]
            if not isinstance(n, int) or n >= 3:
                pe.wait_ge(scores_taken, n - 2)
            for i, off in PACK[b]:
                w = P * (i + 1)
                mm = pe.matmul(bank[:, off:off + w], q_s[rows, P * i:P * i + P], kt[rows, 0:w],
                               start=True, stop=True)
            if b == 2 and not win:
                g = 2 * a + c // 2
                for i in range(TT):
                    mm = pe.matmul(bank[:, 256 + NCMP * i:256 + NCMP * (i + 1)], q_s[rows, P * i:P * i + P],
                                   k_cmp[rows, NCMP * g:NCMP * (g + 1)], start=True, stop=True)
            mm.then_inc(scores_done, 1)

        TURN = []
        for c in range(4):
            for b in range(3 if c % 2 else 4):
                TURN.append((c, b, "act" if b in (0, 3) else "dve"))
        TACT = sum(e == "act" for *_, e in TURN)
        TDVE = len(TURN) - TACT

        def turn_index(c, b):
            return [x[:2] for x in TURN].index((c, b))

        def pT_taken(it, k):
            if k < 0:
                k, it = k + len(TURN), it - 1
            e = TURN[k][2]
            n = sum(x[2] == e for x in TURN[:k]) + 1
            return (pT_act, TACT * it + n) if e == "act" else (pT_dve, TDVE * it + n)

        def prob_item(c, i):
            return prob[c][:, POFF[i]:POFF[i] + P * (i + 1)]

        def prob_cmp(c, i):
            return prob[c][:, 1280 + NCMP * i:1280 + NCMP * (i + 1)]

        def turn(pe, it, c, b):
            k = turn_index(c, b)
            if not (isinstance(it, int) and it == 0 and k < 2):
                sg, n = pT_taken(it, k - 2)
                pe.wait_ge(sg, n)
            bank = ps[4 + k % 2]
            if b == 3:
                for i in range(TT):
                    mm = pe.transpose(bank[0:NCMP, P * i:P * i + P], prob_cmp(c, i), ident)
            else:
                for i, off in PACK[b]:
                    for kt in range(i + 1):
                        mm = pe.transpose(bank[:, off + P * kt:off + P * kt + P],
                                          prob_item(c, i)[:, P * kt:P * kt + P], ident)
            mm.then_inc(pT_done, 1)

        def o_slot(c, i, cmp=False):
            bank = ps[6 + c % 2]
            at_ = i if (c % 2 or cmp) else 4 + i
            return bank[:, HD * at_:HD * at_ + HD]

        def pv(pe, a, it, c, b):
            sg, n = pT_taken(it, turn_index(c, b))
            pe.wait_ge(sg, n)
            g = 2 * a + c // 2
            src = pT[c % 2][b]
            if b == 3:
                for i in range(TT):
                    mm = pe.matmul(o_slot(c, i, True), src[0:NCMP, P * i:P * i + P], v_cmp[0:NCMP, g, :],
                                   start=True, stop=True)
                return mm
            col = 256 * (c % 2) + HD * g
            for i, off in PACK[b]:
                for kt in range(i + 1):
                    mm = pe.matmul(o_slot(c, i), src[:, off + P * kt:off + P * kt + P], v_rows[:, kt, col:col + HD],
                                   start=kt == 0, stop=kt == i)
            return mm

        def pe_slot(pe, products, scores):
            if products:
                a, it, c = products
                un = 4 * it + c
                pe.wait_ge(exp_done, un + 1)
                turn(pe, it, c, 0)
            if scores:
                qk_bank(pe, *scores, 0)
            if products:
                turn(pe, it, c, 1)
                if not isinstance(un, int) or un >= 2:
                    pe.wait_ge(o_taken, un - 1)
                pv(pe, a, it, c, 0)
                turn(pe, it, c, 2)
            if scores:
                qk_bank(pe, *scores, 1)
            if products:
                pv(pe, a, it, c, 1)
                if c % 2 == 0:
                    turn(pe, it, c, 3)
            if scores:
                qk_bank(pe, *scores, 2)
            if products:
                mm = pv(pe, a, it, c, 2)
                if c % 2 == 0:
                    mm = pv(pe, a, it, c, 3)
                mm.then_inc(pv_done, 1)

        def pe_pair(pe, it):
            pe.wait_ge(o_part, 4 * it + 4)
            if not isinstance(it, int) or it > 0:
                pe.wait_ge(val_ready, SPLIT["o"] + it)
            for i in range(TT):
                mm = pe.transpose(ps[3][:, P * i:P * i + P], o_pair[:, i, :, :].rearrange("p a d -> p (a d)"), ident)
            mm.then_inc(pair_done, 1)

        def pairs(eng, body):
            for a in range(2):
                body(a, 4 * a)
                with eng.Fori(4 * a + 1, 4 * a + 4) as it:
                    body(a, it)

        def pe_attention(pe):
            pe.wait_ge(cmp_ready, 2)
            pe.wait_ge(signals["act"].sem, freed(jobs["cmp_v"], 1, 0))

            def body(a, it):
                before = not (isinstance(it, int) and it == 0)
                prev = 0 if isinstance(it, int) and it == 4 else a
                pe_slot(pe, (prev, it - 1, 2) if before else None, (a, it, 0))
                pe_slot(pe, (prev, it - 1, 3) if before else None, (a, it, 1))
                pe_slot(pe, (a, it, 0), (a, it, 2))
                if before:
                    pe_pair(pe, it - 1)
                pe_slot(pe, (a, it, 1), (a, it, 3))
            pairs(pe, body)
            pe_slot(pe, (1, 7, 2), None)
            pe_slot(pe, (1, 7, 3), None)
            pe_pair(pe, 7)

        def take_pT(eng, it, c, b):
            un = 4 * it + c
            k = turn_index(c, b)
            if b in (0, 1) and (not isinstance(un, int) or un >= 2):
                eng.wait_ge(pv_done, un - 1)
            eng.wait_ge(pT_done, len(TURN) * it + k + 1)
            rows = NCMP if b == 3 else P
            w = 256 if b == 2 else 512
            dst, src = pT[c % 2][b][0:rows, 0:w], ps[4 + k % 2][0:rows, 0:w]
            if TURN[k][2] == "act":
                eng.activation(dst, src, ACT.Copy).then_inc(pT_act, 1)
            else:
                eng.tensor_copy(dst, src).then_inc(pT_dve, 1)

        def mstat(kind, c):
            return stat[:, kind, c, :]

        def act_exps(act, it, c):
            un = 4 * it + c
            act.wait_ge(negm_ready, un + 1)
            for i in range(TT):
                if c % 2 == 0:
                    act.activation(prob_cmp(c, i), prob_cmp(c, i), ACT.Exp, bias=mstat(1, c)[:, i:i + 1],
                                   scale=SCALE, accum_out=mstat(2, c)[:, i:i + 1])
            for i in (3, 2, 0, 1):
                n = i + 4 * (1 - c % 2)
                ins = act.activation(prob_item(c, i), prob_item(c, i), ACT.Exp, bias=mstat(1, c)[:, n:n + 1],
                                     scale=SCALE, accum_out=mstat(2, c)[:, n:n + 1])
            ins.then_inc(exp_done, 1)

        def act_pair(act, it):
            act.wait_ge(pair_done, it + 1)
            act.activation(oT[:, it, :], ps[3][:, :], ACT.Copy).then_inc(val_ready, 1)

        def act_slot(act, products, probs, pair=None):
            if products:
                take_pT(act, *products, 0)
            if pair is not None:
                act_pair(act, pair)
            if probs:
                act_exps(act, *probs)
            if products and products[1] % 2 == 0:
                take_pT(act, *products, 3)

        def act_attention(act):
            def body(a, it):
                before = not (isinstance(it, int) and it == 0)
                act_slot(act, (it - 1, 2) if before else None, (it - 1, 3) if before else None)
                act_slot(act, (it - 1, 3) if before else None, (it, 0))
                act_slot(act, (it, 0), (it, 1))
                act_slot(act, (it, 1), (it, 2), pair=it - 1 if before else None)
            pairs(act, body)
            act_slot(act, (7, 2), (7, 3))
            act_slot(act, (7, 3), None)
            act_pair(act, 7)

        def dve_max(dve, it, c, b):
            un = 4 * it + c
            items = 4 if c % 2 else 8
            if b == 0 and (not isinstance(un, int) or un >= 4):
                dve.wait_ge(pv_done, un - 3)
            dve.wait_ge(scores_done, 3 * un + b + 1)
            if not isinstance(un, int):
                dve.sem_inc(dve_waited, 1)
            bank = ps[(3 * c + b) % 3]
            todo = [(bank[:, off:off + P * (i + 1)], prob_item(c, i), mask_of(P * (i + 1)), i + items - 4)
                    for i, off in PACK[b]]
            if b == 2 and items == 8:
                a_, b_ = CONST_COLS["cmp"]
                todo += [(bank[:, 256 + NCMP * i:256 + NCMP * (i + 1)], prob_cmp(c, i),
                          consts[:, a_ + NCMP * i:a_ + NCMP * (i + 1)], i) for i in range(TT)]
            for src, dst, mask, n in todo:
                ins = dve.tensor_tensor_reduce(out=dst, in0=src, in1=mask, scale=1.0, scalar=NEG,
                                               op0=ALU.add, op1=ALU.max, accum_out=mstat(0, c)[:, n:n + 1])
            ins.then_inc(scores_taken, 1)
            if b == 2:
                dve.wait_ge(scores_taken, 3 * un + 3)
                dve.tensor_scalar(mstat(1, c)[:, 0:items], mstat(0, c)[:, 0:items], FLOOR, -SCALE,
                                  ALU.max, ALU.mult).then_inc(negm_ready, 1)

        STEPS = 3
        att_step0 = []

        def dve_weigh(dve, a, it, c):
            un = 4 * it + c
            items = 4 if c % 2 else 8
            s0 = att_step0[0] + STEPS * un
            l, w = mstat(2, c)[:, 0:items], mstat(3, c)[:, 0:items]
            dve.wait_ge(exp_done, un + 1)
            dve.tensor_scalar(w, l, 1e-30, None, ALU.max).then_inc(step.sem, 1)
            dve.wait_ge(step.sem, s0 + 1)
            dve.reciprocal(l, w).then_inc(step.sem, 1)
            dve.wait_ge(step.sem, s0 + 2)
            head = it + 4 * a + 4 * (c // 2)
            g = gates[:, :, :].rearrange("p (b h) i -> p h b i", b=3)[:, head, (2 if c % 2 else 0):(3 if c % 2 else 2), :]
            dve.tensor_tensor(w.rearrange("p (b i) -> p b i", i=TT), l.rearrange("p (b i) -> p b i", i=TT), g,
                              ALU.mult).then_inc(step.sem, 1)

        def dve_combine(dve, it, c):
            un = 4 * it + c
            items = 4 if c % 2 else 8
            dve.wait_ge(step.sem, att_step0[0] + STEPS * un + 3)
            dve.wait_ge(pv_done, un + 1)
            w = mstat(3, c)[:, 0:items].unsqueeze(2).to_broadcast([P, items, HD])
            dve.tensor_tensor(o_w[:, 0:items, :], ps[6 + c % 2][:, 0:HD * items].rearrange("p (n d) -> p n d", d=HD),
                              w, ALU.mult).then_inc(o_taken, 1)
            dve.wait_ge(o_taken, un + 1)
            dst = o_pair[:, :, c // 2, :]
            if c == 0 and not (isinstance(it, int) and it == 0):
                dve.wait_ge(pair_done, it)
            if c % 2:
                dve.wait_ge(o_part, un)
                dve.tensor_tensor(dst, dst, o_w[:, 0:4, :], ALU.add).then_inc(o_part, 1)
            else:
                dve.tensor_tensor(dst, o_w[:, 0:4, :], o_w[:, 4:8, :], ALU.add).then_inc(o_part, 1)

        def dve_attention(dve):
            att_step0.append(step.reserve(STEPS * UNITS))

            def slot(products, scores, combined):
                if scores:
                    dve_max(dve, *scores, 0)
                if products:
                    a, it, c = products
                    take_pT(dve, it, c, 1)
                    take_pT(dve, it, c, 2)
                if combined:
                    dve_combine(dve, *combined)
                if scores:
                    dve_max(dve, *scores, 1)
                    dve_max(dve, *scores, 2)
                if products:
                    dve_weigh(dve, *products)

            def body(a, it):
                before = not (isinstance(it, int) and it == 0)
                prev = 0 if isinstance(it, int) and it == 4 else a
                slot((prev, it - 1, 2) if before else None, (it, 0), (it - 1, 1) if before else None)
                slot((prev, it - 1, 3) if before else None, (it, 1), (it - 1, 2) if before else None)
                slot((a, it, 0), (it, 2), (it - 1, 3) if before else None)
                slot((a, it, 1), (it, 3), (it, 0))
            pairs(dve, body)
            slot((1, 7, 2), None, (7, 1))
            slot((1, 7, 3), None, (7, 2))
            dve_combine(dve, 7, 3)

        def pool_stage_q(pool):
            def body(a, it):
                for half in range(2):
                    rows = slice(64 * half, 64 * half + 64)
                    if isinstance(it, int) and it == 0:
                        pool.wait_ge(signals["act"].sem, freed(jobs["q"], 3, 1))
                        pool.wait_ge(blk_lo_ready, 2)
                        pool.wait_ge(w_lo_done, jobs["attn_out"].panel0)
                        if half:
                            pool.wait_ge(q_staged, half)
                    else:
                        pool.wait_ge(scores_done, 12 * it - 6 * (1 - half))
                        pool.wait_ge(q_staged, 2 * it + half)
                        if not isinstance(it, int):
                            pool.sem_inc(pool_waited, 1)
                    pool.tensor_copy(q_s[rows, :], q[rows, it, :]).then_inc(q_staged, 1)
            pairs(pool, body)

        def halves(t, n):
            m = 1 << n
            v = t[:, :, :].rearrange("p h s -> p (h s)").rearrange("p (b a m) -> p b a m", a=2, m=m)
            return v[:, :, 0, :], v[:, :, 1, :]

        def level_mask(n):
            a, _ = CONST_COLS["level"]
            return consts[:, a + P * n:a + P * n + P].unsqueeze(1).to_broadcast([P, TT, P])

        def act_level(act, n):
            act.wait_ge(level_moved, n + 1)
            if n:
                act.wait_ge(level_done, 4 * (n + 1))
            if n == LEVELS:
                act.activation(qt[:], pre[:], ACT.Exp)
                act.activation(decay, pre[:].rearrange("p h (c t) -> p h c t", t=P)[:, :, :, P - 1], ACT.Exp)
                act.activation(kt_[:], suf[:], ACT.Exp).then_inc(level_exp, 1)
                return
            if n:
                act.activation(halves(kt_, n)[0], halves(suf, n)[0], ACT.Exp)
            act.activation(halves(qt, n)[1], halves(pre, n)[1], ACT.Exp).then_inc(level_exp, 1)

        def dve_level_mul(dve, n):
            dve.wait_ge(level_exp, n + 1)
            if n == LEVELS:
                dve.tensor_tensor(kt_[:], kt_[:], hk[:], ALU.mult)
                dve.tensor_tensor(qt[:], qt[:], hq[:], ALU.mult).then_inc(level_mul, 1)
                return
            k1, q2 = halves(kt_, n)[0], halves(qt, n)[1]
            if n:
                dve.tensor_tensor(k1, k1, halves(hk, n)[0], ALU.mult)
            else:
                dve.tensor_copy(k1, halves(hk, n)[0])
            dve.tensor_tensor(q2, q2, halves(hq, n)[1], ALU.mult).then_inc(level_mul, 1)
            m = 1 << n
            (p1, p2), (s1, _) = halves(pre, n), halves(suf, n)
            B = p1.shape[1]
            dve_step(dve, dve.tensor_tensor(s1, s1, p2[:, :, m - 1:m].to_broadcast([P, B, m]), ALU.add))
            dve.tensor_tensor(p2, p2, p1[:, :, m - 1:m].to_broadcast([P, B, m]), ALU.add).then_inc(level_moved, 1)

        def pe_level(pe, n):
            if n >= 0:
                pe.wait_ge(level_mul, n + 1)
            k, q_ = (hk, hq) if n < 0 else (kt_, qt)
            for j in range(H2):
                at_ = 4 * (n + 1) + j
                if at_ >= 4:
                    pe.wait_ge(level_kept, at_ - 3)
                for c in range(TT):
                    cs = slice(P * c, P * c + P)
                    mm = pe.matmul(ps[4 + j][:, cs], k[:, j, cs], q_[:, j, cs], start=True, stop=True)
                mm.then_inc(level_done, 1)

        def dve_level_keep(dve, n):
            for j in range(H2):
                at_ = 4 * (n + 1) + j
                dve.wait_ge(level_done, at_ + 1)
                src = ps[4 + j][:, :].rearrange("p (c t) -> p c t", t=P)
                dst = aT[:, j, :].rearrange("p (c t) -> p c t", t=P)
                if n < 0:
                    ins = dve.tensor_tensor(dst, src, level_mask(0), ALU.mult)
                else:
                    dve.wait_ge(level_kept, at_ - 3)
                    ins = dve.copy_predicated(dst, level_mask(n + 1).bitcast(I32), src)
                ins.then_inc(level_kept, 1)

        def dve_recurrence_inputs(dve):
            l0, l1 = (gains[:, GAIN_ROWS["lb"] + 4 * n:GAIN_ROWS["lb"] + 4 * n + 4] for n in range(2))
            top, e, total, lb, rest = (lbv[:, a:b] for a, b in ((0, 4), (4, 12), (12, 16), (16, 20), (20, 24)))
            dve_step(dve, dve.tensor_tensor(top, l0, l1, ALU.max))
            dve.tensor_tensor(e[:, 0:4], l0, top, ALU.subtract).then_inc(lb_exp, 1)
            dve.tensor_tensor(e[:, 4:8], l1, top, ALU.subtract).then_inc(lb_exp, 1)
            dve.wait_ge(lb_exp, 3)
            dve_step(dve, dve.tensor_tensor(total, e[:, 0:4], e[:, 4:8], ALU.add))
            dve_step(dve, dve.reciprocal(rest, total))
            dve_step(dve, dve.tensor_tensor(lb, rest, e[:, 0:4], ALU.mult))
            dve_step(dve, dve.tensor_scalar(rest, lb, -1.0, 1.0, ALU.mult, ALU.add))
            for t in range(H2):
                dve.wait_ge(signals["act"].sem, freed(jobs["f"], t, 0))
                dve.tensor_scalar(hk[:, t, :], hk[:, t, :], rest[:, t:t + 1], lb[:, t:t + 1],
                                  ALU.mult, ALU.add).then_inc(f_ready, 1)
            dve_step(dve, dve.memset(suf[:], 0.0))
            dve.wait_ge(decay_logs, 1)
            dve.tensor_scalar(pre[:], pre[:], 0.0, None, ALU.min).then_inc(level_moved, 1)
            dve.tensor_scalar(hk[:], hk[:], -1.0, 1.0, ALU.mult, ALU.add).then_inc(hk_ready, 1)
            dve.wait_ge(signals["act"].sem, freed(jobs["hq"], 3, 0))
            dve.tensor_scalar(hq[:], hq[:], P ** -0.5, None, ALU.mult).then_inc(hq_ready, 1)
            dve.wait_ge(hk_ready, 1)
            dve.wait_ge(hq_ready, 1)

        def pe_chunks(pe):
            pe.wait_ge(level_mul, LEVELS + 1)
            pe.wait_ge(rstd_ready, norms["mem_q3"]["n"] + 1)
            pe.wait_ge(level_kept, 4 * (LEVELS + 1))
            for c in range(3):
                for j in range(H2):
                    mm = pe.transpose(ps[4 + c][:, P * j:P * j + P], kt_[:, j, P * c:P * c + P], ident)
                mm.then_inc(k_turned, 1)
            pe.wait_ge(signals["act"].sem, freed(jobs["i"], 3, 0))
            for c in range(TT):
                heads = [slice(P * j, P * j + P) for j in range(H2)]
                if c < 3:
                    pe.wait_ge(k_rows_ready, 3)
                    if c == 2:
                        pe.wait_ge(state_ready, 1)
                    for j in range(H2):
                        mm = pe.matmul(ps[4 + c % 2][:, heads[j]], k_rows[:, c, heads[j]], hv[:, c, heads[j]],
                                       start=True, stop=True)
                    mm.then_inc(chunk_done, 1)
                if c:
                    pe.wait_ge(state_ready, c)
                if c >= 2:
                    pe.wait_ge(chunk_out, c - 1)
                for j in range(H2):
                    cs = slice(P * c, P * c + P)
                    o = ps[6 + c % 2][:, heads[j]]
                    mm = pe.matmul(o, aT[:, j, cs], hv[:, c, heads[j]], start=True, stop=c == 0)
                    if c:
                        mm = pe.matmul(o, qt[:, j, cs], state[:, j, :], start=False, stop=True)
                mm.then_inc(chunk_done, 1)

        def act_chunks(act):
            act.wait_ge(gemm_done, tile_done(jobs["g"], 3, 0))
            for c in range(3):
                act.wait_ge(k_turned, c + 1)
                act.activation(k_rows[:, c, :], ps[4 + c][:, :], ACT.Copy).then_inc(k_rows_ready, 1)
            for c in range(TT):
                act.wait_ge(chunk_done, min(2 * c + 2, 7))
                act.activation(o_rows[:, c, :], ps[6 + c % 2][:, :], ACT.Copy).then_inc(chunk_out, 1)

        def dve_chunks(dve):
            dve.wait_ge(gemm_done, tile_done(jobs["g"], 3, 0))
            for c in range(3):
                new = ps[4 + c % 2]
                dve.wait_ge(chunk_done, 2 * c + 1 if c == 0 else 2 * c + 2)
                if c == 0:
                    dve.tensor_copy(state[:].rearrange("p h e -> p (h e)"), new[:, :]).then_inc(state_ready, 1)
                    continue
                dve.wait_ge(state_ready, c)
                for j in range(H2):
                    ins = dve.scalar_tensor_tensor(state[:, j, :], state[:, j, :], decay[:, j, c:c + 1],
                                                   new[:, P * j:P * j + P], ALU.mult, ALU.add)
                ins.then_inc(state_ready, 1)

        FIN = [dict(y=o_rows, parts=16, width=P, gain="hg_out", out=(hgm_hi, hgm_lo), split=SPLIT["hgm"]),
               dict(y=y_mla, parts=4, width=W2, gain="mla_out", out=(mlam_hi, mlam_lo), split=SPLIT["mlam"]),
               dict(y=y_mem, parts=4, width=W2, gain="mem_out", out=(memm_hi, memm_lo), split=SPLIT["memm"])]

        def act_rows(act, n):
            f = FIN[n]
            act.wait_ge(*f["ready"])
            if n:
                act.wait_ge(rows_ready, 4 * n)
            for k in range(f["parts"]):
                src = f["y"][:, k // 4, P * (k % 4):P * (k % 4) + P] if n == 0 else f["y"][:, k, :]
                dst = squares[0][:, k // 4, P * (k % 4):P * (k % 4) + P] if n == 0 else squares[1][:, k, :]
                ins = act.activation(dst, src, ACT.Square, accum_out=ssq[:, k:k + 1])
            ins.then_inc(rows_sq, 1)
            act.wait_ge(rows_sq, n + 1)
            act.activation(rroot[:, 0:f["parts"]], ssq[:, 0:f["parts"]], ACT.Sqrt, scale=1.0 / f["width"],
                           bias=const("eps")).then_inc(rows_root, 1)

        def dve_rows(dve, n):
            f = FIN[n]
            dve.wait_ge(rows_root, n + 1)
            dve_step(dve, dve.reciprocal(rinv[:, 0:f["parts"]], rroot[:, 0:f["parts"]]))
            for i in range(TT):
                y = f["y"][:, i, :]
                if n == 0:
                    v_ = y.rearrange("p (h e) -> p h e", e=P)
                    ins = dve.tensor_tensor(v_, v_, rinv[:, 4 * i:4 * i + 4].unsqueeze(2).to_broadcast([P, H2, P]), ALU.mult)
                else:
                    ins = dve.tensor_scalar(y, y, rinv[:, i:i + 1], None, ALU.mult)
                ins.then_inc(rows_ready, 1)

        def pe_rows(pe, n):
            f = FIN[n]
            pe.wait_ge(rows_ready, 4 * n + 4)
            for j in range(4):
                if j or n:
                    pe.wait_ge(val_ready, f["split"] + j)
                else:
                    pe.wait_ge(signals["act"].sem, freed(jobs["ukv_v"], 3, 0))
                for i in range(TT):
                    mm = pe.transpose(ps[3][:, P * i:P * i + P], f["y"][:, i, P * j:P * j + P], ident)
                mm.then_inc(rows_turned, 1)

        def dve_rows_out(dve, n):
            f = FIN[n]
            for j in range(4):
                k = f["split"] + j
                dve.wait_ge(rows_turned, 4 * n + j + 1)
                val_free(dve, k)
                if n == 0:
                    ins = dve.scalar_tensor_tensor(val[k % 2][:, :], ps[3][:, :], gain(f["gain"], j), sg[:, j, :],
                                                   ALU.mult, ALU.mult)
                else:
                    ins = dve.tensor_scalar(val[k % 2][:, :], ps[3][:, :], gain(f["gain"], j), None, ALU.mult)
                ins.then_inc(val_ready, 1)
                dve_lo(dve, k, f["out"][1][:, j, :], f["out"][0][:, j, :], slot=k % 2)

        def act_rows_out(act, n):
            f = FIN[n]
            for j in range(4):
                k = f["split"] + j
                act_hi(act, k, f["out"][0][:, j, :], slot=k % 2)

        MAGIC = 1.5 * 2.0 ** 23
        TURN1, TURN2, TURN3 = 6.28125, 0.0019354820251464844, -1.7484556025237907e-07

        def dve_angles(dve):
            dve.wait_ge(pos_loaded, 16)
            dve_step(dve, dve.tensor_copy(rb[:], pos_i[:]))
            dve_step(dve, dve.tensor_scalar(rb[:], rb[:], const("freq"), None, ALU.mult))
            for dst, shift, quarter in ((sin, 0.0, 0.0), (cos, 0.25, float(np.pi / 2))):
                dve_step(dve, dve.tensor_scalar(ra[:], rb[:], float(1 / (2 * np.pi)), shift, ALU.mult, ALU.add))
                dve_step(dve, dve.tensor_scalar(ra[:], ra[:], MAGIC, None, ALU.add))
                dve_step(dve, dve.tensor_scalar(ra[:], ra[:], MAGIC, None, ALU.subtract))
                dve_step(dve, dve.scalar_tensor_tensor(dst[:], ra[:], -TURN1, rb[:], ALU.mult, ALU.add))
                dve_step(dve, dve.scalar_tensor_tensor(dst[:], ra[:], -TURN2, dst[:], ALU.mult, ALU.add))
                dve_step(dve, dve.scalar_tensor_tensor(dst[:], ra[:], -TURN3, dst[:], ALU.mult, ALU.add))
                dve_step(dve, dve.tensor_scalar(dst[:], dst[:], quarter, 3.1415925, ALU.add, ALU.min))
                dve.tensor_scalar(dst[:], dst[:], -3.1415925, None, ALU.max).then_inc(angle_ready, 1)

        def act_angles(act):
            for n, dst in enumerate((sin, cos)):
                act.wait_ge(angle_ready, n + 1)
                act.activation(dst[:], dst[:], ACT.Sin).then_inc(angle_sin, 1)

        ROT = [krb[:, :], qr[:, 0, :], qr[:, 1, :]]

        def pe_rope(pe, n):
            if n == 0:
                pe.wait_ge(rope_ready, 1)
            else:
                pe.wait_ge(part_ready, part_done(f"q{2 * n - 1}"))
                pe.wait_ge(rope_ready, n + 1)
            pe.matmul(ps[6][:, :], const("rot"), ROT[n], start=True, stop=True).then_inc(rot_done, 1)

        def dve_rope(dve, n):
            x = ROT[n]
            if n == 0:
                dve.wait_ge(angle_sin, 2)
                dve.tensor_scalar(krb[:], kr[:], gain("mla_k", 1), None, ALU.mult).then_inc(rope_ready, 1)
            dve.wait_ge(rot_done, n + 1)
            dve_step(dve, dve.tensor_tensor(ra[:], x, cos[:], ALU.mult))
            dve_step(dve, dve.tensor_tensor(rb[:], ps[6][:, :], sin[:], ALU.mult))
            dve.tensor_tensor(x, ra[:], rb[:], ALU.add).then_inc(rope_ready, 1)
            if n == 0:
                dve.wait_ge(rope_ready, 2)

        def part_done(name):
            return norm_done(norms[name])[1]

        CAUSAL_PACK = [[(3, 0, 512)], [(2, 0, 384), (0, 384, 128)], [(1, 0, 256)]]
        MEM_PACK = [[(3, 0, 256), (2, 256, 256)], [(1, 0, 256), (0, 256, 256)]]
        units2 = []
        n_score = n_turn = 0
        for n in range(2 * H2):
            mla, j = n < H2, n % H2
            pack = CAUSAL_PACK if mla else MEM_PACK
            units2.append(dict(n=n, mla=mla, head=j, pack=pack, score0=n_score, turn0=n_turn,
                               off=POFF if mla else {i: 256 * i for i in range(4)},
                               scale=(QKH if mla else P) ** -0.5))
            n_score += len(pack)
            n_turn += len(pack)

        def taken_of(k):
            return (pT2_act if k % 2 == 0 else pT2_dve), k // 2 + 1

        def pe_qk2(pe, w):
            j = w["head"]
            if w["n"] == 0:
                pe.wait_ge(rope_ready, 4)
                pe.wait_ge(part_ready, part_done("k3"))
                pe.wait_ge(signals["act"].sem, freed(jobs["ukv_v"], 3, 0))
            for b, items in enumerate(w["pack"]):
                k = w["score0"] + b
                if k >= 3:
                    pe.wait_ge(taken2, k - 2)
                for i, off, width in items:
                    o = ps[k % 3][:, off:off + width]
                    ts = slice(P * i, P * i + P)
                    if w["mla"]:
                        r = slice(ROPE * (j % 2), ROPE * (j % 2) + ROPE)
                        pe.matmul(o, qn[:, j, ts], kn[:, j, 0:width], start=True, stop=False)
                        mm = pe.matmul(o, qr[r, j // 2, ts], krh[r, j // 2, 0:width], start=False, stop=True)
                    else:
                        mm = pe.matmul(o, mq[:, j, ts], mem_k[:, j, 0:width], start=True, stop=True)
                mm.then_inc(scores2, 1)

        def item2(w, i, width):
            return prob2[w["n"] % 3][:, w["off"][i]:w["off"][i] + width]

        def dve_max2(dve, w):
            n = w["n"]
            if n >= 3:
                dve.wait_ge(pv2, n - 2)
            for b, items in enumerate(w["pack"]):
                k = w["score0"] + b
                dve.wait_ge(scores2, k + 1)
                for i, off, width in items:
                    a_, _ = CONST_COLS["causal"]
                    mask = mask_of(width) if w["mla"] else consts[:, a_:a_ + width]
                    ins = dve.tensor_tensor_reduce(out=item2(w, i, width), in0=ps[k % 3][:, off:off + width], in1=mask,
                                                   scale=1.0, scalar=NEG, op0=ALU.add, op1=ALU.max,
                                                   accum_out=mstat(0, n % 4)[:, i:i + 1])
                ins.then_inc(taken2, 1)
            dve.wait_ge(taken2, w["score0"] + len(w["pack"]))
            dve.tensor_scalar(mstat(1, n % 4)[:, 0:TT], mstat(0, n % 4)[:, 0:TT], FLOOR, -w["scale"],
                              ALU.max, ALU.mult).then_inc(negm2, 1)

        def act_exps2(act, w):
            n = w["n"]
            act.wait_ge(negm2, n + 1)
            for items in w["pack"]:
                for i, _, width in items:
                    x = item2(w, i, width)
                    ins = act.activation(x, x, ACT.Exp, bias=mstat(1, n % 4)[:, i:i + 1], scale=w["scale"],
                                         accum_out=mstat(2, n % 4)[:, i:i + 1])
            ins.then_inc(exp2, 1)

        def pe_tpv2(pe, w):
            n, j = w["n"], w["head"]
            pe.wait_ge(exp2, n + 1)
            rows = v2 if w["mla"] else mem_v

            def turn2(b):
                k = w["turn0"] + b
                if k >= 2:
                    pe.wait_ge(*taken_of(k - 2))
                for i, off, width in w["pack"][b]:
                    for kt in range(width // P):
                        mm = pe.transpose(ps[4 + k % 2][:, off + P * kt:off + P * kt + P],
                                          item2(w, i, width)[:, P * kt:P * kt + P], ident)
                mm.then_inc(turned2, 1)

            def product2(b):
                pe.wait_ge(*taken_of(w["turn0"] + b))
                for i, off, width in w["pack"][b]:
                    for kt in range(width // P):
                        mm = pe.matmul(ps[6 + n % 2][:, P * i:P * i + P],
                                       pT2[n % 2][b][:, off + P * kt:off + P * kt + P],
                                       rows[:, kt, P * j:P * j + P], start=kt == 0, stop=kt == width // P - 1)
                return mm

            turn2(0)
            if n >= 2:
                pe.wait_ge(y_ready, n - 1)
            for b in range(1, len(w["pack"])):
                turn2(b)
                product2(b - 1)
            product2(len(w["pack"]) - 1).then_inc(pv2, 1)

        def take2(eng, which, w):
            n = w["n"]
            if n >= 2:
                eng.wait_ge(pv2, n - 1)
            elif n == 0:
                eng.wait_ge(rows_turned, 4)
            for b in range(len(w["pack"])):
                k = w["turn0"] + b
                if k % 2 != (which == "dve"):
                    continue
                eng.wait_ge(turned2, k + 1)
                width = 256 if w["mla"] and b == 2 else 512
                dst, src = pT2[n % 2][b][:, 0:width], ps[4 + k % 2][:, 0:width]
                if which == "act":
                    eng.activation(dst, src, ACT.Copy).then_inc(pT2_act, 1)
                else:
                    eng.tensor_copy(dst, src).then_inc(pT2_dve, 1)

        def dve_combine2(dve, w):
            n, j = w["n"], w["head"]
            dve.wait_ge(exp2, n + 1)
            r = mstat(3, n % 4)[:, 0:TT]
            dve_step(dve, dve.reciprocal(r, mstat(2, n % 4)[:, 0:TT]))
            dve.wait_ge(pv2, n + 1)
            y = y_mla if w["mla"] else y_mem
            dve.tensor_tensor(y[:, :, P * j:P * j + P], ps[6 + n % 2][:, :].rearrange("p (i e) -> p i e", e=P),
                              r.unsqueeze(2).to_broadcast([P, TT, P]), ALU.mult).then_inc(y_ready, 1)

        def pe_attention2(pe):
            for w in units2:
                pe_qk2(pe, w)
                if w["n"] >= 2:
                    pe_tpv2(pe, units2[w["n"] - 2])
                if w["n"] == 6:
                    pe_rows(pe, 1)
            pe_tpv2(pe, units2[6])
            pe_tpv2(pe, units2[7])
            pe_rows(pe, 2)

        def act_attention2(act):
            for w in units2:
                if w["n"] >= 2:
                    take2(act, "act", units2[w["n"] - 2])
                act_exps2(act, w)
                if w["n"] == 5:
                    act_rows(act, 1)
                if w["n"] == 6:
                    act_rows_out(act, 1)
            take2(act, "act", units2[6])
            take2(act, "act", units2[7])
            act_rows(act, 2)
            act_rows_out(act, 2)

        def dve_attention2(dve):
            for w in units2:
                dve_max2(dve, w)
                if w["n"] >= 2:
                    take2(dve, "dve", units2[w["n"] - 2])
                    dve_combine2(dve, units2[w["n"] - 2])
                if w["n"] == 5:
                    dve_rows(dve, 1)
                if w["n"] == 6:
                    dve_rows_out(dve, 1)
            for w in units2[6:]:
                take2(dve, "dve", w)
                dve_combine2(dve, w)
            dve_rows(dve, 2)
            dve_rows_out(dve, 2)

        FIN[0]["ready"] = (chunk_out, 4)
        FIN[1]["ready"] = (y_ready, H2)
        FIN[2]["ready"] = (y_ready, 2 * H2)

        def act_hi_from(act, n, dst, src):
            act.activation(dst, src, ACT.Copy).then_inc(hi_ready, 1)

        def act_mlp(act, name, norm):
            act_norm(act, norm)
            job = jobs[name]

            def silus(i):
                for t in range(2):
                    n = job.split0 + 2 * i + t
                    act.wait_ge(val_ready, n - 1)
                    act.wait_ge(gemm_done, tile_done(job, t, i))
                    act.activation(silu[:, t, :], ps[t][:, :], ACT.Silu).then_inc(signals["act"].sem, 1)
                for t in range(2):
                    n = job.split0 + 2 * i + t
                    act_hi(act, n, hid_hi[:, 2 * i + t, :], slot=(job.split0 + t) % 2)
            over_blocks(act, job, silus)

        def i_is(i, n):
            return isinstance(i, int) and i == n

        def dve_mlp(dve, name, down, norm, first_block=None):
            dve_norm(dve, norm)
            job = jobs[name]

            def products(i):
                for t in range(2):
                    dve.wait_ge(signals["act"].sem, freed(job, t, i))
                    dve.wait_ge(gemm_done, tile_done(job, t + 2, i))
                    val_free(dve, job.split0 + 2 * i + t)
                    dve.tensor_tensor(val[(job.split0 + t) % 2][:, :], ps[t + 2][:, :], silu[:, t, :],
                                      ALU.mult).then_inc(val_ready, 1)
                for t in range(2):
                    n = job.split0 + 2 * i + t
                    dve_lo(dve, n, hid_lo[:, 2 * i + t, :], hid_hi[:, 2 * i + t, :], slot=(job.split0 + t) % 2)
            over_blocks(dve, job, products)
            job = jobs[down]

            def adds(i):
                for t in range(2):
                    dve.wait_ge(gemm_done, tile_done(job, t, i))
                    dve.tensor_tensor(h[:, 2 * i + t, :], ps[t][:, :], h[:, 2 * i + t, :],
                                      ALU.add).then_inc(signals["dve"].sem, 1)
                    if i_is(i, 0) and t == 0 and first_block:
                        first_block()
            over_blocks(dve, job, adds)

        def act_take(act, name, dsts, func=ACT.Copy):
            job = jobs[name]
            for t, dst in enumerate(dsts):
                act.wait_ge(gemm_done, tile_done(job, t, 0))
                act.activation(dst, ps[job.banks[t]][:, 0:dst.shape[-1]], func).then_inc(signals["act"].sem, 1)

        OUT = out[0].rearrange("(t p) d -> p t d", p=P)

        def out_bank(t, half):
            return (2 * t + half + 2) % 8

        block = ctx.enter_context(nc.Block())
        SET1 = ["conv_in", "gate_attn", "conv_out", "gate_conv", "q", "kv_cmp", "k", "v", "gates", "cmp_k", "cmp_v"]

        @block.sync
        def _(sp):
            for job in order:
                sp_job(sp, job.name)
            for t in range(TT):
                sp.wait_ge(out_act, t + 1)
                sp.wait_ge(out_dve, t + 1)
                sp.dma_start(OUT[:, t, :], out_rows[:, t, :]).then_inc(out_sent, 16)
            sp.wait_ge(out_sent, 16 * TT)

        @block.gpsimd
        def _(pool):
            for name in SET1:
                pool_job(pool, name)
            pool_stage_q(pool)
            pool.wait_ge(q_staged, 2 * 8)
            for job in order[len(SET1):]:
                pool_job(pool, job.name)

        @block.scalar
        def _(act):
            act.dma_start(x_rows[:], A["x"][0].rearrange("(t p) d -> p t d", p=P)).then_inc(x_loaded, 16)
            act.dma_start(consts[:], A["consts"]).then_inc(consts_loaded, 16)
            for name, key in (("g_mix", "g_mix"), ("g_ffn", "g_ffn"), ("g_final", "g_final")):
                r = GAIN_ROWS[name]
                src = A[key] if key == "g_final" else A[key][0]
                act.dma_start(gain_rows[r:r + 8, :], src.rearrange("(c p) -> c p", p=P)).then_inc(gains_loaded, 16)
            n_rows = 3
            for name, key in (("norm_mix", "norm_mix_2"), ("norm_mem", "norm_mem_2"), ("q_a", "q_a_norm_2"),
                              ("kv_a", "kv_a_norm_2"), ("hg_out", "hg_out_norm_2"), ("mem_q", "mem_q_norm_2"),
                              ("mem_k", "mem_k_norm_2"), ("mla_out", "mla_out_norm_2"),
                              ("mem_out", "mem_out_norm_2"), ("norm_ffn", "norm_ffn_2")):
                r = GAIN_ROWS[name]
                src = A[key][0].rearrange("(c p) -> c p", p=P)
                act.dma_start(gain_rows[r:r + src.shape[0], :], src).then_inc(gains_loaded, 16)
                n_rows += 1
            for name, key in (("mla_q", "mla_q_norm_2"), ("mla_k", "mla_k_norm_2")):
                r = GAIN_ROWS[name]
                src = A[key]
                act.dma_start(gain_rows[r:r + 1, :], src[:, 0:NOPE]).then_inc(gains_loaded, 16)
                for half in range(2):
                    act.dma_start(gain_rows[r + 1:r + 2, ROPE * half:ROPE * half + ROPE],
                                  src[:, NOPE:QKH]).then_inc(gains_loaded, 16)
                n_rows += 3
            r = GAIN_ROWS["conv_w"]
            act.dma_start(gain_rows[r:r + 12, :], A["conv_w"][0].rearrange("k (c p) -> (k c) p", p=P)).then_inc(gains_loaded, 16)
            r = GAIN_ROWS["lb"]
            act.dma_start(gain_rows[r:r + 8, :], A["hg_lb_logits_2"].rearrange("k (c p) -> (k c) p", p=P)).then_inc(gains_loaded, 16)
            for name, key in (("pos_k", "cmp_pos_k"), ("pos_v", "cmp_pos_v")):
                r = GAIN_ROWS[name]
                act.dma_start(gain_rows[r:r + NPAIR, :], A[key][0].rearrange("(j e) d -> j (e d)", e=2)).then_inc(gains_loaded, 16)
            n_rows += 4
            assert n_rows == 23
            for half in range(2):
                act.dma_start(w2k[:, :, HD * half:HD * half + HD],
                              A["cmp_w2_k"][0].rearrange("(t p) d -> p t d", p=P)).then_inc(w2_loaded, 16)
            act.dma_start(w2v[:], A["cmp_w2_v"][0].rearrange("(t p) d -> p t d", p=P)).then_inc(w2_loaded, 16)

            act.wait_ge(consts_loaded, 16)
            act_norm(act, "mix")

            job = jobs["conv_in"]
            def copies(i):
                for t in range(4):
                    act.wait_ge(gemm_done, tile_done(job, t, i))
                    act.activation(bch[:, 4 * i + t, :], ps[t][:, :], ACT.Copy).then_inc(signals["act"].sem, 1)
            over_blocks(act, job, copies)

            job = jobs["gate_attn"]
            for i in range(2):
                for t in range(4):
                    act.wait_ge(gemm_done, tile_done(job, t, i))
                    act.activation(g_attn[:, 4 * i + t, :], ps[t][:, :], ACT.Sigmoid).then_inc(signals["act"].sem, 1)
                if i == 0:
                    for c in range(4):
                        n = SPLIT["conv"] + c
                        act_hi(act, n, cv_hi[:, c, :], slot=n % 2)

            job = jobs["gate_conv"]
            for i in range(2):
                for t in range(4):
                    n = 4 * i + t
                    if n >= 2:
                        act.wait_ge(mixc_ready, n - 1)
                    act.wait_ge(gemm_done, tile_done(job, t, i))
                    act.activation(sig[:, n % 2, :], ps[t][:, :], ACT.Sigmoid).then_inc(signals["act"].sem, 1)

            job = jobs["q"]
            for i in range(2):
                for t in range(4):
                    act.wait_ge(gemm_done, tile_done(job, t, i))
                    act.activation(q[:, 4 * i + t, :], ps[t][:, :], ACT.Copy).then_inc(signals["act"].sem, 1)
            job = jobs["k"]
            for t in range(4):
                act.wait_ge(gemm_done, tile_done(job, t, 0))
                act.activation(kT[:, t, :], ps[t][:, :], ACT.Copy).then_inc(signals["act"].sem, 1)
            act.wait_ge(signals["dve"].sem, freed(jobs["kv_cmp"], 1, 0))
            act.activation(blk_hi[0][:], blk[0][:].rearrange("p j h n -> p j (h n)"), ACT.Copy).then_inc(blk_hi_ready, 1)
            job = jobs["v"]
            for t in range(4):
                act.wait_ge(gemm_done, tile_done(job, t, 0))
                act.activation(v_rows[:, t, :], ps[t][:, :], ACT.Copy).then_inc(signals["act"].sem, 1)
            job = jobs["gates"]
            for t in range(4):
                act.wait_ge(gemm_done, tile_done(job, t, 0))
                act.activation(gates[:, :, t], ps[t][:, 0:3 * NH], ACT.Sigmoid).then_inc(signals["act"].sem, 1)
            act.activation(blk_hi[1][:], blk[1][:].rearrange("p j h n -> p j (h n)"), ACT.Copy).then_inc(blk_hi_ready, 1)
            for n, name in enumerate(("cmp_k", "cmp_v")):
                job = jobs[name]
                for t in range(2):
                    act.wait_ge(gemm_done, tile_done(job, t, 0))
                    act.activation(hid_cmp[n][:, t, :], ps[job.banks[t]][:, 0:NKV * NCMP],
                                   ACT.Gelu_apprx_tanh).then_inc(signals["act"].sem, 1)

            act_attention(act)
            for c in range(KC):
                n = SPLIT["o"] + c
                if c == 0:
                    act.wait_ge(val_ready, SPLIT["o"] + 8)
                act_hi_from(act, n, o_hi[:, c, :], oT[:, c, :])
            for c in range(KC):
                n = jobs["attn_out"].split0 + c
                act_hi(act, n, mix_hi[:, c, :], slot=n % 2)
            act_mlp(act, "up", "ffn")

            act.wait_ge(gemm_done, tile_done(jobs["up"], 3, 10))
            act.dma_start(mem_rows[:], A["mem_2"][0].rearrange("(t p) d -> p t d", p=P)).then_inc(mem_loaded, 16)
            act_norm(act, "mem")
            act_norms(act)
            act.wait_ge(lb_exp, 2)
            act.activation(lbv[:, 4:12], lbv[:, 4:12], ACT.Exp).then_inc(lb_exp, 1)
            act_take(act, "f", [hk[:, t, :] for t in range(H2)], ACT.Sigmoid)
            act.wait_ge(f_ready, H2)
            act.activation(pre[:], hk[:], ACT.Ln).then_inc(decay_logs, 1)
            act_take(act, "hq", [hq[:, t, :] for t in range(H2)], ACT.Silu)
            act_level(act, 0)
            act_take(act, "lat_a", [cq[:, 0, :], cq[:, 1, :], cq[:, 2, :], ckv[:, 0, :]])
            act_level(act, 1)
            act_level(act, 2)
            act_take(act, "lat_b", [ckv[:, 1, :], kr[:, :]])
            act_level(act, 3)
            act_level(act, 4)
            act_take(act, "mq", [mq[:, t, :] for t in range(H2)])
            act_level(act, 5)
            act_level(act, 6)
            act_level(act, LEVELS)
            act_norm(act, "cq")
            act_norm(act, "ckv")
            act.wait_ge(lo_ready, SPLIT["ckv"] + 2)
            act.dma_start(pos_i[:], A["positions_2"][0:1, :].to_broadcast([P, S])).then_inc(pos_loaded, 16)
            act_take(act, "i", [hv[:, t, :] for t in range(TT)])
            for n in range(H2):
                act_norm(act, f"mem_k{n}")
            for n in range(H2):
                act_norm(act, f"mem_q{n}")
            act_take(act, "g", [sg[:, t, :] for t in range(H2)], ACT.Silu)
            act_chunks(act)
            act_take(act, "uq_nope", [qn[:, t, :] for t in range(H2)])
            act_take(act, "uq_rope", [qr[:, t, :] for t in range(2)])
            act_take(act, "ukv_k", [kn[:, t, :] for t in range(H2)])
            act_take(act, "ukv_v", [v2[:, t, :] for t in range(TT)])
            act_angles(act)
            act_rows(act, 0)
            act_rows_out(act, 0)
            for n in range(H2):
                act_norm(act, f"q{n}")
                act_norm(act, f"k{n}")
            act_attention2(act)
            act_mlp(act, "up_2", "ffn_2")
            for t in range(TT):
                act.wait_ge(out_turned, 2 * t + 1)
                act.activation(out_rows[:, t, 0:S], ps[out_bank(t, 0)][:, :], ACT.Copy).then_inc(out_act, 1)

        @block.vector
        def _(dve):
            for c in range(KC):
                dve.wait_ge(xT_done, c + 1)
                dve.tensor_copy(h[:, c, :], ps[c % 4][:, :]).then_inc(h_ready, 1)
            dve.wait_ge(gainsT_done, 1)
            dve.tensor_copy(gains[:, 0:NGAIN], ps[5][:, 0:NGAIN]).then_inc(gains_ready, 1)
            dve.memset(u[:, :, 0:2], 0.0).then_inc(step.sem, 1)
            step.reserve(1)
            dve.wait_ge(gains_ready, 1)
            dve_norm(dve, "mix")

            job = jobs["conv_in"]
            for t in range(4):
                dve.wait_ge(signals["act"].sem, freed(job, t, 2))
                dve_step(dve, dve.tensor_tensor(u[:, t, 2:S + 2], bch[:, 4 + t, :], bch[:, 8 + t, :], ALU.mult))
            for t in range(4):
                n = SPLIT["conv"] + t
                val_free(dve, n)
                z = val[n % 2][:, :]
                dve_step(dve, dve.tensor_scalar(z, u[:, t, 0:S], gain("conv_w", t), None, ALU.mult))
                for k in (1, 2):
                    dve_step(dve, dve.scalar_tensor_tensor(z, u[:, t, k:k + S], gain("conv_w", 4 * k + t), z,
                                                           ALU.mult, ALU.add))
                dve.tensor_tensor(z, z, bch[:, t, :], ALU.mult).then_inc(val_ready, 1)
                if t:
                    dve_lo(dve, n - 1, cv_lo[:, t - 1, :], cv_hi[:, t - 1, :], slot=(n - 1) % 2)
            dve_lo(dve, n, cv_lo[:, 3, :], cv_hi[:, 3, :], slot=n % 2)

            job = jobs["conv_out"]
            for i in range(2):
                for t in range(4):
                    dve.wait_ge(gemm_done, tile_done(job, t, i))
                    dve.tensor_copy(mixc[:, 4 * i + t, :], ps[t][:, :]).then_inc(signals["dve"].sem, 1)
            job = jobs["gate_conv"]
            for i in range(2):
                for t in range(4):
                    n = 4 * i + t
                    dve.wait_ge(signals["act"].sem, freed(job, t, i))
                    dve.tensor_tensor(mixc[:, n, :], mixc[:, n, :], sig[:, n % 2, :], ALU.mult).then_inc(mixc_ready, 1)

            job = jobs["kv_cmp"]
            dve.wait_ge(mixc_ready, 8)
            for t in range(4):
                dve.wait_ge(gemm_done, tile_done(job, t, 0))
                kv = t // 2
                pos = GAIN_ROWS["pos_v" if kv else "pos_k"]
                for half in range(2):
                    head = 2 * (t % 2) + half
                    rows = ps[t][64 * half:64 * half + 64, :].rearrange("p (n l) -> p l n", l=CMP_STRIDE)
                    for e in range(2):
                        for jj in range(2):
                            src = rows[:, e:CMP_STRIDE:2, jj:jj + NCMP]
                            dst = blk[kv][64 * e:64 * e + 64, 8 * jj:8 * jj + 8, head, :]
                            add = gains[64 * e:64 * e + 64, pos + 8 * jj:pos + 8 * jj + 8]
                            ins = dve.tensor_tensor(dst, src, add.unsqueeze(2).to_broadcast([64, 8, NCMP]), ALU.add)
                ins.then_inc(signals["dve"].sem, 1)
            for kv in range(2):
                dve.wait_ge(blk_hi_ready, kv + 1)
                dve.tensor_tensor(blk_lo[kv][:], blk[kv][:].rearrange("p j h n -> p j (h n)"),
                                  blk_hi[kv][:].bitcast(F32), ALU.subtract).then_inc(blk_lo_ready, 1)
            dve.wait_ge(cmp_done, 1)
            dve.tensor_copy(k_cmp[:, :], ps[4][:, 0:NKV * NCMP]).then_inc(cmp_ready, 1)
            dve.wait_ge(cmp_done, 2)
            dve.tensor_copy(v_cmp[0:NCMP, :, :],
                            ps[5][0:NCMP, 0:NKV * HD].rearrange("p (g d) -> p g d", d=HD)).then_inc(cmp_ready, 1)

            dve_attention(dve)
            for c in range(KC):
                n = SPLIT["o"] + c
                dve.wait_ge(hi_ready, n + 1)
                dve.tensor_tensor(o_lo[:, c, :], oT[:, c, :], o_hi[:, c, :].bitcast(F32), ALU.subtract).then_inc(lo_ready, 1)
            job = jobs["attn_out"]
            for i in range(2):
                for t in range(4):
                    c = 4 * i + t
                    n = job.split0 + c
                    dve.wait_ge(gemm_done, tile_done(job, t, i))
                    dve.tensor_tensor(mixp[:, :], ps[t][:, :], g_attn[:, c, :], ALU.mult).then_inc(signals["dve"].sem, 1)
                    dve.wait_ge(signals["dve"].sem, freed(job, t, i))
                    val_free(dve, n)
                    dve.tensor_tensor(val[n % 2][:, :], mixp[:, :], mixc[:, c, :], ALU.add).then_inc(val_ready, 1)
                    dve_lo(dve, n, mix_lo[:, c, :], mix_hi[:, c, :], slot=n % 2)
            job = jobs["w_o"]
            for i in range(2):
                for t in range(4):
                    c = 4 * i + t
                    dve.wait_ge(gemm_done, tile_done(job, t, i))
                    dve.tensor_tensor(h[:, c, :], ps[t][:, :], h[:, c, :], ALU.add).then_inc(signals["dve"].sem, 1)
            def memory():
                for n in range(KC // 2):
                    dve.wait_ge(memT_done, n + 1)
                    dve.tensor_copy(memT[:, 2 * n:2 * n + 2, :].rearrange("p c t -> p (c t)"),
                                    ps[4 + n][:, :]).then_inc(memT_ready, 1)
                dve_norm(dve, "mem")
            dve_mlp(dve, "up", "down", "ffn", memory)

            dve_norms(dve)
            dve.memset(qt[:], 0.0)
            dve.memset(kt_[:], 0.0)
            dve_recurrence_inputs(dve)
            dve_level_mul(dve, 0)
            dve_level_keep(dve, -1)
            for n in range(1, LEVELS):
                dve_level_mul(dve, n)
                dve_level_keep(dve, n - 1)
            dve_level_keep(dve, LEVELS - 1)
            dve_level_mul(dve, LEVELS)
            dve_norm(dve, "cq")
            dve_norm(dve, "ckv")
            for n in range(H2):
                dve_norm(dve, f"mem_k{n}")
            for n in range(H2):
                dve_norm(dve, f"mem_q{n}")
            dve_chunks(dve)
            dve_angles(dve)
            dve_rows(dve, 0)
            dve_rows_out(dve, 0)
            dve_rope(dve, 0)
            for n in range(H2):
                dve_norm(dve, f"q{n}")
                dve_norm(dve, f"k{n}")
                if n % 2:
                    dve_rope(dve, n // 2 + 1)
            dve_attention2(dve)
            job = jobs["w_out"]
            for i in range(2):
                for t in range(4):
                    dve.wait_ge(gemm_done, tile_done(job, t, i))
                    dve.tensor_tensor(h[:, 4 * i + t, :], ps[t][:, :], h[:, 4 * i + t, :],
                                      ALU.add).then_inc(signals["dve"].sem, 1)
            dve_mlp(dve, "up_2", "down_2", "ffn_2")
            for t in range(TT):
                dve.wait_ge(out_turned, 2 * t + 2)
                dve.tensor_copy(out_rows[:, t, S:D], ps[out_bank(t, 1)][:, :]).then_inc(out_dve, 1)

        @block.tensor
        def _(pe):
            pe.wait_ge(x_loaded, 16)
            pe.wait_ge(consts_loaded, 16)
            for c in range(KC):
                if c >= 4:
                    pe.wait_ge(h_ready, c - 3)
                for t in range(TT):
                    mm = pe.transpose(ps[c % 4][:, P * t:P * t + P], x_rows[:, t, P * c:P * c + P], ident)
                mm.then_inc(xT_done, 1)
            pe.wait_ge(gains_loaded, 16 * 23)
            pe.transpose(ps[5][:, 0:NGAIN], gain_rows[0:NGAIN, :], ident[0:NGAIN, 0:NGAIN]).then_inc(gainsT_done, 1)
            pe_norm(pe, "mix")
            pe.wait_ge(h_ready, 8)
            for name in SET1:
                pe_job(pe, name)
            pe.wait_ge(w2_loaded, 48)
            pe.wait_ge(rstd_ready, 1)
            pe.wait_ge(gains_ready, 1)
            pe.wait_ge(signals["act"].sem, freed(jobs["cmp_k"], 1, 0))
            for t in range(2):
                mm = pe.matmul(ps[4][:, 0:NKV * NCMP], w2k[:, t, :], hid_cmp[0][:, t, :], start=t == 0, stop=t == 1)
            mm.then_inc(cmp_done, 1)
            pe.wait_ge(signals["act"].sem, freed(jobs["cmp_v"], 1, 0))
            for g in range(NKV):
                for t in range(2):
                    mm = pe.matmul(ps[5][0:NCMP, HD * g:HD * g + HD], hid_cmp[1][:, t, NCMP * g:NCMP * (g + 1)],
                                   w2v[:, t, :], start=t == 0, stop=t == 1)
            mm.then_inc(cmp_done, 1)
            pe_attention(pe)
            pe.wait_ge(val_ready, SPLIT["o"] + 8)
            pe_job(pe, "attn_out")
            pe_job_with_sums(pe, "w_o", "ffn")
            pe_job(pe, "up")

            def with_down(i, panel, tile):
                first = i_is(i, 0)
                if first and panel == 1:
                    pe.wait_ge(mem_loaded, 16)
                    pe.wait_ge(rstd_ready, norms["ffn"]["n"] + 1)
                    for n in range(KC // 2):
                        for c in range(2):
                            for t in range(2):
                                mm = pe.transpose(ps[4 + n][:, NMEM * c + P * t:NMEM * c + P * t + P],
                                                  mem_rows[:, t, P * (2 * n + c):P * (2 * n + c) + P], ident)
                        mm.then_inc(memT_done, 1)
                if first and panel == 2:
                    pe.wait_ge(memT_ready, KC // 2)
                    pe_norm(pe, "mem")
                if first and panel == 3:
                    pe.wait_ge(rstd_ready, norms["mem"]["n"] + 1)
                    pe_sums(pe, 0, start=True)
                if not first and panel == 1:
                    pe_sums(pe, 2 * i - 1)
                if not first and panel == 3:
                    pe_sums(pe, 2 * i)
            pe_job(pe, "down", with_down)
            pe_sums(pe, KC - 1, stop=True)
            pe_job(pe, "mem_k")
            pe_job(pe, "mem_v")
            pe_job(pe, "f")
            pe_job(pe, "hq")
            pe.wait_ge(rstd_ready, norms["mix_2"]["n"] + 1)

            def levels(*ns):
                last = {}

                def after(i, panel, tile):
                    last[panel] = last.get(panel, 0) + 1
                    if last[panel] == per_panel[0]:
                        ns[panel]() if callable(ns[panel]) else pe_level(pe, ns[panel])
                return after

            def diagonal():
                pe.wait_ge(hk_ready, 1)
                pe.wait_ge(hq_ready, 1)
                pe_level(pe, -1)

            for name, ns in (("lat_a", (diagonal, 0)), ("lat_b", (1, 2)), ("mq", (3, 4))):
                per_panel = [jobs[name].tiles]
                pe_job(pe, name, levels(*ns))
            pe_level(pe, 5)
            pe_level(pe, 6)
            pe.wait_ge(level_kept, H2 * (LEVELS + 1))
            pe_norm(pe, "cq")
            pe_norm(pe, "ckv")
            pe_job(pe, "i")
            for n in range(H2):
                pe_norm(pe, f"mem_k{n}")
            for n in range(H2):
                pe_norm(pe, f"mem_q{n}")
            pe_job(pe, "g")
            pe_chunks(pe)
            for name in ("uq_nope", "uq_rope", "ukv_k", "ukv_v"):
                pe_job(pe, name)
            pe_rows(pe, 0)
            pe_rope(pe, 0)
            for n in range(H2):
                pe_norm(pe, f"q{n}")
                pe_norm(pe, f"k{n}")
                if n % 2:
                    pe_rope(pe, n // 2 + 1)
            pe_attention2(pe)
            pe_job_with_sums(pe, "w_out", "ffn_2")
            pe_job(pe, "up_2")
            pe_job(pe, "down_2")
            pe.wait_ge(signals["dve"].sem, freed(jobs["down_2"], 1, 3))
            for t in range(TT):
                for half in range(2):
                    for c in range(4):
                        mm = pe.transpose(ps[out_bank(t, half)][:, P * c:P * c + P],
                                          h[:, 4 * half + c, P * t:P * t + P], ident)
                    mm.then_inc(out_turned, 1)


_INS = ("x w_in conv_w w_conv_out cmp_pos_k cmp_w1_k cmp_w2_k cmp_pos_v cmp_w1_v cmp_w2_v w_attn_out w_o "
        "g_mix g_ffn w_gate w_up w_down g_final mem_2 positions_2 norm_mix_2 norm_mem_2 w_in_2 q_a_norm_2 "
        "w_uq_2 kv_a_norm_2 w_ukv_2 mla_q_norm_2 mla_k_norm_2 hg_lb_logits_2 hg_out_norm_2 w_mem_kv_2 "
        "mem_q_norm_2 mem_k_norm_2 mla_out_norm_2 mem_out_norm_2 w_out_2 norm_ffn_2 w_gate_2 w_up_2 "
        "w_down_2").split()


def kernel(**inputs):
    import numpy as _np
    import concourse.bacc as _bacc
    from concourse import mybir as _mybir
    from concourse.bass_utils import run_bass_kernel_spmd as _run

    nc = _bacc.Bacc("TRN2", target_bir_lowering=False, num_devices=1)
    arrays = {name: _np.ascontiguousarray(inputs[name]) for name in _INS}
    arrays["consts"] = shape_constants()
    A = {name: nc.dram_tensor(f"in_{name}", a.shape, _mybir.dt.from_np(a.dtype), kind="ExternalInput").ap()
         for name, a in arrays.items()}
    out = nc.dram_tensor("out_0", (1, S, D), _mybir.dt.float32, kind="ExternalOutput").ap()
    build(nc, A, out)
    r = _run(nc, [{f"in_{name}": a for name, a in arrays.items()}], core_ids=[0])
    return r.results[0]["out_0"]
```

```python
from contextlib import ExitStack

import numpy as np

import concourse.bass as bass
from concourse import mybir

F32 = mybir.dt.float32
F32R = mybir.dt.float32r
I32 = mybir.dt.int32
ALU = mybir.AluOpType
ACT = mybir.ActivationFunctionType
AX = mybir.AxisListType

P = 128
D = 1024
S = 512
TT = S // P
KC = D // P
CONV = 512
CW = 3
NH, NKV, HD = 16, 4, 64
GROUP = NH // NKV
CMP_LEN, CMP_STRIDE, CMP_HID = 32, 16, 256
NCMP = (S - CMP_LEN) // CMP_STRIDE + 1
NPAIR = CMP_LEN // 2
DFF = 2816
FC = DFF // P
EPS = 1e-6
NEG = -1e30
FLOOR = -1e29

NMEM = 256
QLORA, KVLORA, ROPE, NOPE, VH = 384, 256, 64, 128, 128
QKH = NOPE + ROPE
H2 = 4
W2 = 512
MIX2 = 3 * W2
LEVELS = 7

C_B, C_C, C_H, C_Q = 0, CONV, 2 * CONV, 3 * CONV
C_KC = C_Q + NH * HD
C_VC, C_KS, C_VS, C_KW, C_VW = (C_KC + 256 * n for n in range(1, 6))
C_BR = C_VW + 256
C_GC = C_BR + 3 * NH
C_GA = C_GC + D
I_CQ, I_CKV, I_KR = 0, QLORA, QLORA + KVLORA
I_HQ = I_KR + ROPE
I_HF, I_HI, I_HG, I_MQ = (I_HQ + W2 * n for n in range(1, 5))

CONST_COLS = {}
_at = 0
for _name, _n in (("ident", P), ("ones", P), ("rot", P), ("freq", 1), ("eps", 1), ("causal", S),
                  ("cmp", TT * NCMP), ("level", (LEVELS + 1) * P)):
    CONST_COLS[_name] = (_at, _at + _n)
    _at += _n
NCONST = _at

GAIN_ROWS = {}
_at = 0
for _name, _n in (("g_mix", 8), ("g_ffn", 8), ("g_final", 8), ("conv_w", CW * 4), ("pos_k", NPAIR),
                  ("pos_v", NPAIR), ("norm_mix", 8), ("norm_mem", 8), ("q_a", 3), ("kv_a", 2),
                  ("mla_q", 2), ("mla_k", 2), ("lb", 8), ("hg_out", 4), ("mem_q", 1), ("mem_k", 1),
                  ("mla_out", 4), ("mem_out", 4), ("norm_ffn", 8)):
    GAIN_ROWS[_name] = _at
    _at += _n
NGAIN = _at


def shape_constants():
    c = np.zeros((P, NCONST), np.float32)

    def put(name, value):
        a, b = CONST_COLS[name]
        c[:, a:b] = value.reshape(P, b - a)

    i = np.arange(P)
    put("ident", np.eye(P, dtype=np.float32))
    causal = np.zeros((P, S), np.float32)
    causal[:, S - P:] = np.where(i[None, :] > i[:, None], NEG, 0.0)
    put("causal", causal)
    t = np.arange(TT)[None, :, None] * P + i[:, None, None]
    end = np.arange(NCMP)[None, None, :] * CMP_STRIDE + CMP_LEN - 1
    put("cmp", np.where(end <= t, 0.0, NEG).astype(np.float32))
    put("ones", np.ones((P, P), np.float32))
    rot = np.zeros((P, P), np.float32)
    half = ROPE // 2
    for base in (0, ROPE):
        for k in range(half):
            rot[base + half + k, base + k] = -1.0
            rot[base + k, base + half + k] = 1.0
    put("rot", rot)
    freq = np.power(np.float32(10000.0), -np.arange(half, dtype=np.float32) / np.float32(half))
    put("freq", np.tile(freq.astype(np.float32), P // half)[:, None])
    put("eps", np.full((P, 1), EPS, np.float32))
    s, t = i[:, None], i[None, :]
    level = np.zeros((P, LEVELS + 1, P), np.float32)
    level[:, 0] = s == t
    for n in range(LEVELS):
        m = 1 << n
        level[:, n + 1] = (s // (2 * m) == t // (2 * m)) & (s // m % 2 == 0) & (t // m % 2 == 1)
    put("level", level)
    return c


class Signal:

    def __init__(self, sem):
        self.sem, self.n = sem, 0

    def reserve(self, n):
        base = self.n
        self.n += n
        return base


LOADS = {"q": 8, "kv_cmp": 1, "k": 2, "v": 2, "attn_out": 2, "up": 2, "up_2": 2, "lat_b": 3,
         "uq_nope": 4, "uq_rope": 4, "ukv_k": 4, "ukv_v": 4}


class Job:

    def __init__(self, name, blocks, panels, chunks, groups, freed_by, cols, rows=P, natural=False,
                 tokens=S, banks=None):
        self.name, self.blocks, self.panels, self.chunks, self.groups = name, blocks, panels, chunks, groups
        self.freed_by, self.cols, self.rows, self.natural, self.tokens = freed_by, cols, rows, natural, tokens
        self.tiles = len(freed_by)
        self.banks = banks or list(range(self.tiles))
        self.used = chunks * cols
        self.loads = LOADS.get(name, 1)
        self.looped = blocks >= 3 and panels % 2 == 0
        self.last_group = {}
        self.end_of_panel = {}
        for n, (panel, tile, _) in enumerate(groups):
            self.last_group[tile] = n + 1
            self.end_of_panel[panel] = n + 1


def wide(chunks, tiles, panels):
    return [(h, t, [(k, h * chunks + k) for k in range(chunks)]) for h in range(panels) for t in range(tiles)]


def deep(chunks, tiles):
    return [(2 * t + h, t, [(k, h * chunks + k) for k in range(chunks)]) for t in range(tiles) for h in range(2)]


def make_jobs():
    a, v = "act", "dve"
    return [
        Job("conv_in", 3, 2, 4, wide(4, 4, 2), [a] * 4, 512),
        Job("gate_attn", 2, 2, 4, wide(4, 4, 2), [a] * 4, 512),
        Job("conv_out", 2, 1, 4, wide(4, 4, 1), [v] * 4, 512),
        Job("gate_conv", 2, 2, 4, wide(4, 4, 2), [a] * 4, 512),
        Job("q", 2, 2, 4, wide(4, 4, 2), [a] * 4, 512),
        Job("kv_cmp", 1, 2, 4, wide(4, 4, 2), [v] * 4, 512),
        Job("k", 1, 2, 4, wide(4, 4, 2), [v] * 4, 512),
        Job("v", 1, 2, 4, wide(4, 4, 2), [a] * 4, 512, natural=True),
        Job("gates", 1, 1, 8, wide(8, 1, 1), [a], 3 * NH, rows=3 * NH),
        Job("cmp_k", 1, 2, 8, wide(8, 1, 2), [a], CMP_HID, natural=True, rows=NKV * NCMP, banks=[1]),
        Job("cmp_v", 1, 2, 8, wide(8, 1, 2), [a], CMP_HID, natural=True, rows=NKV * NCMP, banks=[2]),
        Job("attn_out", 2, 2, 4, wide(4, 4, 2), [v] * 4, 512),
        Job("w_o", 2, 2, 4, wide(4, 4, 2), [v] * 4, 512),
        Job("up", 11, 2, 4, wide(4, 4, 2), [a, a, "val", "val"], 512),
        Job("down", 4, 4, 11, deep(11, 2), [v] * 2, P),
        Job("mem_k", 1, 2, 4, wide(4, 4, 2), [a] * 4, 512, tokens=NMEM),
        Job("mem_v", 1, 2, 4, wide(4, 2, 2), [a] * 2, 512, natural=True),
        Job("f", 1, 2, 4, wide(4, 4, 2), [a] * 4, 512),
        Job("hq", 1, 2, 4, wide(4, 4, 2), [a] * 4, 512),
        Job("lat_a", 1, 2, 4, wide(4, 4, 2), [a] * 4, 512),
        Job("lat_b", 1, 2, 4, wide(4, 2, 2), [a] * 2, 256),
        Job("mq", 1, 2, 4, wide(4, 4, 2), [a] * 4, 512),
        Job("i", 1, 2, 4, wide(4, 4, 2), [a] * 4, 512, natural=True),
        Job("uq_nope", 1, 1, 3, wide(3, 4, 1), [a] * 4, 512),
        Job("uq_rope", 1, 1, 3, wide(3, 2, 1), [a] * 2, 256),
        Job("ukv_k", 1, 1, 2, wide(2, 4, 1), [a] * 4, 512),
        Job("ukv_v", 1, 1, 2, wide(2, 4, 1), [a] * 4, 512, natural=True),
        Job("g", 1, 2, 4, wide(4, 4, 2), [a] * 4, 512),
        Job("w_out", 2, 3, 4, [(p, t, [(k, 4 * first + k) for k in range(4)])
                               for p, first in enumerate((1, 2, 0)) for t in range(4)], [v] * 4, 512,
            banks=[0, 1, 2, 4]),
        Job("up_2", 11, 2, 4, wide(4, 4, 2), [a, a, "val", "val"], 512),
        Job("down_2", 4, 4, 11, deep(11, 2), [v] * 2, P),
    ]


def plan(jobs, signals, splits, before, split):
    ends, loads, panel, group = [], [0, 0], 0, 0
    tenant = {}
    for job in jobs:
        if job.name in before:
            for name, n in before[job.name]:
                split[name] = signals["val"].reserve(n)
        if job.name in splits:
            job.split0 = signals["val"].reserve(splits[job.name])
        job.panel0, job.group0, job.load0 = panel, group, list(loads)
        job.free0 = {f: job.split0 if f == "val" else signals[f].n for f in set(job.freed_by)}
        job.tenant0 = {b: tenant.get(b) for b in job.banks}
        for f in job.freed_by:
            if f != "val":
                signals[f].reserve(job.blocks)
        for i in range(job.blocks):
            for h in range(job.panels):
                ends.append(group + len(job.groups) * i + job.end_of_panel[h])
                loads[(panel + job.panels * i + h) % 2] += job.loads
        panel += job.blocks * job.panels
        group += job.blocks * len(job.groups)
        for t, b in enumerate(job.banks):
            tenant[b] = (job.freed_by[t], freed(job, t, job.blocks - 1))
    return ends


def freed(job, tile, block):
    f = job.freed_by[tile]
    each = job.freed_by.count(f)
    return job.free0[f] + each * block + job.freed_by[:tile].count(f) + 1


def tile_done(job, tile, block):
    return job.group0 + len(job.groups) * block + job.last_group[tile]


def build(nc, A, out):
    KB = 1024
    BASE = 16 * KB + 128

    def at(name, shape, dt, kb):
        return nc.alloc_sbuf_tensor_at(name, shape, dt, offset=BASE + int(kb * KB))

    raw = [at(f"raw{n}", [P, 2048], F32, 8 * n) for n in range(2)]
    w_hi = [at(f"w_hi{n}", [P, 2048], F32R, 16 + 8 * n) for n in range(2)]
    w_lo = [at(f"w_lo{n}", [P, 2048], F32R, 32 + 8 * n) for n in range(2)]
    consts = at("consts", [P, NCONST], F32, 48)
    gains = at("gains", [P, P], F32, 56.5)
    stat = at("stat", [P, 4, 4, 8], F32, 57)
    h = at("h", [P, KC, S], F32, 58)
    XN, AR, TAIL = 74, 106, 202
    xn_hi = at("xn_hi", [P, KC, S], F32R, XN)
    xn_lo = at("xn_lo", [P, KC, S], F32R, XN + 16)
    val = [at(f"val{n}", [P, S], F32, TAIL + 2 * n) for n in range(2)]
    w2k = at("w2k", [P, 2, P], F32, TAIL + 4)
    w2v = at("w2v", [P, 2, HD], F32, TAIL + 5)

    sq = [at(f"sq{n}", [P, S], F32, AR + 88 + 2 * n) for n in range(2)]
    rstd = [at(f"rstd{n}", [P, S], F32, AR + 92 + 2 * n) for n in range(2)]

    x_rows = at("x_rows", [P, TT, D], F32, AR)
    gain_rows = at("gain_rows", [P, P], F32, AR + 16)
    bch = at("bch", [P, 12, S], F32, AR)
    u = at("u", [P, 4, S + 2], F32, AR + 24)
    cv_hi = at("cv_hi", [P, 4, S], F32R, AR + 72.75)
    cv_lo = at("cv_lo", [P, 4, S], F32R, AR + 80.75)
    g_attn = at("g_attn", [P, KC, S], F32, AR + 40.75)
    mixc = at("mixc", [P, KC, S], F32, AR + 56.75)
    sig = at("sig", [P, 2, S], F32, AR + 88.75)
    q = at("q", [P, KC, S], F32, AR)
    NCMP_EVEN = NCMP + NCMP % 2
    K_AT = [0, NCMP_EVEN + S, 2 * (NCMP_EVEN + S), 2 * (NCMP_EVEN + S) + S]
    K_WIDTH = K_AT[3] + S
    k_pairs = [at("k_first", [P, K_WIDTH], F32R, AR + 32.25), at("k_second", [P, K_WIDTH], F32R, AR + 16)]
    gates = at("gates", [P, 3 * NH, TT], F32, XN + 22.25)
    v_rows = at("v_rows", [P, TT, 2 * NKV * HD], F32, AR + 24.25)
    blk = [at("blk_k", [P, NPAIR, NKV, NCMP], F32, AR + 33), at("blk_v", [P, NPAIR, NKV, NCMP], F32, AR + 88.25)]
    blk_hi = [at("blk_k_hi", [P, NPAIR, NKV * NCMP], F32R, AR + 72.75),
              at("blk_v_hi", [P, NPAIR, NKV * NCMP], F32R, XN)]
    blk_lo = [at("blk_k_lo", [P, NPAIR, NKV * NCMP], F32R, AR + 80.5),
              at("blk_v_lo", [P, NPAIR, NKV * NCMP], F32R, XN + 7.75)]
    PW = 1280 + TT * NCMP
    prob = [at(f"prob{n}", [P, PW], F32, XN + 5.5 * n) for n in range(4)]
    v_cmp = at("v_cmp", [P, NKV, HD], F32, XN + 23)
    hidT_cmp = [at(f"hidT_cmp{n}", [P, CMP_HID], F32, XN + 26 + n) for n in range(2)]
    gatesT = at("gatesT", [P, S], F32, XN + 28)
    hid_cmp = [at(f"hid_cmp{n}", [P, 2, NKV * NCMP], F32, XN + 24 + n) for n in range(2)]
    pT = [[at(f"pT{n}_{b}", [P, S], F32, AR + 72.75 + 8 * n + 2 * b) for b in range(4 - n)] for n in range(2)]
    diag = [at("diag0", [P, 8, P], F32, AR + 86.75), at("diag1", [P, 4, P], F32, AR + 92.75)]
    q_s = at("q_s", [P, S], F32, XN + 28)
    q_hi = [at("q_hi0", [P, S], F32R, AR + 90.75), at("q_hi1", [P, S], F32R, XN + 24)]
    q_lo = [at("q_lo0", [P, S], F32R, XN + 30), at("q_lo1", [P, S], F32R, XN + 26)]
    oT = q
    o_hi = at("o_hi", [P, KC, S], F32R, AR + 16)
    o_lo = at("o_lo", [P, KC, S], F32R, XN)
    mix_hi = at("mix_hi", [P, KC, S], F32R, XN + 16)
    mix_lo = at("mix_lo", [P, KC, S], F32R, AR)
    mixp = at("mixp", [P, S], F32, AR + 88.75)

    hid_hi = at("hid_hi", [P, FC, S], F32R, AR)
    hid_lo = at("hid_lo", [P, FC, S], F32R, AR + 44)
    silu = at("silu", [P, 2, S], F32, AR + 88)

    mem_rows = at("mem_rows", [P, 2, D], F32, XN)
    memT = at("memT", [P, KC, NMEM], F32, XN + 8)
    mem_hi = at("mem_hi", [P, KC, NMEM], F32R, XN + 16)
    mem_lo = at("mem_lo", [P, KC, NMEM], F32R, XN + 24)
    mem_k = at("mem_k", [P, H2, NMEM], F32, AR + 76)
    mem_v = at("mem_v", [P, 2, W2], F32, AR + 80)
    ff = at("ff", [P, H2, S], F32, AR)
    block_f = [ff] + [at(f"block_f{n}", [P, H2, S >> n], F32, AR + 16 - 16 / 2 ** n) for n in range(1, LEVELS + 1)]
    hq = at("hq", [P, H2, S], F32, AR + 16)
    hk = at("hk", [P, H2, S], F32, AR + 24)
    hv = at("hv", [P, TT, W2], F32, AR + 32)
    sg = at("sg", [P, H2, S], F32, AR + 40)
    aT = at("aT", [P, H2, S], F32, AR + 48)
    mq = at("mq", [P, H2, S], F32, AR + 56)
    cq = at("cq", [P, 3, S], F32, AR + 64)
    ckv = at("ckv", [P, 2, S], F32, AR + 70)
    kr = at("kr", [P, S], F32, AR + 74)
    cq_hi = at("cq_hi", [P, 3, S], F32R, AR)
    cq_lo = at("cq_lo", [P, 3, S], F32R, AR + 6)
    ckv_hi = at("ckv_hi", [P, 2, S], F32R, AR + 12)
    ckv_lo = at("ckv_lo", [P, 2, S], F32R, AR + 84)
    k_rows = at("k_rows", [P, 3, W2], F32, AR + 64)
    state = at("state", [P, H2, P], F32, AR + 70)
    o_rows = hv
    hgm_hi = at("hgm_hi", [P, 4, S], F32R, XN)
    hgm_lo = at("hgm_lo", [P, 4, S], F32R, XN + 8)
    qn = at("qn", [P, H2, S], F32, AR + 16)
    kn = at("kn", [P, H2, S], F32, AR + 24)
    qr = at("qr", [P, 2, S], F32, AR + 70)
    krh = at("krh", [P, 2, S], F32, AR + 84)
    v2 = at("v2", [P, TT, W2], F32, AR + 48)
    cos = at("cos", [P, S], F32, AR + 64)
    sin = at("sin", [P, S], F32, AR + 66)
    krb = at("krb", [P, S], F32, AR + 68)
    ra, rb = val
    pos_i = at("pos_i", [P, S], I32, TAIL)
    prob2 = [at(f"prob2_{n}", [P, 1280], F32, AR + 5 * n) for n in range(3)]
    pT2 = [[at(f"pT2_{n}_{b}", [P, S], F32, XN + 16 + 6 * n + 2 * b) for b in range(3)] for n in range(2)]
    y_mem = at("y_mem", [P, TT, W2], F32, AR + 40)
    y_mla = v2
    memm_hi = at("memm_hi", [P, 4, S], F32R, AR + 56)
    memm_lo = at("memm_lo", [P, 4, S], F32R, AR + 76)
    mlam_hi = at("mlam_hi", [P, 4, S], F32R, AR + 16)
    mlam_lo = at("mlam_lo", [P, 4, S], F32R, AR + 24)
    squares = [at(f"squares{n}", [P, TT, W2], F32, kb) for n, kb in enumerate((AR + 40, AR + 56, AR + 16))]
    acc2 = [at(f"acc2_{n}", [P, S], F32, XN + 2 * n) for n in range(2)]
    small = at("small", [P, 128], F32, TAIL + 4)
    decay = small[:, 0:16].rearrange("p (h c) -> p h c", c=TT)
    ssq, rroot, rinv = small[:, 16:32], small[:, 32:48], small[:, 48:64]
    lbv = small[:, 64:96]
    out_rows = at("out_rows", [P, TT, D], F32, AR)

    ctx = ExitStack()
    with ctx:
        ps = [ctx.enter_context(nc.psum_tensor(f"bank{n}", [P, 512], F32)) for n in range(8)]

        def sem(name):
            return ctx.enter_context(nc.semaphore(name))

        raw_loaded = [sem(f"raw_loaded{n}") for n in range(2)]
        w_hi_done, w_lo_done, gemm_done = sem("w_hi_done"), sem("w_lo_done"), sem("gemm_done")
        signals = {f: Signal(sem(f"{f}_freed")) for f in ("act", "dve")}
        signals["val"] = Signal(sem("val_ready"))
        val_ready = signals["val"].sem
        hi_ready, lo_ready = sem("hi_ready"), sem("lo_ready")
        step = Signal(sem("dve_step"))
        x_loaded, consts_loaded, gains_loaded, w2_loaded = (sem(f"{n}_loaded") for n in ("x", "consts", "gains", "w2"))
        masks_loaded = sem("masks_loaded")
        xT_done, h_ready, gains_ready = sem("xT_done"), sem("h_ready"), sem("gains_ready")
        gainsT_done = sem("gainsT_done")
        sq_ready, sq_used, root_ready, rstd_ready = (sem(n) for n in ("sq_ready", "sq_used", "root_ready", "rstd_ready"))
        mixc_ready = sem("mixc_ready")
        blk_hi_ready, blk_lo_ready = sem("blk_hi_ready"), sem("blk_lo_ready")
        sg_ready = sem("sg_ready")
        small_turned, gates_ready, hid_ready = sem("small_turned"), sem("gates_ready"), sem("hid_ready")
        cmp_done, cmp_ready = sem("cmp_done"), sem("cmp_ready")
        k_hi_ready, q_step, q_copied = sem("k_hi_ready"), sem("q_step"), sem("q_copied")
        q_staged, scores_done, scores_taken, negm_ready, exp_done = (
            sem(n) for n in ("q_staged", "scores_done", "scores_taken", "negm_ready", "exp_done"))
        pT_done, pT_act, pT_dve, pv_done, o_taken, diag_ready = (
            sem(n) for n in ("pT_done", "pT_act", "pT_dve", "pv_done", "o_taken", "diag_ready"))
        memT_done, memT_ready, mem_loaded = sem("memT_done"), sem("memT_ready"), sem("mem_loaded")
        level_mul, level_done, level_kept = (sem(n) for n in ("level_mul", "level_done", "level_kept"))
        between_ready, pair_sq, pair_used = sem("between_ready"), sem("pair_sq"), sem("pair_used")
        hq_ready, lb_exp = sem("hq_ready"), sem("lb_exp")
        k_turned, k_rows_ready, chunk_done, state_ready, chunk_out = (
            sem(n) for n in ("k_turned", "k_rows_ready", "chunk_done", "state_ready", "chunk_out"))
        part_sq, part_used, part_root, part_ready = (sem(n) for n in ("part_sq", "part_used", "part_root", "part_ready"))
        pos_loaded, angle_ready, angle_sin, rot_done, rope_ready = (
            sem(n) for n in ("pos_loaded", "angle_ready", "angle_sin", "rot_done", "rope_ready"))
        scores2, taken2, negm2, exp2, turned2, pT2_act, pT2_dve, pv2, y_ready = (
            sem(n) for n in ("scores2", "taken2", "negm2", "exp2", "turned2", "pT2_act", "pT2_dve", "pv2", "y_ready"))
        rows_sq, rows_root, rows_ready, rows_turned = (
            sem(n) for n in ("rows_sq", "rows_root", "rows_ready", "rows_turned"))
        out_turned, out_act, out_dve = sem("out_turned"), sem("out_act"), sem("out_dve")
        out_sent = sem("out_sent")
        pool_waited, dve_waited = sem("pool_waited"), sem("dve_waited")

        jobs = {}
        for job in make_jobs():
            jobs[job.name] = job

        SPLIT = {"norm_mix": signals["val"].reserve(8), "conv": signals["val"].reserve(4),
                 "o": signals["val"].reserve(8)}
        splits = {"attn_out": 8, "up": FC, "up_2": FC}
        order = list(jobs.values())
        PRE = {"up": [("norm_ffn", 8)], "mem_k": [("norm_mem", 8), ("norm_mix_2", 8)],
               "i": [("cq", 3), ("ckv", 2)], "w_out": [("hgm", 4), ("memm", 4), ("mlam", 4)],
               "up_2": [("norm_ffn_2", 8)]}
        ends = plan(order, signals, splits, PRE, SPLIT)

        def const(name, *idx):
            a, b = CONST_COLS[name]
            return consts[:, a:b]

        ident = const("ident")
        ones = const("ones")

        def gain(name, c=0):
            r = GAIN_ROWS[name] + c
            return gains[:, r:r + 1]

        def mask_of(w):
            a, b = CONST_COLS["causal"]
            return consts[:, b - w:b]

        W_IN = A["w_in"][0].rearrange("(c p) n -> p c n", p=P)

        def in_cols(a, n, h, chunks=4):
            return W_IN[:, chunks * h:chunks * h + chunks, bass.ds(a, n)]

        def panel_view(slot, job, tensors=raw):
            return tensors[slot][:, 0:job.used].rearrange("p (k n) -> p k n", k=job.chunks)

        def chunk(name, K):
            if name == "w_out":
                part = [(mlam_hi, mlam_lo), (hgm_hi, hgm_lo), (memm_hi, memm_lo)][K // 4]
                return part[0][:, K % 4, :], part[1][:, K % 4, :]
            return operand[name][0][:, K, :], operand[name][1][:, K, :]

        def wide_load(w):
            def load(dst, i, hh):
                return [(dst, w[:, 4 * hh:4 * hh + 4, bass.ds(512 * i, 512)])]
            return load

        def in_load(first):
            def load(dst, i, hh):
                return [(dst, in_cols(512 * i + first, 512, hh))]
            return load

        def in_load2(a, b):
            def load(dst, i, hh):
                return [(dst[:, :, 0:256], in_cols(a, 256, hh)), (dst[:, :, 256:512], in_cols(b, 256, hh))]
            return load

        def q_load(dst, i, hh):
            pairs = dst.rearrange("p k (t a d) -> p k t a d", t=4, a=2)
            return [(pairs[:, k, :, a, :],
                     in_cols(C_Q + 512 * i + 256 * a, 256, hh)[:, k].rearrange("p (t d) -> p t d", t=4))
                    for a in range(2) for k in range(4)]

        def gates_load(dst, i, hh):
            return [(dst, in_cols(C_BR, 3 * NH, 0, 8))]

        def cmp_load(name):
            w = A[name][0].rearrange("(c p) n -> p c n", p=P)

            def load(dst, i, hh):
                return [(dst, w[:, 8 * hh:8 * hh + 8, :])]
            return load

        def attn_out_load(dst, i, hh):
            w = A["w_attn_out"][0].rearrange("(a g j d) n -> a g d j n", a=2, g=2, j=4)
            return [(dst[64 * g:64 * g + 64], w[hh, g, :, :, 512 * i:512 * i + 512]) for g in range(2)]

        def up_load(gate, up):
            wg = A[gate][0].rearrange("(c p) n -> p c n", p=P)
            wu = A[up][0].rearrange("(c p) n -> p c n", p=P)

            def load(dst, i, hh):
                return [(dst[:, :, 0:256], wg[:, 4 * hh:4 * hh + 4, bass.ds(256 * i, 256)]),
                        (dst[:, :, 256:512], wu[:, 4 * hh:4 * hh + 4, bass.ds(256 * i, 256)])]
            return load

        def down_load(name):
            w = A[name][0].rearrange("(c p) n -> p c n", p=P)

            def load(dst, i, hh):
                k = hh % 2
                return [(dst, w[:, 11 * k:11 * k + 11, bass.ds(256 * i + P * (hh // 2), P)])]
            return load

        def rows_load(name):
            return wide_load(A[name][0].rearrange("(c p) n -> p c n", p=P))

        def w_out_load(dst, i, hh):
            first = 4 * (1, 2, 0)[hh]
            w = A["w_out_2"][0].rearrange("(c p) n -> p c n", p=P)
            return [(dst, w[:, first:first + 4, 512 * i:512 * i + 512])]

        W_IN2 = A["w_in_2"][0].rearrange("(c p) n -> p c n", p=P)

        def in2(first, n=512):
            def load(dst, i, hh):
                return [(dst, W_IN2[:, 4 * hh:4 * hh + 4, first:first + n])]
            return load

        def lat_b_load(dst, i, hh):
            k = slice(4 * hh, 4 * hh + 4)
            return [(dst[:, :, 0:P], W_IN2[:, k, 512:512 + P])] + [
                (dst[:, :, P + ROPE * x:P + ROPE * x + ROPE], W_IN2[:, k, I_KR:I_KR + ROPE]) for x in range(2)]

        def heads_load(name, each, first, width):
            w = A[name][0].rearrange("(c p) n -> p c n", p=P)

            def load(dst, i, hh):
                return [(dst[:, :, width * n:width * n + width], w[:, :, each * n + first:each * n + first + width])
                        for n in range(H2)]
            return load

        def mem_load(first):
            w = A["w_mem_kv_2"][0].rearrange("(c p) n -> p c n", p=P)

            def load(dst, i, hh):
                return [(dst, w[:, 4 * hh:4 * hh + 4, first:first + 512])]
            return load

        load_of = {
            "mem_k": mem_load(0), "mem_v": mem_load(512), "f": in2(I_HF), "hq": in2(I_HQ), "lat_a": in2(0),
            "lat_b": lat_b_load, "mq": in2(I_MQ), "i": in2(I_HI), "g": in2(I_HG),
            "uq_nope": heads_load("w_uq_2", QKH, 0, NOPE), "uq_rope": heads_load("w_uq_2", QKH, NOPE, ROPE),
            "ukv_k": heads_load("w_ukv_2", NOPE + VH, 0, NOPE), "ukv_v": heads_load("w_ukv_2", NOPE + VH, NOPE, VH),
            "w_out": w_out_load, "up_2": up_load("w_gate_2", "w_up_2"), "down_2": down_load("w_down_2"),
            "conv_in": in_load(0), "gate_attn": in_load(C_GA), "conv_out": rows_load("w_conv_out"),
            "gate_conv": in_load(C_GC), "q": q_load, "kv_cmp": in_load(C_KC), "k": in_load2(C_KS, C_KW),
            "v": in_load2(C_VS, C_VW), "gates": gates_load, "cmp_k": cmp_load("cmp_w1_k"),
            "cmp_v": cmp_load("cmp_w1_v"), "attn_out": attn_out_load, "w_o": rows_load("w_o"),
            "up": up_load("w_gate", "w_up"), "down": down_load("w_down"),
        }
        operand = {
            "mem_k": (mem_hi, mem_lo), "mem_v": (mem_hi, mem_lo), "f": (xn_hi, xn_lo), "hq": (xn_hi, xn_lo),
            "lat_a": (xn_hi, xn_lo), "lat_b": (xn_hi, xn_lo), "mq": (xn_hi, xn_lo), "i": (xn_hi, xn_lo),
            "g": (xn_hi, xn_lo), "uq_nope": (cq_hi, cq_lo), "uq_rope": (cq_hi, cq_lo), "ukv_k": (ckv_hi, ckv_lo),
            "ukv_v": (ckv_hi, ckv_lo), "w_out": None, "up_2": (xn_hi, xn_lo), "down_2": (hid_hi, hid_lo),
            "conv_in": (xn_hi, xn_lo), "gate_attn": (xn_hi, xn_lo), "conv_out": (cv_hi, cv_lo),
            "gate_conv": (xn_hi, xn_lo), "q": (xn_hi, xn_lo), "kv_cmp": (xn_hi, xn_lo), "k": (xn_hi, xn_lo),
            "v": (xn_hi, xn_lo), "gates": (xn_hi, xn_lo), "cmp_k": (blk_hi[0], blk_lo[0]),
            "cmp_v": (blk_hi[1], blk_lo[1]), "attn_out": (o_hi, o_lo), "w_o": (mix_hi, mix_lo),
            "up": (xn_hi, xn_lo), "down": (hid_hi, hid_lo),
        }

        def split_wait(base):
            return lambda k: (lo_ready, base + k + 1)

        operand_ready = {
            "mem_k": split_wait(SPLIT["norm_mem"]), "f": split_wait(SPLIT["norm_mix_2"]),
            "uq_nope": split_wait(SPLIT["cq"]), "ukv_k": split_wait(SPLIT["ckv"]), 
            "w_out": lambda k: (lo_ready, SPLIT[("mlam", "hgm", "memm")[k // 4]] + k % 4 + 1),
            "up_2": split_wait(SPLIT["norm_ffn_2"]), "down_2": split_wait(jobs["up_2"].split0),
            "conv_in": split_wait(SPLIT["norm_mix"]), "conv_out": split_wait(SPLIT["conv"]),
            "cmp_k": lambda k: (blk_lo_ready, 1), "cmp_v": lambda k: (blk_lo_ready, 2),
            "attn_out": split_wait(SPLIT["o"]), "w_o": split_wait(jobs["attn_out"].split0),
            "up": split_wait(SPLIT["norm_ffn"]), "down": split_wait(jobs["up"].split0),
        }

        def over_blocks(eng, job, body, ahead=0):
            body(0)
            if job.looped:
                with eng.Fori(1, job.blocks) as i:
                    body(i)
            else:
                for i in range(1, job.blocks):
                    body(i)

        def loads_until(job, i, hh):
            slot = (job.panel0 + hh) % 2 if job.looped else (job.panel0 + job.panels * i + hh) % 2
            if job.looped:
                before = i * (job.panels // 2) + len([x for x in range(hh) if (hh - x) % 2 == 0]) + 1
            else:
                n = job.panels * i + hh
                before = len([x for x in range(n + 1) if (n - x) % 2 == 0])
            return slot, job.load0[slot] + job.loads * before

        def end_before(job, i, hh):
            if isinstance(i, int):
                p = job.panel0 + job.panels * i + hh
                return ends[p - 2] if p >= 2 else None
            g = len(job.groups)
            if hh >= 2:
                return job.group0 + g * i + job.end_of_panel[hh - 2]
            return job.group0 + g * (i - 1) + job.end_of_panel[hh - 2 + job.panels]

        def sp_job(sp, name):
            job = jobs[name]

            def block(i):
                for hh in range(job.panels):
                    p = job.panel0 + job.panels * i + hh
                    slot = loads_until(job, 0 if job.looped else i, hh)[0]
                    if not isinstance(p, int) or p >= 2:
                        sp.wait_ge(w_lo_done, p - 1)
                    for dst, src in load_of[name](panel_view(slot, job), i, hh):
                        sp.dma_start(dst, src).then_inc(raw_loaded[slot], 16)
            over_blocks(sp, job, block)

        def pool_job(pool, name):
            job = jobs[name]

            def block(i):
                for hh in range(job.panels):
                    p = job.panel0 + job.panels * i + hh
                    slot, n = loads_until(job, i, hh)
                    pool.wait_ge(raw_loaded[slot], n * 16)
                    e = end_before(job, i, hh)
                    if e is not None:
                        pool.wait_ge(gemm_done, e)
                    if not isinstance(i, int):
                        pool.sem_inc(pool_waited, 1)
                    src = raw[slot][:, 0:job.used]
                    hi, lo = w_hi[slot][:, 0:job.used], w_lo[slot][:, 0:job.used]
                    pool.tensor_scalar(hi, src, 1.0, 1.0, ALU.mult, ALU.mult).then_inc(w_hi_done, 1)
                    pool.wait_ge(w_hi_done, p + 1)
                    pool.tensor_tensor(lo, src, hi.bitcast(F32), ALU.subtract).then_inc(w_lo_done, 1)
            over_blocks(pool, job, block)

        def pe_job(pe, name, after=None):
            job = jobs[name]
            seen = set()

            def block(i):
                opened, started = set(), set()
                todo = job.groups
                spread = isinstance(i, int) and i == 0 and name in operand_ready and len(job.groups[0][2]) > 1 \
                    and job.panels < 4
                if spread:
                    now = [x for x in todo if x[0] == 0]
                    todo = [(0, t, [ks[n]]) for n in range(len(now[0][2])) for _, t, ks in now] + [
                        x for x in todo if x[0]]
                for panel, tile, ks in todo:
                    whole = not (spread and panel == 0)
                    p = job.panel0 + job.panels * i + panel
                    slot = loads_until(job, 0 if job.looped else i, panel)[0]
                    if panel not in opened:
                        opened.add(panel)
                        pe.wait_ge(w_lo_done, p + 1)
                    bank = ps[job.banks[tile]]
                    first = tile not in started
                    if first:
                        started.add(tile)
                        if not isinstance(i, int) or i > 0:
                            pe.wait_ge(signals[job.freed_by[tile]].sem, freed(job, tile, i - 1))
                        elif job.tenant0[job.banks[tile]]:
                            f, n = job.tenant0[job.banks[tile]]
                            pe.wait_ge(signals[f].sem, n)
                    last_of_tile = (panel, tile) == [(a, b) for a, b, _ in job.groups if b == tile][-1]
                    hi, lo = panel_view(slot, job, w_hi), panel_view(slot, job, w_lo)
                    for n, (k, K) in enumerate(ks):
                        if K not in seen:
                            seen.add(K)
                            if name in operand_ready:
                                pe.wait_ge(*operand_ready[name](K))
                        xh, xl = chunk(name, K)
                        last_k = n == len(ks) - 1 if whole else K == job.groups[0][2][-1][1]
                        begin, end = first and n == 0, last_of_tile and last_k
                        if job.natural:
                            o = bank[0:job.rows, 0:job.cols]
                            tokens = slice(P * tile, P * tile + job.rows)
                            a, b = xh[:, tokens], xl[:, tokens]
                            pe.matmul(o, a, hi[:, k, :], start=begin, stop=False)
                            pe.matmul(o, a, lo[:, k, :], start=False, stop=False)
                            mm = pe.matmul(o, b, hi[:, k, :], start=False, stop=end)
                        else:
                            o = bank[0:job.rows, 0:job.tokens]
                            a = hi[:, k, P * tile:P * tile + P] if job.cols > P else hi[:, k, :]
                            b = lo[:, k, P * tile:P * tile + P] if job.cols > P else lo[:, k, :]
                            pe.matmul(o, a, xh, start=begin, stop=False)
                            pe.matmul(o, a, xl, start=False, stop=False)
                            mm = pe.matmul(o, b, xh, start=False, stop=end)
                    if last_k:
                        mm.then_inc(gemm_done, 1)
                    if last_k and after:
                        after(i, panel, tile)
            over_blocks(pe, job, block)

        def act_hi(act, n, dst, src=None, slot=None):
            act.wait_ge(val_ready, n + 1)
            act.activation(dst, val[slot][:, 0:dst.shape[-1]] if src is None else src, ACT.Copy).then_inc(hi_ready, 1)

        def val_free(dve, n):
            if not isinstance(n, int) or n >= 2:
                dve.wait_ge(lo_ready, n - 1)

        def dve_lo(dve, n, dst, hi, src=None, slot=None):
            dve.wait_ge(hi_ready, n + 1)
            dve.tensor_tensor(dst, val[slot][:, 0:dst.shape[-1]] if src is None else src, hi.bitcast(F32),
                              ALU.subtract).then_inc(lo_ready, 1)

        norms = {}

        def add_norm(name, src, dst, gain_name, chunks, split0, ready, tokens=S, width=None):
            norms[name] = dict(n=len(norms), bank=4 + len(norms) % 2, sqs=0 if ready is None else chunks, src=src, dst=dst, gain=gain_name, chunks=chunks, split0=split0,
                               ready=ready, tokens=tokens, width=width or chunks * P, done=h_ready,
                               sq0=sum(x["sqs"] for x in norms.values()))

        add_norm("mix", h, (xn_hi, xn_lo), "g_mix", KC, SPLIT["norm_mix"], lambda c: (h_ready, c + 1))
        add_norm("ffn", h, (xn_hi, xn_lo), "g_ffn", KC, SPLIT["norm_ffn"],
                 lambda c: (signals["dve"].sem, freed(jobs["w_o"], c % 4, c // 4)))
        add_norm("mem", memT, (mem_hi, mem_lo), "norm_mem", KC, SPLIT["norm_mem"], lambda c: (memT_ready, c // 2 + 1),
                 tokens=NMEM)
        add_norm("final", h, (h, None), "g_final", KC, None, None)
        add_norm("mix_2", h, (xn_hi, xn_lo), "norm_mix", KC, SPLIT["norm_mix_2"], None)
        add_norm("cq", cq, (cq_hi, cq_lo), "q_a", 3, SPLIT["cq"],
                 lambda c: (signals["act"].sem, freed(jobs["lat_a"], c, 0)))
        add_norm("ckv", ckv, (ckv_hi, ckv_lo), "kv_a", 2, SPLIT["ckv"],
                 lambda c: (signals["act"].sem, freed(jobs["lat_b"], 0, 0)))

        def add_parts(name, parts, width, tokens, ready):
            add_norm(name, None, None, None, len(parts), None, ready, tokens, width)
            norms[name].update(parts=parts, done=part_ready)

        for n in range(H2):
            k_ = mem_k[:, n, :]
            add_parts(f"mem_k{n}", [(k_, k_, gain("mem_k"), k_)], P, NMEM,
                      lambda c: (signals["act"].sem, freed(jobs["mem_k"], 3, 0)))
        for n in range(H2):
            q_ = mq[:, n, :]
            add_parts(f"mem_q{n}", [(q_, q_, gain("mem_q"), q_)], P, S,
                      lambda c: (signals["act"].sem, freed(jobs["mq"], 3, 0)))
        for n in range(2 * H2):
            j = n % H2
            r_ = slice(ROPE * (j % 2), ROPE * (j % 2) + ROPE)
            q_, qr_, k_, kr_ = qn[:, j, :], qr[r_, j // 2, :], kn[:, j, :], krh[r_, j // 2, :]
            if n < H2:
                add_parts(f"q{j}", [(q_, q_, gain("mla_q"), q_), (qr_, qr_, gain("mla_q", 1)[r_, :], qr_)], QKH, S,
                          lambda c: (signals["act"].sem, freed(jobs["uq_rope"], 1, 0)))
            else:
                add_parts(f"k{j}", [(k_, k_, gain("mla_k"), k_), (kr[0:ROPE, :], krb[r_, :], None, kr_)], QKH, S,
                          lambda c: (signals["act"].sem, freed(jobs["ukv_k"], 3, 0)))
        add_norm("ffn_2", h, (xn_hi, xn_lo), "norm_ffn", KC, SPLIT["norm_ffn_2"],
                 lambda c: (signals["dve"].sem, freed(jobs["w_out"], c % 4, c // 4)))

        def parts_of(m):
            N = m["tokens"]
            if "parts" in m:
                return m["parts"]
            return [(m["src"][:, c, 0:N], m["src"][:, c, 0:N], gain(m["gain"], c), m["dst"][0][:, c, 0:N])
                    for c in range(m["chunks"])]

        def act_rstd(act, sums, dst, n, width):
            act.activation(sums, sums, ACT.Ln, scale=1.0 / width, bias=const("eps")).then_inc(root_ready, 1)
            act.wait_ge(root_ready, n + 1)
            act.activation(dst, sums, ACT.Exp, scale=-0.5).then_inc(rstd_ready, 1)

        def norm_table(act):
            act.preload_act_table_set("natural_log_exp_and_others")

        def act_norm(act, name):
            act_squares(act, name)
            act_factor(act, name)

        def act_norms_in_turn(act, names, between=lambda n: None):
            for n, name in enumerate(names):
                if n == 0:
                    act_squares(act, name)
                between(n)
                if n + 1 < len(names):
                    act_squares(act, names[n + 1])
                act_factor(act, name)

        def act_squares(act, name):
            m = norms[name]
            N = m["tokens"]
            for c, (src, *_) in enumerate(parts_of(m)):
                if m["ready"](c) is not None:
                    act.wait_ge(*m["ready"](c))
                k = m["sq0"] + c
                if k >= 2:
                    act.wait_ge(sq_used, k - 1)
                rows = src.shape[0]
                act.activation(sq[k % 2][0:rows, 0:N], src, ACT.Square).then_inc(sq_ready, 1)

        def act_factor(act, name):
            m = norms[name]
            N = m["tokens"]
            act.wait_ge(sq_used, m["sq0"] + m["chunks"])
            if m["n"] >= 2:
                act.wait_ge(*norm_done([x for x in norms.values() if x["n"] == m["n"] - 2][0]))
            act_rstd(act, ps[m["bank"]][:, 0:N], rstd[m["n"] % 2][:, 0:N], m["n"], m["width"])
            if m["split0"] is not None:
                for c in range(m["chunks"]):
                    act_hi(act, m["split0"] + c, m["dst"][0][:, c, :], slot=(m["split0"] + c) % 2)

        def pe_sum(pe, name, c):
            m = norms[name]
            N = m["tokens"]
            if c == 0 and m["n"] >= 2:
                pe.wait_ge(rstd_ready, m["n"] - 1)
            k = m["sq0"] + c
            rows = parts_of(m)[c][0].shape[0]
            pe.wait_ge(sq_ready, k + 1)
            pe.matmul(ps[m["bank"]][:, 0:N], ones[0:rows, :], sq[k % 2][0:rows, 0:N], start=c == 0,
                      stop=c == m["chunks"] - 1).then_inc(sq_used, 1)

        def pe_norm(pe, name, first=0):
            for c in range(first, norms[name]["chunks"]):
                pe_sum(pe, name, c)

        def dve_sum(dve, name, c):
            m = norms[name]
            acc = rstd[m["n"] % 2]
            if c == 0:
                return
            dve.wait_ge(sq_ready, m["sq0"] + c + 1)
            if c == 1:
                dve.tensor_tensor(acc[:], sq[0][:], sq[1][:], ALU.add).then_inc(sq_used, 2)
            else:
                dve.wait_ge(sq_used, m["sq0"] + c)
                dve.tensor_tensor(acc[:], acc[:], sq[(m["sq0"] + c) % 2][:], ALU.add).then_inc(sq_used, 1)

        def pe_norm_rest(pe, name):
            m = norms[name]
            bank = ps[m["bank"]]
            pe.wait_ge(rstd_ready, m["n"] - 1)
            pe.wait_ge(sq_used, m["sq0"] + KC - 1)
            pe.matmul(bank[:, :], ones[:, :], rstd[m["n"] % 2][:, :], start=True, stop=False)
            pe.wait_ge(sq_ready, m["sq0"] + KC)
            pe.matmul(bank[:, :], ones[:, :], sq[(m["sq0"] + KC - 1) % 2][:, :], start=False,
                      stop=True).then_inc(sq_used, 1)

        def dve_adds(dve, name, norm):
            for i in range(2):
                for t in range(4):
                    c = 4 * i + t
                    dve.wait_ge(gemm_done, tile_done(jobs[name], t, i))
                    dve.tensor_tensor(h[:, c, :], ps[jobs[name].banks[t]][:, :], h[:, c, :],
                                      ALU.add).then_inc(signals["dve"].sem, 1)
                    if c:
                        dve_sum(dve, norm, c - 1)

        def pe_sums(pe):
            for x, name in enumerate(("final", "mix_2")):
                bank = ps[norms[name]["bank"]]
                pe.wait_ge(pair_used, 2 * (KC - 2))
                pe.matmul(bank[:, :], ones[:, :], acc2[x][:, :], start=True, stop=False)
                pe.wait_ge(pair_sq, 2 * KC)
                pe.matmul(bank[:, :], ones[:, :], sq[x][:, :], start=False, stop=True).then_inc(pair_used, 1)

        def dve_sums(dve, c, first=False):
            for x in range(2):
                dve.wait_ge(pair_sq, 2 * c + x + 1)
                if not first:
                    dve.wait_ge(pair_used, 2 * c + x - 3)
                dve.tensor_tensor(acc2[x][:], acc2[x][:], sq[x][:], ALU.add).then_inc(pair_used, 1)

        def act_norms(act):
            job = jobs["down"]

            def squares(i):
                for t in range(2):
                    c = 2 * i + t
                    act.wait_ge(signals["dve"].sem, freed(job, t, i))
                    for x in range(2):
                        dst = acc2[x] if i_is(i, 0) and t == 0 else sq[x]
                        if not i_is(i, 0):
                            act.wait_ge(pair_used, 2 * c + x - 3)
                        g = GAIN_ROWS["g_final"]
                        act.activation(dst[:, :], h[:, c, :], ACT.Square,
                                       scale=gains[:, bass.ds(g + c, 1)] if x else 1.0).then_inc(pair_sq, 1)
            over_blocks(act, job, squares)
            act.wait_ge(pair_used, 2 * (KC - 1))
            b1 = ps[norms["final"]["bank"]]
            n1, n2 = norms["final"]["n"], norms["mix_2"]["n"]
            act_rstd(act, b1[:, :], rstd[n1 % 2][:, :], n1, D)
            act.wait_ge(*norm_done(norms["mem"]))
            act.activation(rstd[n2 % 2][:, :], b1[:, :], ACT.Exp, scale=-1.0).then_inc(pair_sq, 1)
            act.wait_ge(between_ready, 1)
            act_rstd(act, sq[0][:, :], rstd[n2 % 2][:, :], n2, D)
            for c in range(KC):
                act_hi(act, SPLIT["norm_mix_2"] + c, xn_hi[:, c, :], slot=(SPLIT["norm_mix_2"] + c) % 2)
                if c == 1:
                    act_take(act, "mem_k", [mem_k[:, t, :] for t in range(H2)])
                    act_take(act, "mem_v", [mem_v[:, t, :] for t in range(2)])

        def dve_norms(dve):
            n1, n2 = norms["final"]["n"], norms["mix_2"]["n"]
            r1, r2 = rstd[n1 % 2], rstd[n2 % 2]
            dve.wait_ge(pair_sq, 2 * KC + 1)
            dve.tensor_tensor(sq[0][:], r2[:], ps[norms["mix_2"]["bank"]][:, :], ALU.mult).then_inc(between_ready, 1)
            s0 = SPLIT["norm_mix_2"]

            def scale(c):
                dve.scalar_tensor_tensor(h[:, c, :], h[:, c, :], gain("g_final", c), r1[:], ALU.mult,
                                         ALU.mult).then_inc(h_ready, 1)
            scale(0)
            scale(1)
            dve.wait_ge(rstd_ready, n2 + 1)

            def value(c):
                val_free(dve, s0 + c)
                dve.wait_ge(h_ready, KC + c + 1)
                dve.scalar_tensor_tensor(val[(s0 + c) % 2][:, :], h[:, c, :], gain("norm_mix", c), r2[:],
                                         ALU.mult, ALU.mult).then_inc(val_ready, 1)
            for c in range(KC):
                value(c)
                if c + 2 < KC:
                    scale(c + 2)
                if c == 1:
                    dve.wait_ge(gemm_done, tile_done(jobs["mem_v"], 1, 0))
                if c:
                    dve_lo(dve, s0 + c - 1, xn_lo[:, c - 1, :], xn_hi[:, c - 1, :], slot=(s0 + c - 1) % 2)
            dve_lo(dve, s0 + c, xn_lo[:, c, :], xn_hi[:, c, :], slot=(s0 + c) % 2)

        def dve_step(dve, ins):
            ins.then_inc(step.sem, 1)
            dve.wait_ge(step.sem, step.reserve(1) + 1)

        def norm_done(m):
            if m["split0"] is not None:
                return lo_ready, m["split0"] + m["chunks"]
            if "parts" in m:
                return part_ready, sum(len(x["parts"]) for x in norms.values() if "parts" in x and x["n"] <= m["n"])
            return h_ready, 2 * KC

        def dve_norm(dve, name):
            m = norms[name]
            N = m["tokens"]
            r = rstd[m["n"] % 2]
            dve.wait_ge(rstd_ready, m["n"] + 1)
            s0 = m["split0"]
            if s0 is None:
                done = m["done"]
                for _, src, g, dst in parts_of(m):
                    a = dst.start_partition()
                    rr = r[a:a + dst.shape[0], 0:N]
                    if g is None:
                        ins = dve.tensor_tensor(dst, src, rr, ALU.mult)
                    else:
                        ins = dve.scalar_tensor_tensor(dst, src, g, rr, ALU.mult, ALU.mult)
                    ins.then_inc(done, 1)
                return
            for c in range(m["chunks"]):
                val_free(dve, s0 + c)
                dve.scalar_tensor_tensor(val[(s0 + c) % 2][:, 0:N], m["src"][:, c, 0:N], gain(m["gain"], c),
                                         r[:, 0:N], ALU.mult, ALU.mult).then_inc(val_ready, 1)
                if c:
                    dve_lo(dve, s0 + c - 1, m["dst"][1][:, c - 1, :], m["dst"][0][:, c - 1, :], slot=(s0 + c - 1) % 2)
            c = m["chunks"] - 1
            dve_lo(dve, s0 + c, m["dst"][1][:, c, :], m["dst"][0][:, c, :], slot=(s0 + c) % 2)

        PACK = [[(3, 0)], [(2, NCMP_EVEN)], [(1, NCMP_EVEN), (0, 2 * NCMP_EVEN + 2 * P)]]
        CMP3 = NCMP_EVEN + 3 * P

        POFF = {3: 0, 2: 512, 0: 896, 1: 1024}
        SCALE = HD ** -0.5

        def qk_bank(pe, a, it, c, b):
            win = c % 2
            un = 4 * it + c
            half = c // 2
            at_ = K_AT[2 * win + a] + (0 if win else NCMP_EVEN)
            if b == 0 and not win:
                pe.wait_ge(q_staged, 2 * it + c // 2 + 1)
            n = 3 * un + b
            bank = ps[(3 * c + b) % 3]
            if not isinstance(n, int) or n >= 3:
                pe.wait_ge(scores_taken, n - 2)
            todo = [(i, off, P * (i + 1), 0) for i, off in PACK[b]]
            if not win:
                if b:
                    todo = [(i, off - NCMP_EVEN, w + NCMP_EVEN, -NCMP_EVEN) for i, off, w, _ in todo]
                if b == 1:
                    todo.append((3, CMP3, NCMP_EVEN, -NCMP_EVEN))
            for i, off, w, first in todo:
                o, kt = bank[:, off:off + w], k_pairs[half][:, at_ + first:at_ + first + w]
                pe.matmul(o, q_hi[half][:, P * i:P * i + P], kt, start=True, stop=False)
                mm = pe.matmul(o, q_lo[half][:, P * i:P * i + P], kt, start=False, stop=True)
            mm.then_inc(scores_done, 1)

        TURN = []
        for c in range(4):
            for b in (0, 1, 2) if c % 2 else (0, 3, 1, 2):
                TURN.append((c, b, "act" if b in (0, 3) else "dve"))
        TACT = sum(e == "act" for *_, e in TURN)
        TDVE = len(TURN) - TACT

        def turn_index(c, b):
            return [x[:2] for x in TURN].index((c, b))

        def pT_taken(it, k):
            if k < 0:
                k, it = k + len(TURN), it - 1
            e = TURN[k][2]
            n = sum(x[2] == e for x in TURN[:k]) + 1
            return (pT_act, TACT * it + n) if e == "act" else (pT_dve, TDVE * it + n)

        def prob_item(c, i):
            return prob[c][:, POFF[i]:POFF[i] + P * (i + 1)]

        def prob_cmp(c, i):
            return prob[c][:, 1280 + NCMP * i:1280 + NCMP * (i + 1)]

        KEYS = [[(0, i, P * i) for i in range(4)], [(1, 1, 0), (1, 2, P), (1, 3, 2 * P), (3, 3, 3 * P)],
                [(2, 2, 0), (2, 3, P)]]

        def turn(pe, it, c, b):
            k = turn_index(c, b)
            if not (isinstance(it, int) and it == 0 and k < 2):
                sg, n = pT_taken(it, k - 2)
                pe.wait_ge(sg, n)
            bank = ps[4 + k % 2]
            if b == 3:
                for i in range(TT):
                    mm = pe.matmul(bank[0:NCMP, P * i:P * i + P], prob_cmp(c, i), diag[0][:, i, :],
                                   start=True, stop=True)
            else:
                for kt, i, off in KEYS[b]:
                    mm = pe.matmul(bank[:, off:off + P], prob_item(c, i)[:, P * kt:P * kt + P],
                                   diag[c % 2][:, i + 4 * (1 - c % 2), :], start=True, stop=True)
            mm.then_inc(pT_done, 1)

        def pv(pe, a, it, c, b):
            sg, n = pT_taken(it, turn_index(c, b))
            pe.wait_ge(sg, n)
            g = 2 * a + c // 2
            r = 64 * (c // 2)
            o = ps[6 + c // 2][r:r + 64, :]
            src = pT[c % 2][b]
            if b == 3:
                return pe.matmul(o[:, :], v_cmp[0:NCMP, g, :], src[0:NCMP, :], start=False, stop=False)
            col = 256 * (c % 2) + HD * g
            for kt, off in ((0, 0),) if b == 0 else ((1, 0), (3, 3 * P)) if b == 1 else ((2, 0),):
                w = S - P * kt
                mm = pe.matmul(o[:, P * kt:S], v_rows[:, kt, col:col + HD], src[:, off:off + w],
                               start=kt == 0 and c % 2 == 0, stop=kt == 2 and c % 2 == 1)
            return mm

        def pe_slot(pe, products, scores):
            if products:
                a, it, c = products
                un = 4 * it + c
                pe.wait_ge(diag_ready, un + 1)
                turn(pe, it, c, 0)
            if scores:
                qk_bank(pe, *scores, 0)
            if products:
                if c % 2 == 0:
                    turn(pe, it, c, 3)
                turn(pe, it, c, 1)
                if c % 2 == 0 and not (isinstance(it, int) and it == 0):
                    if c:
                        pe.wait_ge(val_ready, SPLIT["o"] + it)
                    else:
                        pe.wait_ge(o_taken, it)
                pv(pe, a, it, c, 0)
                turn(pe, it, c, 2)
            if scores:
                qk_bank(pe, *scores, 1)
            if products:
                pv(pe, a, it, c, 1)
                if c % 2 == 0:
                    pv(pe, a, it, c, 3)
            if scores:
                qk_bank(pe, *scores, 2)
            if products:
                pv(pe, a, it, c, 2).then_inc(pv_done, 1)

        def pairs(eng, body):
            for a in range(2):
                body(a, 4 * a)
                with eng.Fori(4 * a + 1, 4 * a + 4) as it:
                    body(a, it)

        def pe_attention(pe):
            pe.wait_ge(cmp_ready, 2)
            pe.wait_ge(signals["act"].sem, freed(jobs["cmp_v"], 0, 0))

            def body(a, it):
                before = not (isinstance(it, int) and it == 0)
                prev = 0 if isinstance(it, int) and it == 4 else a
                pe_slot(pe, (prev, it - 1, 1) if before else None, (a, it, 0))
                pe_slot(pe, (prev, it - 1, 2) if before else None, (a, it, 1))
                pe_slot(pe, (prev, it - 1, 3) if before else None, (a, it, 2))
                pe_slot(pe, (a, it, 0), (a, it, 3))
            pairs(pe, body)
            for c in (1, 2, 3):
                pe_slot(pe, (1, 7, c), None)

        def take_pT(eng, it, c, b):
            un = 4 * it + c
            k = turn_index(c, b)
            if b in (0, 1) and (not isinstance(un, int) or un >= 2):
                eng.wait_ge(pv_done, un - 1)
            eng.wait_ge(pT_done, len(TURN) * it + k + 1)
            rows = NCMP if b == 3 else P
            w = 256 if b == 2 else 512
            dst, src = pT[c % 2][b][0:rows, 0:w], ps[4 + k % 2][0:rows, 0:w]
            if TURN[k][2] == "act":
                eng.activation(dst, src, ACT.Copy).then_inc(pT_act, 1)
            else:
                eng.tensor_copy(dst, src).then_inc(pT_dve, 1)

        def mstat(kind, c):
            return stat[:, kind, c, :]

        def act_exps(act, it, c):
            un = 4 * it + c
            act.wait_ge(negm_ready, un + 1)
            for i in range(TT):
                if c % 2 == 0:
                    act.activation(prob_cmp(c, i), prob_cmp(c, i), ACT.Exp, bias=mstat(1, c)[:, i:i + 1],
                                   scale=SCALE, accum_out=mstat(2, c)[:, i:i + 1])
            for i in (3, 2, 0, 1):
                n = i + 4 * (1 - c % 2)
                ins = act.activation(prob_item(c, i), prob_item(c, i), ACT.Exp, bias=mstat(1, c)[:, n:n + 1],
                                     scale=SCALE, accum_out=mstat(2, c)[:, n:n + 1])
            ins.then_inc(exp_done, 1)

        def act_slot(act, products, probs):
            if products:
                take_pT(act, *products, 0)
                if products[1] % 2 == 0:
                    take_pT(act, *products, 3)
            if probs:
                act_exps(act, *probs)

        def act_attention(act):
            def body(a, it):
                before = not (isinstance(it, int) and it == 0)
                act_slot(act, (it - 1, 1) if before else None, (it - 1, 3) if before else None)
                act_slot(act, (it - 1, 2) if before else None, (it, 0))
                act_slot(act, (it - 1, 3) if before else None, (it, 1))
                act_slot(act, (it, 0), (it, 2))
            pairs(act, body)
            act_slot(act, (7, 1), (7, 3))
            act_slot(act, (7, 2), None)
            act_slot(act, (7, 3), None)

        def dve_max(dve, it, c, b):
            un = 4 * it + c
            items = 4 if c % 2 else 8
            if b == 0 and (not isinstance(un, int) or un >= 4):
                dve.wait_ge(pv_done, un - 3)
            dve.wait_ge(scores_done, 3 * un + b + 1)
            if not isinstance(un, int):
                dve.sem_inc(dve_waited, 1)
            bank = ps[(3 * c + b) % 3]
            todo = [(bank[:, off:off + P * (i + 1)], prob_item(c, i), mask_of(P * (i + 1)), i + items - 4)
                    for i, off in PACK[b]]
            if b and items == 8:
                a_, b_ = CONST_COLS["cmp"]
                todo += [(bank[:, off:off + NCMP], prob_cmp(c, i), consts[:, a_ + NCMP * i:a_ + NCMP * (i + 1)], i)
                         for i, off in [(i, off - NCMP_EVEN) for i, off in PACK[b]] + [(3, CMP3)] * (b == 1)]
            for src, dst, mask, n in todo:
                ins = dve.tensor_tensor_reduce(out=dst, in0=src, in1=mask, scale=1.0, scalar=NEG,
                                               op0=ALU.add, op1=ALU.max, accum_out=mstat(0, c)[:, n:n + 1])
            ins.then_inc(scores_taken, 1)
            if b == 2:
                dve.wait_ge(scores_taken, 3 * un + 3)
                dve.tensor_scalar(mstat(1, c)[:, 0:items], mstat(0, c)[:, 0:items], FLOOR, -SCALE,
                                  ALU.max, ALU.mult).then_inc(negm_ready, 1)

        STEPS = 3
        att_step = sem("att_step")

        def dve_weigh(dve, a, it, c):
            un = 4 * it + c
            items = 4 if c % 2 else 8
            s0 = STEPS * un
            l, w = mstat(2, c)[:, 0:items], mstat(3, c)[:, 0:items]
            dve.wait_ge(exp_done, un + 1)
            if not isinstance(un, int) or un >= 2:
                dve.wait_ge(diag_ready, un - 1)
            dve.tensor_scalar(w, l, 1e-30, None, ALU.max).then_inc(att_step, 1)
            dve.wait_ge(att_step, s0 + 1)
            dve.reciprocal(l, w).then_inc(att_step, 1)
            dve.wait_ge(att_step, s0 + 2)
            head = it + 4 * a + 4 * (c // 2)
            g = gates[:, :, :].rearrange("p (b h) i -> p h b i", b=3)[:, head, (2 if c % 2 else 0):(3 if c % 2 else 2), :]
            dve.tensor_tensor(w.rearrange("p (b i) -> p b i", i=TT), l.rearrange("p (b i) -> p b i", i=TT), g,
                              ALU.mult).then_inc(att_step, 1)

        def dve_take_head(dve, it, r):
            dve.wait_ge(pv_done, 4 * it + 2 * r + 2)
            rows = slice(64 * r, 64 * r + 64)
            if r:
                dve.tensor_copy(oT[rows, it, :], ps[7][rows, :]).then_inc(val_ready, 1)
            else:
                dve.tensor_copy(oT[rows, it, :], ps[6][rows, :]).then_inc(o_taken, 1)

        def dve_attention(dve):
            def slot(products, scores, weighed, taken):
                if weighed:
                    dve_weigh(dve, *weighed)
                if scores:
                    dve_max(dve, *scores, 0)
                if products:
                    take_pT(dve, *products, 1)
                    take_pT(dve, *products, 2)
                if taken:
                    dve_take_head(dve, *taken)
                if scores:
                    dve_max(dve, *scores, 1)
                    dve_max(dve, *scores, 2)

            def body(a, it):
                before = not (isinstance(it, int) and it == 0)
                prev = 0 if isinstance(it, int) and it == 4 else a
                slot((it - 1, 1) if before else None, (it, 0), (prev, it - 1, 2) if before else None, None)
                slot((it - 1, 2) if before else None, (it, 1), (prev, it - 1, 3) if before else None,
                     (it - 1, 0) if before else None)
                slot((it - 1, 3) if before else None, (it, 2), (a, it, 0), None)
                slot((it, 0), (it, 3), (a, it, 1), (it - 1, 1) if before else None)
            pairs(dve, body)
            slot((7, 1), None, (1, 7, 2), None)
            slot((7, 2), None, (1, 7, 3), (7, 0))
            slot((7, 3), None, None, None)
            dve_take_head(dve, 7, 1)

        def pool_attention(pool):
            def stage(a, it, half):
                rows = slice(64 * half, 64 * half + 64)
                if isinstance(it, int) and it == 0:
                    pool.wait_ge(signals["act"].sem, freed(jobs["q"], 3, 1))
                    if half:
                        pool.wait_ge(cmp_ready, 2)
                    else:
                        pool.wait_ge(blk_lo_ready, 2)
                        pool.wait_ge(gemm_done, tile_done(jobs["gates"], 0, 0))
                    pool.wait_ge(w_lo_done, jobs["attn_out"].panel0)
                    if half:
                        pool.wait_ge(q_staged, half)
                else:
                    pool.wait_ge(scores_done, 12 * it - 6 * (1 - half))
                    pool.wait_ge(diag_ready, 4 * it - 2 + half)
                    if not isinstance(it, int):
                        pool.sem_inc(pool_waited, 1)
                src, n = q[rows, it, :], 3 * (2 * it + half)
                if not isinstance(it, int):
                    pool.tensor_copy(q_s[rows, :], src).then_inc(q_copied, 1)
                    src = q_s[rows, :]
                    pool.wait_ge(q_copied, 2 * (it - 1 - a) + half + 1)

                def then(k):
                    if k:
                        pool.wait_ge(q_step, n + k)
                    if not isinstance(it, int):
                        pool.sem_inc(pool_waited, 1)
                then(0)
                pool.tensor_scalar(q_hi[half][0:64, :], src, 1.0, 1.0, ALU.mult, ALU.mult).then_inc(q_step, 1)
                then(1)
                pool.tensor_scalar(q_hi[half][64:128, :], src, 1.0, 1.0, ALU.mult, ALU.mult).then_inc(q_step, 1)
                then(2)
                hi = q_hi[half][rows, :].bitcast(F32)
                pool.tensor_tensor(q_lo[half][0:64, :], src, hi, ALU.subtract).then_inc(q_step, 1)
                then(3)
                pool.tensor_tensor(q_lo[half][64:128, :], src, hi, ALU.subtract).then_inc(q_staged, 1)

            def weights(it, c, last=False):
                un = 4 * it + c
                items = 4 if c % 2 else 8
                pool.wait_ge(att_step, STEPS * (un + 1))
                if not isinstance(un, int) or un >= 2:
                    pool.wait_ge(pv_done, un - 1)
                pool.wait_ge(q_staged, 2 * it + 2 if c < 2 or last else 2 * it + 1 + c)
                d = diag[c % 2][:, 0:items, :]
                pool.tensor_tensor(d, ident.unsqueeze(1).to_broadcast([P, items, P]),
                                   mstat(3, c)[:, 0:items].unsqueeze(2).to_broadcast([P, items, P]),
                                   ALU.mult).then_inc(diag_ready, 1)

            def body(a, it):
                first = isinstance(it, int) and it == 0
                stage(a, it, 0)
                if not first:
                    weights(it - 1, 2)
                stage(a, it, 1)
                if not first:
                    weights(it - 1, 3)
                weights(it, 0)
                weights(it, 1)
            pairs(pool, body)
            weights(7, 2, last=True)
            weights(7, 3, last=True)

        def halves(t, m):
            v = t[:, :, :].rearrange("p h s -> p (h s)").rearrange("p (b a m) -> p b a m", a=2, m=m)
            return v[:, :, 0, :], v[:, :, 1, :]

        def group(t, g):
            return t[:, 2 * g:2 * g + 2, :]

        def level_mask(n):
            a, _ = CONST_COLS["level"]
            return consts[:, a + P * n:a + P * n + P].unsqueeze(1).to_broadcast([P, TT, P])

        def dve_level_mul(dve, n):
            for g in range(2):
                dve.wait_ge(level_done, 4 * n + 2 * g + 2)
                if n == 0:
                    dve.tensor_tensor(group(hq, g), group(hq, g), group(ff, g), ALU.mult).then_inc(level_mul, 1)
                    continue
                m = 1 << (n - 1)
                e1, e2 = halves(group(block_f[n - 1], g), 1)
                k1, q2 = halves(group(hk, g), m)[0], halves(group(hq, g), m)[1]
                B = k1.shape[1]
                dve.tensor_tensor(k1, k1, e2.to_broadcast([P, B, m]), ALU.mult)
                dve.tensor_tensor(q2, q2, e1.to_broadcast([P, B, m]), ALU.mult).then_inc(level_mul, 1)

        def dve_level_blocks(dve, n):
            e1, e2 = halves(block_f[n - 1], 1)
            dst = block_f[n][:, :, :].rearrange("p h s -> p (h s)").unsqueeze(2)
            dve_step(dve, dve.tensor_tensor(dst, e1, e2, ALU.mult))

        def pe_level(pe, n):
            for j in range(H2):
                if n >= 0:
                    pe.wait_ge(level_mul, 2 * n + j // 2 + 1)
                at_ = 4 * (n + 1) + j
                if at_ >= 4:
                    pe.wait_ge(level_kept, at_ - 3)
                for c in range(TT):
                    cs = slice(P * c, P * c + P)
                    mm = pe.matmul(ps[4 + j][:, cs], hk[:, j, cs], hq[:, j, cs], start=True, stop=True)
                mm.then_inc(level_done, 1)

        def dve_level_keep(dve, n):
            for j in range(H2):
                at_ = 4 * (n + 1) + j
                dve.wait_ge(level_done, at_ + 1)
                src = ps[4 + j][:, :].rearrange("p (c t) -> p c t", t=P)
                dst = aT[:, j, :].rearrange("p (c t) -> p c t", t=P)
                if n < 0:
                    ins = dve.tensor_tensor(dst, src, level_mask(0), ALU.mult)
                else:
                    dve.wait_ge(level_kept, at_ - 3)
                    ins = dve.copy_predicated(dst, level_mask(n + 1).bitcast(I32), src)
                ins.then_inc(level_kept, 1)

        def dve_recurrence_inputs(dve):
            l0, l1 = (gains[:, GAIN_ROWS["lb"] + 4 * n:GAIN_ROWS["lb"] + 4 * n + 4] for n in range(2))
            top, e, total, lb, rest = (lbv[:, a:b] for a, b in ((0, 4), (4, 12), (12, 16), (16, 20), (20, 24)))
            dve_step(dve, dve.tensor_tensor(top, l0, l1, ALU.max))
            dve.tensor_tensor(e[:, 0:4], l0, top, ALU.subtract).then_inc(lb_exp, 1)
            dve.tensor_tensor(e[:, 4:8], l1, top, ALU.subtract).then_inc(lb_exp, 1)
            dve.wait_ge(lb_exp, 3)
            dve_step(dve, dve.tensor_tensor(total, e[:, 0:4], e[:, 4:8], ALU.add))
            dve_step(dve, dve.reciprocal(rest, total))
            dve_step(dve, dve.tensor_tensor(lb, rest, e[:, 0:4], ALU.mult))
            dve_step(dve, dve.tensor_scalar(rest, lb, -1.0, 1.0, ALU.mult, ALU.add))
            for t in range(H2):
                dve.wait_ge(signals["act"].sem, freed(jobs["f"], t, 0))
                dve_step(dve, dve.tensor_scalar(ff[:, t, :], ff[:, t, :], rest[:, t:t + 1], lb[:, t:t + 1],
                                                ALU.mult, ALU.add))
                dve_step(dve, dve.tensor_scalar(hk[:, t, :], ff[:, t, :], -1.0, 1.0, ALU.mult, ALU.add))
            dve_step(dve, dve.tensor_scalar(ff[:], ff[:], 1.0, None, ALU.min))
            dve.wait_ge(signals["act"].sem, freed(jobs["hq"], 3, 0))
            dve.tensor_scalar(hq[:], hq[:], P ** -0.5, None, ALU.mult).then_inc(hq_ready, 1)

        def dve_levels(dve):
            dve_level_mul(dve, 0)
            dve_level_blocks(dve, 1)
            dve_level_keep(dve, -1)
            for n in range(1, LEVELS + 1):
                dve_level_mul(dve, n)
                if n < LEVELS:
                    dve_level_blocks(dve, n + 1)
                dve_level_keep(dve, n - 1)
            decay_ = block_f[LEVELS][:, :, :].rearrange("p h c -> p (h c)")
            dve_step(dve, dve.tensor_copy(small[:, 0:16], decay_))

        HEADS = [slice(P * j, P * j + P) for j in range(H2)]

        def pe_turn_keys(pe):
            pe.wait_ge(level_mul, 2 * (LEVELS + 1))
            pe.wait_ge(rstd_ready, norms["mem_k3"]["n"] + 1)
            pe.wait_ge(level_kept, 4 * (LEVELS + 1))
            for c in range(3):
                for j in range(H2):
                    mm = pe.transpose(ps[4 + c][:, P * j:P * j + P], hk[:, j, P * c:P * c + P], ident)
                mm.then_inc(k_turned, 1)

        def pe_chunk(pe, c):
            if c == 0:
                pe.wait_ge(signals["act"].sem, freed(jobs["i"], 3, 0))
            if c < 3:
                pe.wait_ge(k_rows_ready, 3)
                if c == 2:
                    pe.wait_ge(state_ready, 1)
                for j in range(H2):
                    mm = pe.matmul(ps[4 + c % 2][:, HEADS[j]], k_rows[:, c, HEADS[j]], hv[:, c, HEADS[j]],
                                   start=True, stop=True)
                mm.then_inc(chunk_done, 1)
            if c:
                pe.wait_ge(state_ready, c)
            if c >= 2:
                pe.wait_ge(chunk_out, c - 1)
            for j in range(H2):
                cs = slice(P * c, P * c + P)
                o = ps[6 + c % 2][:, HEADS[j]]
                mm = pe.matmul(o, aT[:, j, cs], hv[:, c, HEADS[j]], start=True, stop=c == 0)
                if c:
                    mm = pe.matmul(o, hq[:, j, cs], state[:, j, :], start=False, stop=True)
            mm.then_inc(chunk_done, 1)

        def act_turned_keys(act):
            for c in range(3):
                act.wait_ge(k_turned, c + 1)
                act.activation(k_rows[:, c, :], ps[4 + c][:, :], ACT.Copy).then_inc(k_rows_ready, 1)

        def act_chunk(act, c):
            act.wait_ge(chunk_done, min(2 * c + 2, 7))
            src = ps[6 + c % 2]
            for j in range(H2):
                act.activation(squares[0][:, c, HEADS[j]], src[:, HEADS[j]], ACT.Square,
                               accum_out=ssq[:, 4 * c + j:4 * c + j + 1])
            act.activation(o_rows[:, c, :], src[:, :], ACT.Copy).then_inc(chunk_out, 1)

        def dve_chunk(dve, c):
            new = ps[4 + c % 2]
            dve.wait_ge(chunk_done, 2 * c + 1 if c == 0 else 2 * c + 2)
            if c == 0:
                dve.tensor_copy(state[:].rearrange("p h e -> p (h e)"), new[:, :]).then_inc(state_ready, 1)
                return
            dve.wait_ge(state_ready, c)
            for j in range(H2):
                ins = dve.scalar_tensor_tensor(state[:, j, :], state[:, j, :], decay[:, j, c:c + 1],
                                               new[:, P * j:P * j + P], ALU.mult, ALU.add)
            ins.then_inc(state_ready, 1)

        FIN = [dict(y=o_rows, parts=16, width=P, gain="hg_out", out=(hgm_hi, hgm_lo), split=SPLIT["hgm"]),
               dict(y=y_mem, parts=4, width=W2, gain="mem_out", out=(memm_hi, memm_lo), split=SPLIT["memm"]),
               dict(y=y_mla, parts=4, width=W2, gain="mla_out", out=(mlam_hi, mlam_lo), split=SPLIT["mlam"])]
        FIN[0]["bank"], FIN[1]["bank"], FIN[2]["bank"] = 3, 3, 6

        def act_rows(act, n):
            f = FIN[n]
            act.wait_ge(*f["ready"])
            if n:
                act.wait_ge(rows_ready, 4 * n)
            if n:
                for k in range(f["parts"]):
                    ins = act.activation(squares[n][:, k, :], f["y"][:, k, :], ACT.Square, accum_out=ssq[:, k:k + 1])
                ins.then_inc(rows_sq, 1)
                act.wait_ge(rows_sq, n)
            act.activation(rroot[:, 0:f["parts"]], ssq[:, 0:f["parts"]], ACT.Ln, scale=1.0 / f["width"],
                           bias=const("eps")).then_inc(rows_root, 1)
            act.wait_ge(rows_root, 2 * n + 1)
            act.activation(rinv[:, 0:f["parts"]], rroot[:, 0:f["parts"]], ACT.Exp, scale=-0.5).then_inc(rows_root, 1)

        def dve_rows(dve, n):
            f = FIN[n]
            dve.wait_ge(rows_root, 2 * n + 2)
            for i in range(TT):
                y = f["y"][:, i, :]
                if n == 0:
                    v_ = y.rearrange("p (h e) -> p h e", e=P)
                    ins = dve.tensor_tensor(v_, v_, rinv[:, 4 * i:4 * i + 4].unsqueeze(2).to_broadcast([P, H2, P]), ALU.mult)
                else:
                    ins = dve.tensor_scalar(y, y, rinv[:, i:i + 1], None, ALU.mult)
                ins.then_inc(rows_ready, 1)

        def pe_row(pe, n, j):
            f = FIN[n]
            if j == 0:
                pe.wait_ge(rows_ready, 4 * n + 4)
            else:
                pe.wait_ge(val_ready, f["split"] + j)
            for i in range(TT):
                mm = pe.transpose(ps[f["bank"]][:, P * i:P * i + P], f["y"][:, i, P * j:P * j + P], ident)
            mm.then_inc(rows_turned, 1)

        def dve_row_out(dve, n, j):
            f = FIN[n]
            k = f["split"] + j
            dve.wait_ge(rows_turned, 4 * n + j + 1)
            val_free(dve, k)
            if n == 0:
                dve.wait_ge(sg_ready, 1)
                ins = dve.scalar_tensor_tensor(val[k % 2][:, :], ps[f["bank"]][:, :], gain(f["gain"], j), sg[:, j, :],
                                               ALU.mult, ALU.mult)
            else:
                ins = dve.tensor_scalar(val[k % 2][:, :], ps[f["bank"]][:, :], gain(f["gain"], j), None, ALU.mult)
            ins.then_inc(val_ready, 1)

        def dve_row_lo(dve, n, j):
            f = FIN[n]
            k = f["split"] + j
            dve_lo(dve, k, f["out"][1][:, j, :], f["out"][0][:, j, :], slot=k % 2)

        def act_row_out(act, n, j):
            f = FIN[n]
            act_hi(act, f["split"] + j, f["out"][0][:, j, :], slot=(f["split"] + j) % 2)

        MAGIC = 1.5 * 2.0 ** 23
        TURN1, TURN2, TURN3 = 6.28125, 0.0019354820251464844, -1.7484556025237907e-07

        def dve_angles(dve, n):
            if n == 0:
                dve.wait_ge(pos_loaded, 16)
                dve_step(dve, dve.tensor_copy(rb[:], pos_i[:]))
                dve_step(dve, dve.tensor_scalar(rb[:], rb[:], const("freq"), None, ALU.mult))
            dst, shift, quarter = ((sin, 0.0, 0.0), (cos, 0.25, float(np.pi / 2)))[n]
            dve_step(dve, dve.tensor_scalar(ra[:], rb[:], float(1 / (2 * np.pi)), shift, ALU.mult, ALU.add))
            dve_step(dve, dve.tensor_scalar(ra[:], ra[:], MAGIC, None, ALU.add))
            dve_step(dve, dve.tensor_scalar(ra[:], ra[:], MAGIC, None, ALU.subtract))
            dve_step(dve, dve.scalar_tensor_tensor(dst[:], ra[:], -TURN1, rb[:], ALU.mult, ALU.add))
            dve_step(dve, dve.scalar_tensor_tensor(dst[:], ra[:], -TURN2, dst[:], ALU.mult, ALU.add))
            dve_step(dve, dve.scalar_tensor_tensor(dst[:], ra[:], -TURN3, dst[:], ALU.mult, ALU.add))
            dve_step(dve, dve.tensor_scalar(dst[:], dst[:], quarter, 3.1415925, ALU.add, ALU.min))
            dve.tensor_scalar(dst[:], dst[:], -3.1415925, None, ALU.max).then_inc(angle_ready, 1)

        def act_angles(act):
            for n, dst in enumerate((sin, cos)):
                act.wait_ge(angle_ready, n + 1)
                act.activation(dst[:], dst[:], ACT.Sin).then_inc(angle_sin, 1)

        ROT = [krb[:, :], qr[:, 0, :], qr[:, 1, :]]

        def pe_rope(pe, n):
            if n == 0:
                pe.wait_ge(rope_ready, 1)
            else:
                pe.wait_ge(part_ready, part_done(f"q{2 * n - 1}"))
                pe.wait_ge(rope_ready, n + 1)
            pe.matmul(ps[6][:, :], const("rot"), ROT[n], start=True, stop=True).then_inc(rot_done, 1)

        def dve_rope(dve, n):
            x = ROT[n]
            if n == 0:
                dve.tensor_scalar(krb[:], kr[:], gain("mla_k", 1), None, ALU.mult).then_inc(rope_ready, 1)
                dve.wait_ge(angle_sin, 2)
            dve.wait_ge(rot_done, n + 1)
            dve_step(dve, dve.tensor_tensor(ra[:], x, cos[:], ALU.mult))
            dve_step(dve, dve.tensor_tensor(rb[:], ps[6][:, :], sin[:], ALU.mult))
            dve.tensor_tensor(x, ra[:], rb[:], ALU.add).then_inc(rope_ready, 1)
            if n == 0:
                dve.wait_ge(rope_ready, 2)

        def part_done(name):
            return norm_done(norms[name])[1]

        CAUSAL_PACK = [[(3, 0, 512)], [(2, 0, 384), (0, 384, 128)], [(1, 0, 256)]]
        MEM_PACK = [[(3, 0, 256), (2, 256, 256)], [(1, 0, 256), (0, 256, 256)]]
        units2 = []
        n_score = n_turn = 0
        for n in range(2 * H2):
            mla, j = n >= H2, n % H2
            pack = CAUSAL_PACK if mla else MEM_PACK
            units2.append(dict(n=n, mla=mla, head=j, pack=pack, score0=n_score, turn0=n_turn,
                               off=POFF if mla else {i: 256 * i for i in range(4)},
                               scale=(QKH if mla else P) ** -0.5))
            n_score += len(pack)
            n_turn += len(pack)

        def taken_of(k):
            return (pT2_act if k % 2 == 0 else pT2_dve), k // 2 + 1

        def pe_qk2(pe, w):
            j = w["head"]
            if w["n"] == 0:
                pe.wait_ge(signals["act"].sem, freed(jobs["g"], 3, 0))
                pe.wait_ge(part_ready, part_done("mem_q3"))
            if w["n"] == H2:
                pe.wait_ge(part_ready, part_done("k3"))
                pe.wait_ge(rope_ready, 4)
            for b, items in enumerate(w["pack"]):
                k = w["score0"] + b
                if k >= 3:
                    pe.wait_ge(taken2, k - 2)
                for i, off, width in items:
                    o = ps[k % 3][:, off:off + width]
                    ts = slice(P * i, P * i + P)
                    if w["mla"]:
                        r = slice(ROPE * (j % 2), ROPE * (j % 2) + ROPE)
                        pe.matmul(o, qn[:, j, ts], kn[:, j, 0:width], start=True, stop=False)
                        mm = pe.matmul(o, qr[r, j // 2, ts], krh[r, j // 2, 0:width], start=False, stop=True)
                    else:
                        mm = pe.matmul(o, mq[:, j, ts], mem_k[:, j, 0:width], start=True, stop=True)
                mm.then_inc(scores2, 1)

        def item2(w, i, width):
            return prob2[w["n"] % 3][:, w["off"][i]:w["off"][i] + width]

        def dve_max2(dve, w):
            n = w["n"]
            if n >= 3:
                dve.wait_ge(pv2, n - 2)
            for b, items in enumerate(w["pack"]):
                k = w["score0"] + b
                dve.wait_ge(scores2, k + 1)
                for i, off, width in items:
                    a_, _ = CONST_COLS["causal"]
                    mask = mask_of(width) if w["mla"] else consts[:, a_:a_ + width]
                    ins = dve.tensor_tensor_reduce(out=item2(w, i, width), in0=ps[k % 3][:, off:off + width], in1=mask,
                                                   scale=1.0, scalar=NEG, op0=ALU.add, op1=ALU.max,
                                                   accum_out=mstat(0, n % 4)[:, i:i + 1])
                ins.then_inc(taken2, 1)
            dve.wait_ge(taken2, w["score0"] + len(w["pack"]))
            dve.tensor_scalar(mstat(1, n % 4)[:, 0:TT], mstat(0, n % 4)[:, 0:TT], FLOOR, -w["scale"],
                              ALU.max, ALU.mult).then_inc(negm2, 1)

        def act_exps2(act, w):
            n = w["n"]
            act.wait_ge(negm2, n + 1)
            for items in w["pack"]:
                for i, _, width in items:
                    x = item2(w, i, width)
                    ins = act.activation(x, x, ACT.Exp, bias=mstat(1, n % 4)[:, i:i + 1], scale=w["scale"],
                                         accum_out=mstat(2, n % 4)[:, i:i + 1])
            ins.then_inc(exp2, 1)

        def pe_tpv2(pe, w):
            n, j = w["n"], w["head"]
            pe.wait_ge(exp2, n + 1)
            rows = v2 if w["mla"] else mem_v

            def turn2(b):
                k = w["turn0"] + b
                if k >= 2:
                    pe.wait_ge(*taken_of(k - 2))
                for i, off, width in w["pack"][b]:
                    for kt in range(width // P):
                        mm = pe.transpose(ps[4 + k % 2][:, off + P * kt:off + P * kt + P],
                                          item2(w, i, width)[:, P * kt:P * kt + P], ident)
                mm.then_inc(turned2, 1)

            def product2(b):
                pe.wait_ge(*taken_of(w["turn0"] + b))
                for i, off, width in w["pack"][b]:
                    for kt in range(width // P):
                        mm = pe.matmul(ps[6 + n % 2][:, P * i:P * i + P],
                                       pT2[n % 2][b][:, off + P * kt:off + P * kt + P],
                                       rows[:, kt, P * j:P * j + P], start=kt == 0, stop=kt == width // P - 1)
                return mm

            if n == 0:
                pe.wait_ge(rstd_ready, norms["k3"]["n"] + 1)
                pe.wait_ge(rope_ready, 4)
            turn2(0)
            if n >= 2:
                pe.wait_ge(y_ready, n - 1)
            for b in range(1, len(w["pack"])):
                turn2(b)
                product2(b - 1)
            product2(len(w["pack"]) - 1).then_inc(pv2, 1)

        def take2(eng, which, w):
            n = w["n"]
            if n >= 2:
                eng.wait_ge(pv2, n - 1)
            elif n == 0:
                eng.wait_ge(gemm_done, tile_done(jobs["g"], 3, 0))
            for b in range(len(w["pack"])):
                k = w["turn0"] + b
                if k % 2 != (which == "dve"):
                    continue
                eng.wait_ge(turned2, k + 1)
                width = 256 if w["mla"] and b == 2 else 512
                dst, src = pT2[n % 2][b][:, 0:width], ps[4 + k % 2][:, 0:width]
                if which == "act":
                    eng.activation(dst, src, ACT.Copy).then_inc(pT2_act, 1)
                else:
                    eng.tensor_copy(dst, src).then_inc(pT2_dve, 1)

        def dve_combine2(dve, w):
            n, j = w["n"], w["head"]
            dve.wait_ge(exp2, n + 1)
            r = mstat(3, n % 4)[:, 0:TT]
            dve_step(dve, dve.reciprocal(r, mstat(2, n % 4)[:, 0:TT]))
            dve.wait_ge(pv2, n + 1)
            y = y_mla if w["mla"] else y_mem
            dve.tensor_tensor(y[:, :, P * j:P * j + P], ps[6 + n % 2][:, :].rearrange("p (i e) -> p i e", e=P),
                              r.unsqueeze(2).to_broadcast([P, TT, P]), ALU.mult).then_inc(y_ready, 1)

        def pe_attention2(pe):
            for w in units2:
                n = w["n"]
                pe_qk2(pe, w)
                if n < 2:
                    pe_row(pe, 0, n)
                if n == 2:
                    pe_row(pe, 0, 2)
                    pe_row(pe, 0, 3)
                if n == 7:
                    pe_row(pe, 1, 0)
                if n >= 2:
                    pe_tpv2(pe, units2[n - 2])
            pe_row(pe, 1, 1)
            pe_tpv2(pe, units2[6])
            pe_row(pe, 1, 2)
            pe_tpv2(pe, units2[7])
            pe_row(pe, 1, 3)

        def act_attention2(act):
            for w in units2:
                n = w["n"]
                if n >= 2:
                    take2(act, "act", units2[n - 2])
                if n == 7:
                    act_row_out(act, 1, 0)
                act_exps2(act, w)
                if n < 2:
                    act_row_out(act, 0, n)
                if n == 1:
                    act_row_out(act, 0, 2)
                if n == 2:
                    act_row_out(act, 0, 3)
                if n == 5:
                    act_rows(act, 1)
            take2(act, "act", units2[6])
            act_row_out(act, 1, 1)
            take2(act, "act", units2[7])
            act_row_out(act, 1, 2)
            act_rows(act, 2)
            act_row_out(act, 1, 3)
            for j in range(4):
                act_row_out(act, 2, j)

        def dve_attention2(dve):
            for w in units2:
                n = w["n"]
                dve_max2(dve, w)
                if n < 2:
                    dve_row_out(dve, 0, n)
                if n == 2:
                    for j in (0, 1):
                        dve_row_lo(dve, 0, j)
                    for j in (2, 3):
                        dve_row_out(dve, 0, j)
                if n == 3:
                    for j in (2, 3):
                        dve_row_lo(dve, 0, j)
                if n == 6:
                    dve_rows(dve, 1)
                if n == 7:
                    dve_row_out(dve, 1, 0)
                if n >= 2:
                    take2(dve, "dve", units2[n - 2])
                    dve_combine2(dve, units2[n - 2])
            dve_row_out(dve, 1, 1)
            dve_row_lo(dve, 1, 0)
            take2(dve, "dve", units2[6])
            dve_combine2(dve, units2[6])
            dve_row_out(dve, 1, 2)
            dve_row_lo(dve, 1, 1)
            take2(dve, "dve", units2[7])
            dve_combine2(dve, units2[7])
            dve_row_out(dve, 1, 3)
            dve_row_lo(dve, 1, 2)
            dve_row_lo(dve, 1, 3)
            dve_rows(dve, 2)
            for j in range(4):
                dve_row_out(dve, 2, j)
                if j:
                    dve_row_lo(dve, 2, j - 1)
            dve_row_lo(dve, 2, 3)

        FIN[0]["ready"] = (chunk_out, 4)
        FIN[1]["ready"] = (y_ready, H2)
        FIN[2]["ready"] = (y_ready, 2 * H2)

        def act_hi_from(act, n, dst, src):
            act.activation(dst, src, ACT.Copy).then_inc(hi_ready, 1)

        def act_mlp(act, name, norm):
            act_norm(act, norm)
            act.preload_act_table_set("silu_and_others")
            job = jobs[name]

            def silus(i):
                for t in range(2):
                    n = job.split0 + 2 * i + t
                    act.wait_ge(val_ready, n - 1)
                    act.wait_ge(gemm_done, tile_done(job, t, i))
                    act.activation(silu[:, t, :], ps[t][:, :], ACT.Silu).then_inc(signals["act"].sem, 1)
                for t in range(2):
                    n = job.split0 + 2 * i + t
                    act_hi(act, n, hid_hi[:, 2 * i + t, :], slot=(job.split0 + t) % 2)
            over_blocks(act, job, silus)

        def i_is(i, n):
            return isinstance(i, int) and i == n

        def dve_mlp(dve, name, down, norm, first_block=None):
            dve_norm(dve, norm)
            job = jobs[name]

            def products(i):
                for t in range(2):
                    dve.wait_ge(signals["act"].sem, freed(job, t, i))
                    dve.wait_ge(gemm_done, tile_done(job, t + 2, i))
                    val_free(dve, job.split0 + 2 * i + t)
                    dve.tensor_tensor(val[(job.split0 + t) % 2][:, :], ps[t + 2][:, :], silu[:, t, :],
                                      ALU.mult).then_inc(val_ready, 1)
                for t in range(2):
                    n = job.split0 + 2 * i + t
                    dve_lo(dve, n, hid_lo[:, 2 * i + t, :], hid_hi[:, 2 * i + t, :], slot=(job.split0 + t) % 2)
            over_blocks(dve, job, products)
            job = jobs[down]

            def adds(i):
                for t in range(2):
                    dve.wait_ge(gemm_done, tile_done(job, t, i))
                    dve.tensor_tensor(h[:, 2 * i + t, :], ps[t][:, :], h[:, 2 * i + t, :],
                                      ALU.add).then_inc(signals["dve"].sem, 1)
                    if first_block and i_is(i, 0):
                        if t == 0:
                            first_block()
                    elif first_block and i_is(i, 1) and t == 0:
                        dve_sums(dve, 1, first=True)
                    elif first_block:
                        dve_sums(dve, 2 * i + t - 1)
            if first_block:
                adds(0)
                adds(1)
                with dve.Fori(2, job.blocks) as i:
                    adds(i)
            else:
                over_blocks(dve, job, adds)

        def act_take(act, name, dsts, func=ACT.Copy, then={}):
            job = jobs[name]
            for t, dst in enumerate(dsts):
                act.wait_ge(gemm_done, tile_done(job, t, 0))
                act.activation(dst, ps[job.banks[t]][:, 0:dst.shape[-1]], func).then_inc(signals["act"].sem, 1)
                if t in then:
                    then[t]()

        OUT = out[0].rearrange("(t p) d -> p t d", p=P)

        def out_bank(t, half):
            return (2 * t + half + 2) % 8

        def k_cols(t):
            a = K_AT[t] + (NCMP_EVEN if t < 2 else 0)
            return slice(a, a + S)

        block = ctx.enter_context(nc.Block())
        SET1 = ["conv_in", "gate_attn", "conv_out", "gate_conv", "q", "kv_cmp", "k", "v", "gates", "cmp_k", "cmp_v"]

        @block.sync
        def _(sp):
            for job in order:
                sp_job(sp, job.name)
            for t in range(TT):
                sp.wait_ge(out_act, t + 1)
                sp.wait_ge(out_dve, t + 1)
                sp.dma_start(OUT[:, t, :], out_rows[:, t, :]).then_inc(out_sent, 16)
            sp.wait_ge(out_sent, 16 * TT)

        @block.gpsimd
        def _(pool):
            for name in SET1:
                pool_job(pool, name)
            pool_attention(pool)
            for job in order[len(SET1):]:
                pool_job(pool, job.name)

        @block.scalar
        def _(act):
            masks = CONST_COLS["causal"][0]
            act.dma_start(consts[:, 0:masks], A["consts"][:, 0:masks]).then_inc(consts_loaded, 16)
            act.dma_start(x_rows[:], A["x"][0].rearrange("(t p) d -> p t d", p=P)).then_inc(x_loaded, 16)
            for name, key in (("g_mix", "g_mix"), ("g_ffn", "g_ffn"), ("g_final", "g_final")):
                r = GAIN_ROWS[name]
                src = A[key] if key == "g_final" else A[key][0]
                act.dma_start(gain_rows[r:r + 8, :], src.rearrange("(c p) -> c p", p=P)).then_inc(gains_loaded, 16)
            n_rows = 3
            for name, key in (("norm_mix", "norm_mix_2"), ("norm_mem", "norm_mem_2"), ("q_a", "q_a_norm_2"),
                              ("kv_a", "kv_a_norm_2"), ("hg_out", "hg_out_norm_2"), ("mem_q", "mem_q_norm_2"),
                              ("mem_k", "mem_k_norm_2"), ("mla_out", "mla_out_norm_2"),
                              ("mem_out", "mem_out_norm_2"), ("norm_ffn", "norm_ffn_2")):
                r = GAIN_ROWS[name]
                src = A[key][0].rearrange("(c p) -> c p", p=P)
                act.dma_start(gain_rows[r:r + src.shape[0], :], src).then_inc(gains_loaded, 16)
                n_rows += 1
            for name, key in (("mla_q", "mla_q_norm_2"), ("mla_k", "mla_k_norm_2")):
                r = GAIN_ROWS[name]
                src = A[key]
                act.dma_start(gain_rows[r:r + 1, :], src[:, 0:NOPE]).then_inc(gains_loaded, 16)
                for half in range(2):
                    act.dma_start(gain_rows[r + 1:r + 2, ROPE * half:ROPE * half + ROPE],
                                  src[:, NOPE:QKH]).then_inc(gains_loaded, 16)
                n_rows += 3
            r = GAIN_ROWS["conv_w"]
            act.dma_start(gain_rows[r:r + 12, :], A["conv_w"][0].rearrange("k (c p) -> (k c) p", p=P)).then_inc(gains_loaded, 16)
            r = GAIN_ROWS["lb"]
            act.dma_start(gain_rows[r:r + 8, :], A["hg_lb_logits_2"].rearrange("k (c p) -> (k c) p", p=P)).then_inc(gains_loaded, 16)
            for name, key in (("pos_k", "cmp_pos_k"), ("pos_v", "cmp_pos_v")):
                r = GAIN_ROWS[name]
                act.dma_start(gain_rows[r:r + NPAIR, :], A[key][0].rearrange("(j e) d -> j (e d)", e=2)).then_inc(gains_loaded, 16)
            n_rows += 4
            assert n_rows == 23
            act.dma_start(consts[:, masks:NCONST], A["consts"][:, masks:NCONST]).then_inc(masks_loaded, 16)
            for half in range(2):
                act.dma_start(w2k[:, :, HD * half:HD * half + HD],
                              A["cmp_w2_k"][0].rearrange("(t p) d -> p t d", p=P)).then_inc(w2_loaded, 16)
            act.dma_start(w2v[:], A["cmp_w2_v"][0].rearrange("(t p) d -> p t d", p=P)).then_inc(w2_loaded, 16)

            norm_table(act)
            act.wait_ge(consts_loaded, 16)
            act_norm(act, "mix")

            job = jobs["conv_in"]
            def copies(i):
                for t in range(4):
                    act.wait_ge(gemm_done, tile_done(job, t, i))
                    act.activation(bch[:, 4 * i + t, :], ps[t][:, :], ACT.Copy).then_inc(signals["act"].sem, 1)
            over_blocks(act, job, copies)

            job = jobs["gate_attn"]
            for i in range(2):
                for t in range(4):
                    act.wait_ge(gemm_done, tile_done(job, t, i))
                    act.activation(g_attn[:, 4 * i + t, :], ps[t][:, :], ACT.Sigmoid).then_inc(signals["act"].sem, 1)
                if i == 0:
                    for c in range(4):
                        n = SPLIT["conv"] + c
                        act_hi(act, n, cv_hi[:, c, :], slot=n % 2)

            job = jobs["gate_conv"]
            for i in range(2):
                for t in range(4):
                    n = 4 * i + t
                    if n >= 2:
                        act.wait_ge(mixc_ready, n - 1)
                    act.wait_ge(gemm_done, tile_done(job, t, i))
                    act.activation(sig[:, n % 2, :], ps[t][:, :], ACT.Sigmoid).then_inc(signals["act"].sem, 1)

            job = jobs["q"]
            for i in range(2):
                for t in range(4):
                    act.wait_ge(gemm_done, tile_done(job, t, i))
                    act.activation(q[:, 4 * i + t, :], ps[t][:, :], ACT.Copy).then_inc(signals["act"].sem, 1)
            act.wait_ge(signals["dve"].sem, freed(jobs["kv_cmp"], 1, 0))
            act.activation(blk_hi[0][:], blk[0][:].rearrange("p j h n -> p j (h n)"), ACT.Copy).then_inc(blk_hi_ready, 1)
            act.wait_ge(blk_lo_ready, 1)
            job = jobs["k"]
            for t in range(4):
                act.wait_ge(gemm_done, tile_done(job, t, 0))
                first, second = (x[:, k_cols(t)] for x in k_pairs)
                act.activation(first[0:64, :], ps[t][0:64, :], ACT.Copy)
                act.activation(second[64:128, :], ps[t][64:128, :], ACT.Copy).then_inc(k_hi_ready, 1)
            job = jobs["v"]
            for t in range(4):
                act.wait_ge(gemm_done, tile_done(job, t, 0))
                act.activation(v_rows[:, t, :], ps[t][:, :], ACT.Copy).then_inc(signals["act"].sem, 1)
            act.wait_ge(gemm_done, tile_done(jobs["gates"], 0, 0))
            act.activation(gatesT[0:3 * NH, :], ps[0][0:3 * NH, :], ACT.Sigmoid).then_inc(signals["act"].sem, 1)
            act.activation(blk_hi[1][:], blk[1][:].rearrange("p j h n -> p j (h n)"), ACT.Copy).then_inc(blk_hi_ready, 1)
            for n, name in enumerate(("cmp_k", "cmp_v")):
                rows = slice(0, NKV * NCMP)
                act.wait_ge(gemm_done, tile_done(jobs[name], 0, 0))
                act.activation(hidT_cmp[n][rows, :], ps[jobs[name].banks[0]][rows, 0:CMP_HID],
                               ACT.Gelu_apprx_tanh).then_inc(signals["act"].sem, 1)

            norm_table(act)
            act_attention(act)
            for c in range(KC):
                n = SPLIT["o"] + c
                if c == 0:
                    act.wait_ge(val_ready, SPLIT["o"] + 8)
                act_hi_from(act, n, o_hi[:, c, :], oT[:, c, :])
            for c in range(KC):
                n = jobs["attn_out"].split0 + c
                act_hi(act, n, mix_hi[:, c, :], slot=n % 2)
            act_mlp(act, "up", "ffn")

            act.wait_ge(gemm_done, tile_done(jobs["up"], 3, 10))
            act.dma_start(mem_rows[:], A["mem_2"][0].rearrange("(t p) d -> p t d", p=P)).then_inc(mem_loaded, 16)
            norm_table(act)
            act_norm(act, "mem")
            act_norms(act)
            act.wait_ge(lb_exp, 2)
            act.activation(lbv[:, 4:12], lbv[:, 4:12], ACT.Exp).then_inc(lb_exp, 1)
            act_take(act, "f", [ff[:, t, :] for t in range(H2)], ACT.Sigmoid)
            act_take(act, "hq", [hq[:, t, :] for t in range(H2)], ACT.Silu)
            norm_table(act)
            act_take(act, "lat_a", [cq[:, 0, :], cq[:, 1, :], cq[:, 2, :], ckv[:, 0, :]])
            act_take(act, "lat_b", [ckv[:, 1, :], kr[:, :]])
            act_take(act, "mq", [mq[:, t, :] for t in range(H2)])
            act_norms_in_turn(act, ["cq", "ckv"] + [f"mem_k{n}" for n in range(H2)])
            act.wait_ge(*norm_done(norms["ckv"]))
            act.dma_start(pos_i[:], A["positions_2"][0:1, :].to_broadcast([P, S])).then_inc(pos_loaded, 16)
            act_take(act, "i", [hv[:, t, :] for t in range(TT)])
            act_turned_keys(act)
            for c in range(TT):
                act_chunk(act, c)
            act_rows(act, 0)
            act_squares(act, "mem_q0")
            act_take(act, "uq_nope", [qn[:, t, :] for t in range(H2)],
                     then={0: lambda: act_factor(act, "mem_q0"), 1: lambda: act_squares(act, "mem_q1"),
                           2: lambda: act_factor(act, "mem_q1"), 3: lambda: act_squares(act, "mem_q2")})
            act_take(act, "uq_rope", [qr[:, t, :] for t in range(2)],
                     then={0: lambda: act_factor(act, "mem_q2"), 1: lambda: act_squares(act, "mem_q3")})
            act_take(act, "ukv_k", [kn[:, t, :] for t in range(H2)], then={0: lambda: act_factor(act, "mem_q3")})
            act_take(act, "ukv_v", [v2[:, t, :] for t in range(TT)])
            act_angles(act)
            norm_table(act)

            def take_gate(n):
                if n >= H2:
                    t = n - H2
                    act.wait_ge(gemm_done, tile_done(jobs["g"], t, 0))
                    act.activation(sg[:, t, :], ps[t][:, :], ACT.Copy).then_inc(signals["act"].sem, 1)
            act_norms_in_turn(act, [f"{x}{n}" for x in "qk" for n in range(H2)], take_gate)
            act.wait_ge(signals["act"].sem, freed(jobs["g"], 3, 0))
            act.activation(sg[:], sg[:], ACT.Silu).then_inc(sg_ready, 1)
            norm_table(act)
            act_attention2(act)
            act_mlp(act, "up_2", "ffn_2")
            for t in range(TT):
                act.wait_ge(out_turned, 2 * t + 1)
                act.activation(out_rows[:, t, 0:S], ps[out_bank(t, 0)][:, :], ACT.Copy).then_inc(out_act, 1)

        @block.vector
        def _(dve):
            for c in range(KC):
                dve.wait_ge(xT_done, c + 1)
                dve.tensor_copy(h[:, c, :], ps[c % 4][:, :]).then_inc(h_ready, 1)
            dve.wait_ge(gainsT_done, 1)
            dve.tensor_copy(gains[:, 0:NGAIN], ps[5][:, 0:NGAIN]).then_inc(gains_ready, 1)
            dve.memset(u[:, :, 0:2], 0.0).then_inc(step.sem, 1)
            step.reserve(1)
            dve.wait_ge(gains_ready, 1)
            dve_norm(dve, "mix")

            job = jobs["conv_in"]
            for t in range(4):
                dve.wait_ge(signals["act"].sem, freed(job, t, 2))
                dve_step(dve, dve.tensor_tensor(u[:, t, 2:S + 2], bch[:, 4 + t, :], bch[:, 8 + t, :], ALU.mult))
            for t in range(4):
                n = SPLIT["conv"] + t
                val_free(dve, n)
                z = val[n % 2][:, :]
                dve_step(dve, dve.tensor_scalar(z, u[:, t, 0:S], gain("conv_w", t), None, ALU.mult))
                for k in (1, 2):
                    dve_step(dve, dve.scalar_tensor_tensor(z, u[:, t, k:k + S], gain("conv_w", 4 * k + t), z,
                                                           ALU.mult, ALU.add))
                dve.tensor_tensor(z, z, bch[:, t, :], ALU.mult).then_inc(val_ready, 1)
                if t:
                    dve_lo(dve, n - 1, cv_lo[:, t - 1, :], cv_hi[:, t - 1, :], slot=(n - 1) % 2)
            dve_lo(dve, n, cv_lo[:, 3, :], cv_hi[:, 3, :], slot=n % 2)

            job = jobs["conv_out"]
            for i in range(2):
                for t in range(4):
                    dve.wait_ge(gemm_done, tile_done(job, t, i))
                    dve.tensor_copy(mixc[:, 4 * i + t, :], ps[t][:, :]).then_inc(signals["dve"].sem, 1)
            job = jobs["gate_conv"]
            for i in range(2):
                for t in range(4):
                    n = 4 * i + t
                    dve.wait_ge(signals["act"].sem, freed(job, t, i))
                    dve.tensor_tensor(mixc[:, n, :], mixc[:, n, :], sig[:, n % 2, :], ALU.mult).then_inc(mixc_ready, 1)

            job = jobs["kv_cmp"]
            dve.wait_ge(mixc_ready, 8)
            for t in range(4):
                dve.wait_ge(gemm_done, tile_done(job, t, 0))
                kv = t // 2
                pos = GAIN_ROWS["pos_v" if kv else "pos_k"]
                for half in range(2):
                    head = 2 * (t % 2) + half
                    rows = ps[t][64 * half:64 * half + 64, :].rearrange("p (n l) -> p l n", l=CMP_STRIDE)
                    for e in range(2):
                        for jj in range(2):
                            src = rows[:, e:CMP_STRIDE:2, jj:jj + NCMP]
                            dst = blk[kv][64 * e:64 * e + 64, 8 * jj:8 * jj + 8, head, :]
                            add = gains[64 * e:64 * e + 64, pos + 8 * jj:pos + 8 * jj + 8]
                            ins = dve.tensor_tensor(dst, src, add.unsqueeze(2).to_broadcast([64, 8, NCMP]), ALU.add)
                ins.then_inc(signals["dve"].sem, 1)
            for kv in range(2):
                dve.wait_ge(blk_hi_ready, kv + 1)
                dve.tensor_tensor(blk_lo[kv][:], blk[kv][:].rearrange("p j h n -> p j (h n)"),
                                  blk_hi[kv][:].bitcast(F32), ALU.subtract).then_inc(blk_lo_ready, 1)
                if kv == 0:
                    for t in range(4):
                        dve.wait_ge(k_hi_ready, t + 1)
                        first, second = (x[:, k_cols(t)] for x in k_pairs)
                        dve.tensor_tensor(first[64:128, :], ps[t][0:64, :], first[0:64, :].bitcast(F32), ALU.subtract)
                        dve.tensor_tensor(second[0:64, :], ps[t][64:128, :], second[64:128, :].bitcast(F32),
                                          ALU.subtract).then_inc(signals["dve"].sem, 1)
            dve.wait_ge(small_turned, 1)
            dve.tensor_copy(gates[:, :, :].rearrange("p h i -> p i h"),
                            ps[5][:, 0:3 * NH * TT].rearrange("p (i h) -> p i h", i=TT)).then_inc(gates_ready, 1)

            def hidden(n):
                dve.wait_ge(small_turned, n + 2)
                dve.tensor_copy(hid_cmp[n][:, :, :].rearrange("p t x -> p (t x)"),
                                ps[6 + n][:, 0:2 * NKV * NCMP]).then_inc(hid_ready, 1)
            hidden(0)
            dve.wait_ge(cmp_done, 1)
            made = ps[4][:, 0:NKV * NCMP].rearrange("p (a g n) -> p g a n", a=2, n=NCMP)
            spots = [x[:, 0:K_AT[2]].rearrange("p (a n) -> p a n", a=2) for x in k_pairs]
            for g in range(2):
                dve.tensor_copy(spots[g][:, :, NCMP:NCMP_EVEN], made[:, g, :, NCMP - 1:NCMP])
                dve_step(dve, dve.tensor_copy(spots[g][:, :, 0:NCMP], made[:, g]))
            for g in range(2):
                ins = dve.tensor_tensor(spots[g][64:128, :, 0:NCMP], made[64:128, g],
                                        spots[g][64:128, :, 0:NCMP].bitcast(F32), ALU.subtract)
            ins.then_inc(cmp_ready, 1)
            hidden(1)
            dve.wait_ge(cmp_done, 2)
            dve.tensor_copy(v_cmp[0:NCMP, :, :],
                            ps[5][0:NCMP, 0:NKV * HD].rearrange("p (g d) -> p g d", d=HD)).then_inc(cmp_ready, 1)

            dve.wait_ge(masks_loaded, 16)
            dve_attention(dve)
            for c in range(KC):
                n = SPLIT["o"] + c
                dve.wait_ge(hi_ready, n + 1)
                dve.tensor_tensor(o_lo[:, c, :], oT[:, c, :], o_hi[:, c, :].bitcast(F32), ALU.subtract).then_inc(lo_ready, 1)
            job = jobs["attn_out"]
            for i in range(2):
                for t in range(4):
                    c = 4 * i + t
                    n = job.split0 + c
                    dve.wait_ge(gemm_done, tile_done(job, t, i))
                    dve.tensor_tensor(mixp[:, :], ps[t][:, :], g_attn[:, c, :], ALU.mult).then_inc(signals["dve"].sem, 1)
                    dve.wait_ge(signals["dve"].sem, freed(job, t, i))
                    val_free(dve, n)
                    dve.tensor_tensor(val[n % 2][:, :], mixp[:, :], mixc[:, c, :], ALU.add).then_inc(val_ready, 1)
                    dve_lo(dve, n, mix_lo[:, c, :], mix_hi[:, c, :], slot=n % 2)
            dve_adds(dve, "w_o", "ffn")

            def memory():
                for n in range(KC // 2):
                    dve.wait_ge(memT_done, n + 1)
                    dve.tensor_copy(memT[:, 2 * n:2 * n + 2, :].rearrange("p c t -> p (c t)"),
                                    ps[4 + n][:, :]).then_inc(memT_ready, 1)
                dve_norm(dve, "mem")
            dve_mlp(dve, "up", "down", "ffn", memory)

            dve_norms(dve)
            dve_recurrence_inputs(dve)
            dve_levels(dve)
            dve_norm(dve, "cq")
            dve_norm(dve, "ckv")
            for n in range(H2):
                dve_norm(dve, f"mem_k{n}")
            for c in range(3):
                dve_chunk(dve, c)
            for n in range(H2):
                if n < 2:
                    dve_angles(dve, n)
                dve_norm(dve, f"mem_q{n}")
            dve_rope(dve, 0)
            for n in range(H2):
                dve_norm(dve, f"q{n}")
                if n == 2:
                    dve_rope(dve, 1)
            for n in range(H2):
                dve_norm(dve, f"k{n}")
                if n == 0:
                    dve_rope(dve, 2)
            dve_rows(dve, 0)
            dve.wait_ge(rope_ready, 4)
            dve_attention2(dve)
            dve_adds(dve, "w_out", "ffn_2")
            dve_mlp(dve, "up_2", "down_2", "ffn_2")
            for t in range(TT):
                dve.wait_ge(out_turned, 2 * t + 2)
                dve.tensor_copy(out_rows[:, t, S:D], ps[out_bank(t, 1)][:, :]).then_inc(out_dve, 1)

        @block.tensor
        def _(pe):
            pe.wait_ge(x_loaded, 16)
            pe.wait_ge(consts_loaded, 16)
            for c in range(KC):
                if c >= 4:
                    pe.wait_ge(h_ready, c - 3)
                for t in range(TT):
                    mm = pe.transpose(ps[c % 4][:, P * t:P * t + P], x_rows[:, t, P * c:P * c + P], ident)
                mm.then_inc(xT_done, 1)
            pe.wait_ge(gains_loaded, 16 * 23)
            pe.transpose(ps[5][:, 0:NGAIN], gain_rows[0:NGAIN, :], ident[0:NGAIN, 0:NGAIN]).then_inc(gainsT_done, 1)
            pe_norm(pe, "mix")
            pe.wait_ge(h_ready, 8)
            for name in SET1[:-1]:
                pe_job(pe, name)

            def turn_hidden(n):
                X = NKV * NCMP
                pe.wait_ge(signals["act"].sem, freed(jobs[f"cmp_{'kv'[n]}"], 0, 0))
                for t in range(2):
                    mm = pe.transpose(ps[6 + n][:, X * t:X * t + X], hidT_cmp[n][0:X, P * t:P * t + P],
                                      ident[0:X, 0:X])
                mm.then_inc(small_turned, 1)

            def with_cmp_v(i, panel, tile):
                if panel == 0:
                    pe.wait_ge(signals["act"].sem, freed(jobs["gates"], 0, 0))
                    pe.wait_ge(rstd_ready, 1)
                    pe.wait_ge(gains_ready, 1)
                    for t in range(TT):
                        mm = pe.transpose(ps[5][:, 3 * NH * t:3 * NH * t + 3 * NH], gatesT[0:3 * NH, P * t:P * t + P],
                                          ident[0:3 * NH, 0:3 * NH])
                    mm.then_inc(small_turned, 1)
                    turn_hidden(0)
            pe_job(pe, "cmp_v", with_cmp_v)
            pe.wait_ge(w2_loaded, 48)
            pe.wait_ge(hid_ready, 1)
            for t in range(2):
                mm = pe.matmul(ps[4][:, 0:NKV * NCMP], w2k[:, t, :], hid_cmp[0][:, t, :], start=t == 0, stop=t == 1)
            mm.then_inc(cmp_done, 1)
            turn_hidden(1)
            pe.wait_ge(hid_ready, 2)
            pe.wait_ge(gates_ready, 1)
            for g in range(NKV):
                for t in range(2):
                    mm = pe.matmul(ps[5][0:NCMP, HD * g:HD * g + HD], hid_cmp[1][:, t, NCMP * g:NCMP * (g + 1)],
                                   w2v[:, t, :], start=t == 0, stop=t == 1)
            mm.then_inc(cmp_done, 1)
            pe_attention(pe)
            pe.wait_ge(val_ready, SPLIT["o"] + 8)
            pe_job(pe, "attn_out")
            pe_job(pe, "w_o")
            pe_norm_rest(pe, "ffn")
            pe_job(pe, "up")

            def with_down(i, panel, tile):
                first = i_is(i, 0)
                if first and panel == 1:
                    pe.wait_ge(mem_loaded, 16)
                    pe.wait_ge(rstd_ready, norms["ffn"]["n"] + 1)
                    for n in range(KC // 2):
                        for c in range(2):
                            for t in range(2):
                                mm = pe.transpose(ps[4 + n][:, NMEM * c + P * t:NMEM * c + P * t + P],
                                                  mem_rows[:, t, P * (2 * n + c):P * (2 * n + c) + P], ident)
                        mm.then_inc(memT_done, 1)
                if first and panel == 2:
                    pe.wait_ge(memT_ready, KC // 2)
                    pe_norm(pe, "mem")
            pe_job(pe, "down", with_down)
            pe.wait_ge(rstd_ready, norms["mem"]["n"] + 1)
            pe_sums(pe)
            pe_job(pe, "mem_k")
            pe_job(pe, "mem_v")
            pe_job(pe, "f")
            pe_job(pe, "hq")
            pe.wait_ge(rstd_ready, norms["mix_2"]["n"] + 1)

            def with_lat_a(i, panel, tile):
                if (panel, tile) == (0, 1):
                    pe.wait_ge(hq_ready, 1)
                    pe_level(pe, -1)
                if (panel, tile) == (0, 3):
                    pe_level(pe, 0)
                if (panel, tile) == (1, 1):
                    pe_level(pe, 1)
                if (panel, tile) == (1, 3):
                    pe_level(pe, 2)

            def with_lat_b(i, panel, tile):
                if tile == 1:
                    pe_level(pe, 3 + panel)

            def with_mq(i, panel, tile):
                if panel == 0 and tile % 2:
                    pe_level(pe, 5 + tile // 2)

            def with_i(i, panel, tile):
                if (panel, tile) == (0, 1):
                    pe.wait_ge(level_kept, H2 * (LEVELS + 1))
                    pe_norm(pe, "cq")
                if (panel, tile) == (0, 2):
                    pe_norm(pe, "ckv")
                if (panel, tile) == (0, 3):
                    pe_norm(pe, "mem_k0")
                if panel == 1 and tile < 3:
                    pe_norm(pe, f"mem_k{tile + 1}")

            def with_uq(i, panel, tile):
                if tile == 0:
                    pe.wait_ge(state_ready, 3)
                if tile % 2 == 0:
                    pe_norm(pe, f"mem_q{tile // 2}")

            def with_uq_rope(i, panel, tile):
                if tile == 0:
                    pe_norm(pe, "mem_q2")

            def with_ukv_k(i, panel, tile):
                if tile == 0:
                    pe_norm(pe, "mem_q3")

            def with_g(i, panel, tile):
                pe_norm(pe, f"{'qk'[panel]}{tile}")
                if (panel, tile) == (0, 2):
                    pe_rope(pe, 1)
                if (panel, tile) == (1, 0):
                    pe_rope(pe, 2)

            pe_job(pe, "lat_a", with_lat_a)
            pe_job(pe, "lat_b", with_lat_b)
            pe_job(pe, "mq", with_mq)
            pe_job(pe, "i", with_i)
            pe_turn_keys(pe)
            for c in range(TT):
                pe_chunk(pe, c)
            pe_job(pe, "uq_nope", with_uq)
            pe_job(pe, "uq_rope", with_uq_rope)
            pe_job(pe, "ukv_k", with_ukv_k)
            pe_job(pe, "ukv_v")
            pe_rope(pe, 0)
            pe_job(pe, "g", with_g)
            pe_attention2(pe)
            def with_w_out(i, panel, tile):
                if i == 0 and (panel, tile) == (0, 3):
                    pe_row(pe, 2, 0)
                if i == 0 and panel == 1 and tile < 3:
                    pe_row(pe, 2, tile + 1)
            pe_job(pe, "w_out", with_w_out)
            pe_norm_rest(pe, "ffn_2")
            pe_job(pe, "up_2")
            pe_job(pe, "down_2")
            pe.wait_ge(signals["dve"].sem, freed(jobs["down_2"], 1, 3))
            for t in range(TT):
                for half in range(2):
                    for c in range(4):
                        mm = pe.transpose(ps[out_bank(t, half)][:, P * c:P * c + P],
                                          h[:, 4 * half + c, P * t:P * t + P], ident)
                    mm.then_inc(out_turned, 1)


_INS = ("x w_in conv_w w_conv_out cmp_pos_k cmp_w1_k cmp_w2_k cmp_pos_v cmp_w1_v cmp_w2_v w_attn_out w_o "
        "g_mix g_ffn w_gate w_up w_down g_final mem_2 positions_2 norm_mix_2 norm_mem_2 w_in_2 q_a_norm_2 "
        "w_uq_2 kv_a_norm_2 w_ukv_2 mla_q_norm_2 mla_k_norm_2 hg_lb_logits_2 hg_out_norm_2 w_mem_kv_2 "
        "mem_q_norm_2 mem_k_norm_2 mla_out_norm_2 mem_out_norm_2 w_out_2 norm_ffn_2 w_gate_2 w_up_2 "
        "w_down_2").split()


def kernel(**inputs):
    import numpy as _np
    import concourse.bacc as _bacc
    from concourse import mybir as _mybir
    from concourse.bass_utils import run_bass_kernel_spmd as _run

    nc = _bacc.Bacc("TRN2", target_bir_lowering=False, num_devices=1)
    arrays = {name: _np.ascontiguousarray(inputs[name]) for name in _INS}
    arrays["consts"] = shape_constants()
    A = {name: nc.dram_tensor(f"in_{name}", a.shape, _mybir.dt.from_np(a.dtype), kind="ExternalInput").ap()
         for name, a in arrays.items()}
    out = nc.dram_tensor("out_0", (1, S, D), _mybir.dt.float32, kind="ExternalOutput").ap()
    build(nc, A, out)
    r = _run(nc, [{f"in_{name}": a for name, a in arrays.items()}], core_ids=[0])
    return r.results[0]["out_0"]
```
